# Optimizing a Trainium2 kernel written in Bass

```python
import math
import jax, jax.numpy as jnp
from jax import lax
import numpy as np

D_MODEL = 1024
BATCH = 1
SEQ = 512
DEPTH = 1
DEC_BATCH = 1
DEC_SEQ = 256
PAST_LEN = 128

MIX_W = D_MODEL
ATT_W = MIX_W // 2
ATT_HEADS = 4
ATT_V_DIM = ATT_W // ATT_HEADS
ATT_QK_DIM = ATT_V_DIM // 2
ROT_DIM = ATT_QK_DIM // 4
ROPE_THETA = 500000.0
Q_BLOCK = 128
M_W = MIX_W - ATT_W
M_HEADS = 4
M_HEAD_DIM = M_W // M_HEADS
M_CHUNK = 128
CONV_K = 5
N_GATES = 4 * M_HEADS
SPLITS = (ATT_W, ATT_W, ATT_W, M_W, M_W, M_W, M_W, N_GATES)
PROJ_W = sum(SPLITS)
SPLIT_AT = tuple(sum(SPLITS[:j + 1]) for j in range(len(SPLITS) - 1))
PEER_HEADS = 8
PEER_QDIM = 256
PEER_HALF = PEER_QDIM // 2
N_KEYS = 128
N_EXPERTS = N_KEYS * N_KEYS
PEER_TOPK = 16
PEER_BLOCK = 128
PLE_DIM = 256
EPS = 1e-6

kernel_name = "hymba_diffattn_mlstm_peer_encoder"

def rms_norm(x, w):
    x32 = x.astype(jnp.float32)
    y = x32 * lax.rsqrt(jnp.mean(x32 * x32, axis=-1, keepdims=True) + EPS)
    return (y * w.astype(jnp.float32)).astype(x.dtype)

def rope_tables(seq):
    inv = ROPE_THETA ** (-jnp.arange(0, ROT_DIM, 2, dtype=jnp.float32) / ROT_DIM)
    ang = jnp.arange(seq, dtype=jnp.float32)[:, None] * inv[None, :]
    return jnp.cos(ang), jnp.sin(ang)

def apply_partial_rope(x, cos, sin):
    half = ROT_DIM // 2
    xf = x.astype(jnp.float32)
    c = cos[:, None, None, :]
    s = sin[:, None, None, :]
    x1 = xf[..., :half]
    x2 = xf[..., half:ROT_DIM]
    out = jnp.concatenate([x1 * c - x2 * s, x2 * c + x1 * s, xf[..., ROT_DIM:]], axis=-1)
    return out.astype(x.dtype)

def diff_attention(q, k, v, lam):
    b, s = q.shape[:2]
    nb = s // Q_BLOCK
    qb = jnp.moveaxis(q.reshape(b, nb, Q_BLOCK, ATT_HEADS, 2, ATT_QK_DIM), 1, 0)

    def block(qi):
        sc = jnp.einsum('bqhcd,bkhcd->bhcqk', qi, k).astype(jnp.float32)
        p = jax.nn.softmax(sc, axis=-1)
        a = p[:, :, 0] - lam * p[:, :, 1]
        return jnp.einsum('bhqk,bkhe->bqhe', a.astype(v.dtype), v)

    out = lax.map(block, qb)
    return jnp.moveaxis(out, 0, 1).reshape(b, s, ATT_HEADS, ATT_V_DIM)

def centered_conv(x, w):
    c = x.shape[-1]
    return lax.conv_general_dilated(
        x, w[:, None, :].astype(x.dtype), window_strides=(1,),
        padding=[(CONV_K // 2, CONV_K // 2)],
        dimension_numbers=('NWC', 'WIO', 'NWC'), feature_group_count=c)

def mlstm_scan(q, k, v, ig, fg):
    b, h, s, d = q.shape
    nc = s // M_CHUNK

    def chunks(t):
        return jnp.moveaxis(t.reshape(b, h, nc, M_CHUNK, *t.shape[3:]), 2, 0)

    logf = jax.nn.log_sigmoid(fg)
    lower = jnp.tril(jnp.ones((M_CHUNK, M_CHUNK), dtype=bool))

    def step(carry, xs):
        C, n, m = carry
        qc, kc, vc, ic, lfc = xs
        bcum = jnp.cumsum(lfc, axis=-1)
        dlog = jnp.where(lower, bcum[..., :, None] - bcum[..., None, :] + ic[..., None, :], -jnp.inf)
        inter = bcum + m[..., None]
        m_t = jnp.maximum(inter, jnp.max(dlog, axis=-1))
        w = jnp.exp(dlog - m_t[..., None])
        sc = jnp.exp(inter - m_t)
        wqk = w * jnp.einsum('bhtd,bhsd->bhts', qc, kc)
        num = sc[..., None] * jnp.einsum('bhtd,bhde->bhte', qc, C) + jnp.einsum('bhts,bhse->bhte', wqk, vc)
        den = sc * jnp.einsum('bhtd,bhd->bht', qc, n) + jnp.sum(wqk, axis=-1)
        h_out = num / jnp.maximum(jnp.abs(den), jnp.exp(-m_t))[..., None]
        b_last = bcum[..., -1]
        rel = b_last[..., None] - bcum + ic
        m_new = jnp.maximum(b_last + m, jnp.max(rel, axis=-1))
        dec = jnp.exp(rel - m_new[..., None])
        keep = jnp.exp(b_last + m - m_new)
        C_new = keep[..., None, None] * C + jnp.einsum('bhs,bhsd,bhse->bhde', dec, kc, vc)
        n_new = keep[..., None] * n + jnp.einsum('bhs,bhsd->bhd', dec, kc)
        return (C_new, n_new, m_new), h_out

    init = (jnp.zeros((b, h, d, d), jnp.float32), jnp.zeros((b, h, d), jnp.float32),
            jnp.zeros((b, h), jnp.float32))
    _, hs = lax.scan(step, init, (chunks(q), chunks(k), chunks(v), chunks(ig), chunks(logf)))
    return jnp.moveaxis(hs, 0, 2).reshape(b, h, s, d)

def mlstm_mixer(mq, mk, mv, mo, gates, conv_w, gain):
    b, s, _ = mq.shape
    qk = jax.nn.silu(centered_conv(jnp.concatenate([mq, mk], axis=-1), conv_w))
    mq, mk = jnp.split(qk, 2, axis=-1)

    def heads(t):
        return t.reshape(b, s, M_HEADS, M_HEAD_DIM).transpose(0, 2, 1, 3).astype(jnp.float32)

    q = heads(mq)
    k = heads(mk) * (M_HEAD_DIM ** -0.5)
    v = heads(mv)
    g = gates.astype(jnp.float32).transpose(0, 2, 1).reshape(b, 4, M_HEADS, s)
    i_f, f_f, i_b, f_b = g[:, 0], g[:, 1], g[:, 2], g[:, 3]
    h_fwd = mlstm_scan(q, k, v, i_f, f_f)
    flip = lambda t: jnp.flip(t, axis=2)
    h_bwd = flip(mlstm_scan(flip(q), flip(k), flip(v), flip(i_b), flip(f_b)))
    hsum = (h_fwd + h_bwd).transpose(0, 2, 1, 3)
    o = jax.nn.sigmoid(mo.astype(jnp.float32)).reshape(b, s, M_HEADS, M_HEAD_DIM)
    hn = rms_norm(o * hsum, gain.reshape(M_HEADS, M_HEAD_DIM))
    return hn.reshape(b, s, M_W).astype(mq.dtype)

def peer(xn, wq, subkeys, u, v):
    b, s, d = xn.shape
    t = b * s
    xf = xn.reshape(t, d)
    q = (xf @ wq).reshape(t, PEER_HEADS, 2, PEER_HALF)
    s1 = jnp.einsum('thd,hkd->thk', q[:, :, 0], subkeys[:, 0]).astype(jnp.float32)
    s2 = jnp.einsum('thd,hkd->thk', q[:, :, 1], subkeys[:, 1]).astype(jnp.float32)
    v1, i1 = lax.top_k(s1, PEER_TOPK)
    v2, i2 = lax.top_k(s2, PEER_TOPK)
    cand = (v1[..., :, None] + v2[..., None, :]).reshape(t, PEER_HEADS, PEER_TOPK * PEER_TOPK)
    sc, ci = lax.top_k(cand, PEER_TOPK)
    e1 = jnp.take_along_axis(i1, ci // PEER_TOPK, axis=-1)
    e2 = jnp.take_along_axis(i2, ci % PEER_TOPK, axis=-1)
    nblk = t // PEER_BLOCK
    idx = (e1 * N_KEYS + e2).reshape(nblk, PEER_BLOCK, PEER_HEADS * PEER_TOPK)
    g = jax.nn.softmax(sc, axis=-1).reshape(nblk, PEER_BLOCK, PEER_HEADS * PEER_TOPK)

    def block(args):
        xb, ib, gb = args
        a = jnp.einsum('td,tkd->tk', xb, u[ib]).astype(jnp.float32)
        act = (jax.nn.gelu(a, approximate=False) * gb).astype(xb.dtype)
        return jnp.einsum('tk,tkd->td', act, v[ib])

    out = lax.map(block, (xf.reshape(nblk, PEER_BLOCK, d), idx, g))
    return out.reshape(b, s, d)

def encoder_trunk(x, p, norm_mix, w_in, gate_bias, conv_qk, lambda_qk, attn_gain, mlstm_gain,
                  w_out, norm_ffn, peer_wq, peer_subkeys, peer_u, peer_v, norm_ple,
                  ple_w_gate, ple_w_proj, norm_final):
    b, s, _ = x.shape
    cos, sin = rope_tables(s)
    for li in range(DEPTH):
        lam_init = 0.8 - 0.6 * math.exp(-0.3 * li)
        lq = lambda_qk[li].astype(jnp.float32)
        lam = jnp.exp(jnp.sum(lq[0] * lq[1])) - jnp.exp(jnp.sum(lq[2] * lq[3])) + lam_init
        h = rms_norm(x, norm_mix[li])
        proj = h @ w_in[li]
        aq, ak, av, mq, mk, mv, mo, gt = jnp.split(proj, SPLIT_AT, axis=-1)
        aq = apply_partial_rope(aq.reshape(b, s, ATT_HEADS, 2, ATT_QK_DIM), cos, sin) * (ATT_QK_DIM ** -0.5)
        ak = apply_partial_rope(ak.reshape(b, s, ATT_HEADS, 2, ATT_QK_DIM), cos, sin)
        av = av.reshape(b, s, ATT_HEADS, ATT_V_DIM)
        att = diff_attention(aq, ak, av, lam)
        att = (rms_norm(att, attn_gain[li]) * (1.0 - lam_init)).reshape(b, s, ATT_W)
        mem = mlstm_mixer(mq, mk, mv, mo, gt + gate_bias[li], conv_qk[li], mlstm_gain[li])
        x = x + jnp.concatenate([att.astype(x.dtype), mem.astype(x.dtype)], axis=-1) @ w_out[li]
        x = x + peer(rms_norm(x, norm_ffn[li]), peer_wq[li], peer_subkeys[li], peer_u[li], peer_v[li])
        gate = jax.nn.sigmoid((rms_norm(x, norm_ple[li]) @ ple_w_gate[li]).astype(jnp.float32))
        x = x + ((p[li] @ ple_w_proj[li]).astype(jnp.float32) * gate).astype(x.dtype)
    return rms_norm(x, norm_final)

def setup_inputs(seed: int = 0) -> dict:
    key = jax.random.key(seed)
    ks = jax.random.split(key, 24)
    f32 = jnp.float32
    nrm = lambda k, shape, scale: jax.random.normal(k, shape, f32) * scale
    gain = lambda k, shape: 1.0 + 0.02 * jax.random.normal(k, shape, f32)
    f_bias = jnp.linspace(3.0, 6.0, M_HEADS, dtype=f32)
    zb = jnp.zeros((M_HEADS,), f32)
    gate_off = jnp.stack([zb, f_bias, zb, f_bias])
    gate_bias = (0.1 * jax.random.normal(ks[6], (DEPTH, 4, M_HEADS), f32) + gate_off).reshape(DEPTH, N_GATES)
    return {
        "x_prompt": nrm(ks[0], (BATCH, SEQ, D_MODEL), 1.0),
        "x_sample": nrm(ks[1], (DEC_BATCH, DEC_SEQ, D_MODEL), 1.0),
        "p_prompt": nrm(ks[2], (DEPTH, BATCH, SEQ, PLE_DIM), 1.0),
        "p_sample": nrm(ks[3], (DEPTH, DEC_BATCH, DEC_SEQ, PLE_DIM), 1.0),
        "norm_mix": gain(ks[4], (DEPTH, D_MODEL)),
        "w_in": nrm(ks[5], (DEPTH, D_MODEL, PROJ_W), D_MODEL ** -0.5),
        "gate_bias": gate_bias,
        "conv_qk": nrm(ks[7], (DEPTH, CONV_K, 2 * M_W), CONV_K ** -0.5),
        "lambda_qk": nrm(ks[8], (DEPTH, 4, ATT_QK_DIM), 0.1),
        "attn_gain": gain(ks[9], (DEPTH, ATT_V_DIM)),
        "mlstm_gain": gain(ks[10], (DEPTH, M_W)),
        "w_out": nrm(ks[11], (DEPTH, MIX_W, D_MODEL), MIX_W ** -0.5),
        "norm_ffn": gain(ks[12], (DEPTH, D_MODEL)),
        "peer_wq": nrm(ks[13], (DEPTH, D_MODEL, PEER_HEADS * PEER_QDIM), D_MODEL ** -0.5),
        "peer_subkeys": nrm(ks[14], (DEPTH, PEER_HEADS, 2, N_KEYS, PEER_HALF), PEER_HALF ** -0.5),
        "peer_u": nrm(ks[15], (DEPTH, N_EXPERTS, D_MODEL), D_MODEL ** -0.5),
        "peer_v": nrm(ks[16], (DEPTH, N_EXPERTS, D_MODEL), PEER_HEADS ** -0.5),
        "norm_ple": gain(ks[17], (DEPTH, D_MODEL)),
        "ple_w_gate": nrm(ks[18], (DEPTH, D_MODEL, D_MODEL), D_MODEL ** -0.5),
        "ple_w_proj": nrm(ks[19], (DEPTH, PLE_DIM, D_MODEL), PLE_DIM ** -0.5),
        "norm_final": gain(ks[20], (D_MODEL,)),
    }

def reference(x_prompt, x_sample, p_prompt, p_sample, norm_mix, w_in, gate_bias, conv_qk,
              lambda_qk, attn_gain, mlstm_gain, w_out, norm_ffn, peer_wq, peer_subkeys,
              peer_u, peer_v, norm_ple, ple_w_gate, ple_w_proj, norm_final):
    weights = (norm_mix, w_in, gate_bias, conv_qk, lambda_qk, attn_gain, mlstm_gain, w_out,
               norm_ffn, peer_wq, peer_subkeys, peer_u, peer_v, norm_ple, ple_w_gate,
               ple_w_proj, norm_final)
    y_prompt = encoder_trunk(x_prompt, p_prompt, *weights)
    y_sample = encoder_trunk(x_sample, p_sample, *weights)
    return (y_prompt, y_sample)


_drawn_inputs = setup_inputs


def setup_inputs(seed=0):
    import zlib

    import numpy as np

    out = dict(_drawn_inputs(seed))
    spreads = {}
    factors = {'attn_gain': 9.719,
     'mlstm_gain': 8.529,
     'norm_ffn': 9.068,
     'norm_ple': 64.0,
     'norm_final': 8.674}
    for name, (base, spread) in spreads.items():
        noise = np.random.default_rng([zlib.crc32(name.encode()), seed]).standard_normal(out[name].shape)
        drawn = base * np.exp(spread * noise) if base else spread * noise
        out[name] = __import__('jax').numpy.asarray(drawn.astype(out[name].dtype))
    for name, factor in factors.items():
        out[name] = (out[name] * factor).astype(out[name].dtype)
    return out
```

```python
from contextlib import ExitStack

import concourse.bass as bass
from concourse import mybir

ALU = mybir.AluOpType
ACT = mybir.ActivationFunctionType
AX = mybir.AxisListType
F32 = mybir.dt.float32
U32 = mybir.dt.uint32

P = 128
D = 1024
DC = D // P
NT = 6
TOK = NT * P
SEQS = [(0, 4), (4, 2)]
H = 4
HALF = 8
QK = 64
NGATE = 16
PH = 8
K16 = 16
NSLOT = PH * K16
EPS = 1e-6
LAM_INIT = 0.2
NEG = -3.0e38
RING = 16
UNIT = 8
TOPK_STEPS = 1 + 49 + 2 + 25 + 10 + 2 + 3

BLOCKS = [("mq", 1536), ("mk", 2048), ("mv", 2560), ("mo", 3072), ("aq", 0), ("ak", 512), ("av", 1024)]
GATE0 = 3584
NIN = len(BLOCKS)


def hymba_layer(nc, x_a, x_b, pT_a, pT_b, norm_mix, w_in, gate_w, gate_b, conv_w, lambda_qk, attn_gain,
                mlstm_gain, w_out, norm_ffn, peer_wq, subkeysT, peer_u, peer_v, norm_ple,
                ple_w_gate, ple_w_proj, norm_final, rope, y_a, y_b):
    ctx = ExitStack()
    with ctx:
        def sb(name, shape, dt=F32):
            return ctx.enter_context(nc.sbuf_tensor(name, shape, dt))

        def sem(name):
            return ctx.enter_context(nc.semaphore(name))


        WORDS = 48300
        arena = sb("arena", [P, WORDS])

        def view(at, *dims):
            n = 1
            for d in dims:
                n *= d
            assert at + n <= WORDS, (at, dims)
            v = arena[:, at:at + n]
            if len(dims) == 2:
                return v.rearrange("p (a b) -> p a b", a=dims[0])
            if len(dims) == 3:
                return v.rearrange("p (a b c) -> p a b c", a=dims[0], b=dims[1])
            return v

        X = view(0, NT, D)
        HT_AT = NT * D
        hT = view(HT_AT, DC, TOK)
        catT = hT
        W_AT = HT_AT + DC * TOK
        W = view(W_AT, 2, DC, 512)
        FREE = W_AT + 2 * DC * 512

        preA = view(FREE, 2 * H, 516)
        preB = view(FREE + 2 * H * 516, 2 * H, 260)
        aT = view(FREE, 2 * H, TOK)
        at = FREE + 2 * H * (516 + 260)
        mT = view(at, 2 * H, TOK)
        att = view(at, NT, H * P)
        at += 2 * H * TOK
        vm = view(at, NT, H, P + 1)
        at += NT * H * (P + 1)
        mo = view(at, NT, H * P)
        at += NT * H * P
        av = view(at, NT, H * P)
        at += NT * H * P
        wsA = view(at, 2, 4, 512)
        wsB = view(at + 4096, 2, 2, 256)
        hn = view(at, 2, D)
        junk = view(at + 2 * D, D)
        stg = view(at + 3 * D, 2, 512)
        prob = view(at, 2, 2, 512)
        comb = view(at + 2048, 2, 512)
        combT = view(at + 3072, 2, 512)
        at += 2 * 4 * 512 + 2 * 2 * 256
        wbc = view(at, D)
        at += D
        junk_sq = wbc[:, 0:P]
        rot = wbc[:, P:P + 256].rearrange("p (a g n) -> p a g n", a=4, g=8)
        lq = wbc[:, 512:768].rearrange("p (a b) -> p a b", a=4)
        gates = {}
        for i, name in enumerate(("i", "f", "e", "B", "M")):
            gates[name] = arena[0:36, i * TOK:(i + 1) * TOK]
        sel = view(4 * D, 2 * H, P)[0:36]
        assert at <= WORDS, at

        subk = view(FREE, 2 * PH, P)
        rows = view(HT_AT, RING, D)
        assert HT_AT + RING * D == FREE + 2 * PH * P
        at = FREE + 2 * PH * P
        scores = view(at, NT, 2 * PH, P)
        at += NT * 2 * PH * P
        scores_flat = view(FREE + 2 * PH * P, NT * 2 * PH * P)
        qT = view(at, 2, TOK)
        at += 2 * TOK
        xn = view(at, D)
        at += D
        acc = view(at, D)
        at += D
        hn2 = view(at, 2, D)
        at += 2 * D
        junk2 = view(at, D)
        at += D
        wbc2 = view(at, D)
        at += D
        cand = view(at, PH, K16 * K16)
        at += PH * K16 * K16
        onehot = view(at, NSLOT, K16)
        now = view(at, 2 * PH * P)
        at += NSLOT * K16
        assert at <= WORDS, at

        pT = qT
        wp = view(FREE + 2 * PH * P, 2, D)
        sig = view(FREE + 2 * PH * P + 2 * D, 2, 512)
        plp = view(FREE + 2 * PH * P + 2 * D + 1024, 2, 512)

        small = sb("small", [P, 1024])
        spos = [0]

        def tiny(*dims, dt=F32):
            n = 1
            for d in dims:
                n *= d
            v = small[:, spos[0]:spos[0] + n]
            spos[0] += n
            assert spos[0] <= 1024
            if dt != F32:
                v = v.bitcast(dt)
            if len(dims) == 2:
                v = v.rearrange("p (a b) -> p a b", a=dims[0])
            elif len(dims) == 3:
                v = v.rearrange("p (a b c) -> p a b c", a=dims[0], b=dims[1])
            return v

        ident = sb("ident", [P, P])
        gw = sb("gw", [P, DC, 2, 36])
        gb = tiny(2)
        convw = tiny(2 * H, 5)
        again = tiny(1)
        again08 = tiny(1)
        mgain = tiny(H)
        ropet = tiny(4, 2, HALF)
        ssq = tiny(NT)
        var = tiny(NT)
        rstd = tiny(NT)
        lsum = tiny(2)
        lexp = tiny(2)
        nlam = tiny(1)
        acol = tiny(NT, 36)
        floor = tiny(NT, 36)
        den = tiny(2)
        rden = tiny(2)
        hsum = tiny(2, P)
        mss = tiny(NT * H)
        ass_ = tiny(NT * H)
        mrs = tiny(NT * H)
        ars = tiny(NT * H)
        nmax = tiny(2, 2)
        z = tiny(2, 2)
        rz = tiny(2)
        nl = tiny(1)
        pk = sb("pk", [P, 2800])
        kp = [0]

        def peer_tiny(*dims, dt=F32):
            n = 1
            for d in dims:
                n *= d
            v = pk[:, kp[0]:kp[0] + n]
            kp[0] += n
            assert kp[0] <= 2800
            if dt != F32:
                v = v.bitcast(dt)
            if len(dims) == 2:
                v = v.rearrange("p (a b) -> p a b", a=dims[0])
            elif len(dims) == 3:
                v = v.rearrange("p (a b c) -> p a b c", a=dims[0], b=dims[1])
            return v

        topv = peer_tiny(PH, 2, K16)
        topi = peer_tiny(PH, 2, K16, dt=U32)
        topf = peer_tiny(PH, 2, K16)
        bestv = peer_tiny(PH, K16)
        bestc = peer_tiny(PH, K16, dt=U32)
        rank_u = peer_tiny(NSLOT, dt=U32)
        rank = peer_tiny(NSLOT)
        e1 = peer_tiny(NSLOT)
        e2 = peer_tiny(NSLOT)
        idx = peer_tiny(NT * NSLOT, dt=U32)
        dots = peer_tiny(NSLOT)
        coef = peer_tiny(NSLOT)
        gate = peer_tiny(NSLOT)
        dots_now = peer_tiny(RING)
        gsum = peer_tiny(PH)
        iota16 = peer_tiny(K16)
        idx_now = peer_tiny(2, UNIT, dt=U32)

        ps = ctx.enter_context(nc.psum_tensor("ps", [P, 8, 512], F32))

        x_ready = [sem(f"x_ready{t}") for t in range(NT)]
        w_ready = [sem(f"w_ready{i}") for i in range(2)]
        lam_ready = sem("lam_ready")
        consts_ready = sem("consts_ready")
        wbc_ready = sem("wbc_ready")
        made = sem("made")
        mk = sem("mk")
        N = {k: {e: sem(f"{k}_{e}") for e in ("ssq", "var", "rstd", "hn", "trans", "hT")}
             for k in ("mix", "ffn", "ple", "fin")}
        gates_done, gates_copied = sem("gates_done"), sem("gates_copied")
        proj_done, proj_copied = sem("proj_done"), sem("proj_copied")
        rope_done, qk_trans, qk_copied = sem("rope_done"), sem("qk_trans"), sem("qk_copied")
        conv_done, silu_done = sem("conv_done"), sem("silu_done")
        gate_abs, gate_exp, gate_ln = sem("gate_abs"), sem("gate_exp"), sem("gate_ln")
        rows_done, cols_trans, cols_done = sem("rows_done"), sem("cols_trans"), sem("cols_done")
        bc_done, w_exp, w_mask = sem("bc_done"), sem("w_exp"), sem("w_mask")
        s_done, ws_ready = sem("s_done"), sem("ws_ready")
        num_done, num_used = sem("num_done"), sem("num_used")
        mem_squared = sem("mem_squared")
        lam_sum, lam_exp, lam_done = sem("lam_sum"), sem("lam_exp"), sem("lam_done")
        sc_done, nm_done, prob_exp = sem("sc_done"), sem("nm_done"), sem("prob_exp")
        comb_done, ctr_done, combT_done = sem("comb_done"), sem("ctr_done"), sem("combT_done")
        att_mm, att_done = sem("att_mm"), sem("att_done")
        cvar, crstd, cnorm, ctrans, cat_done = (sem(n) for n in ("cvar", "crstd", "cnorm", "ctrans", "cat_done"))
        out_done, out_added = sem("out_done"), sem("out_added")
        subk_ready = sem("subk_ready")
        pq_done, pq_copied, ps_done, ps_copied = (sem(n) for n in ("pq_done", "pq_copied", "ps_done", "ps_copied"))
        dve_step = sem("dve_step")
        topk_step = sem("topk_step")
        best_ready, gate_e = sem("best_ready"), sem("gate_e")
        idx_ready, idx_staged, idx_taken = sem("idx_ready"), sem("idx_staged"), sem("idx_taken")
        row_ready = [sem(f"row_ready{i}") for i in range(RING)]
        row_used = sem("row_used")
        x_done = sem("x_done")
        dve_held, pool_held = sem("dve_held"), sem("pool_held")
        dots_done, gelu_done, coef_done = sem("dots_done"), sem("gelu_done"), sem("coef_done")
        xn_step, dots_copied = sem("xn_step"), sem("dots_copied")
        acc_step = sem("acc_step")
        ple_ready = sem("ple_ready")
        pg_done, pg_sig, pp_used = sem("pg_done"), sem("pg_sig"), sem("pp_used")
        y_ready, y_out = sem("y_ready"), [sem("y_out0"), sem("y_out1")]

        block = ctx.enter_context(nc.Block())

        def seq_of(t):
            return SEQS[0] if t < 4 else SEQS[1]

        def x_rows(t):
            src = x_a if t < 4 else x_b
            r = (t - seq_of(t)[0]) * P
            return src[r:r + P, :]

        def row_of(w):
            return w.rearrange("(a n) -> a n", a=1).to_broadcast([P, D])

        w_blocks = [w_in[:, c:c + 512] for _, c in BLOCKS]
        w_blocks += [w_out[:, 512 * i:512 * i + 512] for i in range(2)]
        w_blocks += [peer_wq[:, 512 * i:512 * i + 512] for i in range(4)]
        PQ0 = NIN + 2
        PG0 = PQ0 + 4
        PROJ_ENDS = (8, 16, 22, 28, 34, 40, 46)

        def block_read(n):
            if n < NIN:
                return proj_done, PROJ_ENDS[n]
            if n < PQ0:
                return out_done, NT * (n - NIN + 1)
            return pq_done, 4 * (n - PQ0 + 1)
        w_blocks += [ple_w_gate[:, 512 * i:512 * i + 512] for i in range(2)]

        @block.sync
        def _(sp):
            def load_block(n):
                if 2 <= n < PG0:
                    sp.wait_ge(*block_read(n - 2))
                sp.dma_start(W[:, n % 2], w_blocks[n].rearrange("(c p) n -> p c n", p=P)).then_inc(w_ready[n % 2], 16)

            sp.dma_start(X[:, 0], x_rows(0)).then_inc(x_ready[0], 16)
            sp.dma_start(wbc, row_of(norm_mix)).then_inc(wbc_ready, 16)
            for t in range(1, NT):
                sp.dma_start(X[:, t], x_rows(t)).then_inc(x_ready[t], 16)
            sp.dma_start(gw[:], gate_w.rearrange("(c p) k n -> p c k n", p=P)).then_inc(consts_ready, 16)
            sp.dma_start(gb[0:36, :], gate_b).then_inc(consts_ready, 16)
            load_block(0)
            load_block(1)
            sp.dma_start(convw, conv_w).then_inc(consts_ready, 16)
            sp.dma_start(again, attn_gain).then_inc(consts_ready, 16)
            sp.dma_start(mgain, mlstm_gain).then_inc(consts_ready, 16)
            sp.dma_start(ropet, rope.rearrange("(t p) a b -> p t a b", p=P)).then_inc(consts_ready, 16)
            sp.wait_ge(N["mix"]["hn"], NT)
            sp.dma_start(lq, lambda_qk.rearrange("(o a) b -> o a b", o=1).to_broadcast([P, 4, QK])).then_inc(lam_ready, 16)
            for n in range(2, NIN + 2):
                load_block(n)
            sp.wait_ge(bc_done, H)
            for t in range(NT):
                sp.dma_start(X[:, t], x_rows(t)).then_inc(x_ready[t], 16)
            sp.wait_ge(att_done, NT * H)
            sp.wait_ge(cat_done, 2 * NT)
            sp.dma_start(wbc2, row_of(norm_ffn)).then_inc(wbc_ready, 16)
            sp.dma_start(subk, subkeysT).then_inc(subk_ready, 16)
            for n in range(NIN + 2, PG0):
                load_block(n)
            sp.wait_ge(row_used, RING + 2 * NT * NSLOT)
            sp.dma_start(wbc2, row_of(norm_ple)).then_inc(wbc_ready, 16)
            sp.dma_start(pT[:, :, 0:512], pT_a.rearrange("(c p) n -> p c n", p=P)).then_inc(ple_ready, 16)
            sp.dma_start(pT[:, :, 512:TOK], pT_b.rearrange("(c p) n -> p c n", p=P)).then_inc(ple_ready, 16)
            sp.dma_start(wp, ple_w_proj.rearrange("(c p) n -> p c n", p=P)).then_inc(ple_ready, 16)
            load_block(PG0)
            load_block(PG0 + 1)
            sp.wait_ge(N["ple"]["hn"], NT)
            sp.dma_start(wbc2, row_of(norm_final)).then_inc(wbc_ready, 16)
            for t in range(NT):
                sp.wait_ge(y_ready, t + 1)
                dst = y_a if t < 4 else y_b
                r = (t - seq_of(t)[0]) * P
                sp.dma_start(dst[r:r + P, :], hn2[:, t % 2]).then_inc(y_out[t % 2], 16)
            for i in range(2):
                sp.wait_ge(y_out[i], 16 * (NT // 2))

        @block.gpsimd
        def _(pool):
            g = nc.gpsimd
            g.memset(ident[:], 0.0).then_inc(mk, 1)
            g.iota(iota16, pattern=[[1, K16]], base=0, channel_multiplier=0,
                   allow_small_or_imprecise_dtypes=True).then_inc(mk, 1)
            pool.wait_ge(mk, 2)
            g.affine_select(out=ident[:], in_=ident[:], compare_op=ALU.not_equal, fill=1.0, base=0,
                            pattern=[[-1, P]], channel_multiplier=1).then_inc(made, 1)
            g.memset(preA[:, :, 0:2], 0.0).then_inc(made, 1)
            g.memset(preA[:, :, 514:516], 0.0).then_inc(made, 1)
            g.memset(preB[:, :, 0:2], 0.0).then_inc(made, 1)
            g.memset(preB[:, :, 258:260], 0.0).then_inc(made, 1)
            g.memset(vm[:, :, :, P:P + 1], 1.0).then_inc(made, 1)
            pool.wait_ge(N["mix"]["hn"], NT)
            g.memset(sel, 0.0).then_inc(mk, 1)
            pool.wait_ge(mk, 3)
            for i in range(2 * H):
                row = 32 * (i // H) + i % H
                g.affine_select(out=sel[:, i], in_=sel[:, i], compare_op=ALU.not_equal, fill=-1.0,
                                base=-row, pattern=[[0, P]], channel_multiplier=1).then_inc(made, 1)
            for h in range(H):
                for j in range(NT):
                    for d in range(2):
                        pool.wait_ge(w_exp, 2 * NT * h + 2 * j + d + 1)
                        t0, n = seq_of(j)
                        o = (j - t0) * P
                        w = (wsA if n == 4 else wsB)[:, d, j - t0, o:o + P]
                        sign = 1 if d == 0 else -1
                        g.affine_select(out=w, in_=w, compare_op=ALU.is_ge, fill=0.0, base=0,
                                        pattern=[[sign, P]], channel_multiplier=-sign).then_inc(w_mask, 1)
            def wait_for(signal, value):
                pool.wait_ge(signal, value)
                pool.sem_inc(pool_held, 1)

            with pool.Fori(0, NT) as t:
                for phase, table in ((0, peer_u), (1, peer_v)):
                    wait_for(idx_ready, t + 1)
                    with pool.Fori(0, NSLOT // (2 * UNIT)) as b:
                        n = t * (2 * NSLOT // RING) + phase * (NSLOT // RING) + b
                        for half in range(2):
                            wait_for(row_used, n * RING + half * UNIT + UNIT)
                            g.tensor_copy(idx_now[:, half], idx[:, bass.ds(t * NSLOT + b * 2 * UNIT + half * UNIT, UNIT)]).then_inc(idx_staged, 1)
                            wait_for(idx_staged, n * 2 + half + 1)
                            for s in range(UNIT):
                                slot = half * UNIT + s
                                g.indirect_dma_start(out=rows[:, slot], out_offset=None, in_=table,
                                                     in_offset=bass.IndirectOffsetOnAxis(ap=idx_now[:, half, s:s + 1], axis=0),
                                                     ).then_inc(row_ready[slot], 16)

        @block.tensor
        def _(pe):
            def norm_transposes(k):
                for t in range(NT):
                    pe.wait_ge(N[k]["hn"], t + 1)
                    for half in range(2):
                        n = 2 * t + half
                        if n >= 2:
                            pe.wait_ge(N[k]["hT"], n - 1)
                        src = (hn if k == "mix" else hn2)[:, t % 2]
                        for c in range(4):
                            mm = nc.tensor.transpose(ps[:, half, c * P:(c + 1) * P],
                                                     src[:, (4 * half + c) * P:(4 * half + c + 1) * P], ident[:])
                        mm.then_inc(N[k]["trans"], 1)

            def contract(out, lhs, rhs, n=DC):
                for c in range(n):
                    mm = nc.tensor.matmul(out, lhs(c), rhs(c), start=(c == 0), stop=(c == n - 1))
                return mm

            pe.wait_ge(made, 1)
            norm_transposes("mix")
            pe.wait_ge(N["mix"]["hT"], 2 * NT)

            pe.wait_ge(consts_ready, 16 * 6)
            for kind in range(2):
                contract(ps[0:36, 2 + kind, :], lambda c: gw[:, c, kind, :], lambda c: hT[:, c, 0:512])
                contract(ps[0:36, 4 + kind, 0:256], lambda c: gw[:, c, kind, :],
                         lambda c: hT[:, c, 512:TOK]).then_inc(gates_done, 1)

            grp = 0
            units = 0

            def bank_free(g):
                if g < 4:
                    pe.wait_ge(gates_copied, 4)
                else:
                    pe.wait_ge(proj_copied, g - 3)

            def qk_transposes(u):
                pe.wait_ge(rope_done, u + 1)
                if u >= 2:
                    pe.wait_ge(qk_copied, u - 1)
                for c in range(4):
                    mm = nc.tensor.transpose(ps[:, 6 + u % 2, c * P:(c + 1) * P], stg[:, u % 2, c * P:(c + 1) * P], ident[:])
                mm.then_inc(qk_trans, 1)

            for n, (name, _) in enumerate(BLOCKS):
                pe.wait_ge(w_ready[n % 2], 16 * (n // 2 + 1))
                Wn = W[:, n % 2]
                if name in ("mq", "mk"):
                    for f in range(4):
                        for t0, nt in SEQS:
                            bank_free(grp)
                            mm = contract(ps[:, 2 + grp % 4, 0:nt * P], lambda c: Wn[:, c, f * P:(f + 1) * P],
                                          lambda c: hT[:, c, t0 * P:(t0 + nt) * P])
                            mm.then_inc(proj_done, 1)
                            grp += 1
                else:
                    for t in range(NT):
                        bank_free(grp)
                        mm = contract(ps[:, 2 + grp % 4, :], lambda c: hT[:, c, t * P:(t + 1) * P], lambda c: Wn[:, c, :])
                        mm.then_inc(proj_done, 1)
                        grp += 1
                        if name in ("aq", "ak"):
                            if units >= 1:
                                qk_transposes(units - 1)
                            units += 1
                        elif name == "av" and t == 0:
                            qk_transposes(units - 1)
                assert grp == PROJ_ENDS[n]

            pe.wait_ge(rows_done, 1)
            pe.wait_ge(qk_copied, 12)
            for t in range(NT):
                nc.tensor.transpose(ps[:, 6, t * 36:(t + 1) * 36], gates["i"][:, t * P:(t + 1) * P], ident[0:36, 0:36])
                mm = nc.tensor.transpose(ps[:, 7, t * 36:(t + 1) * 36], gates["f"][:, t * P:(t + 1) * P], ident[0:36, 0:36])
            mm.then_inc(cols_trans, 1)
            pe.wait_ge(cols_done, 2)
            pe.wait_ge(proj_copied, grp)
            pe.wait_ge(made, 1 + 2 * H + 5)
            for h in range(H):
                if h >= 1:
                    pe.wait_ge(w_exp, 2 * NT * h)
                for d in range(2):
                    nc.tensor.matmul(ps[:, 2 * d, :], sel[:, d * H + h], gates["M"][:, 0:512], start=True, stop=True)
                    mm = nc.tensor.matmul(ps[:, 1, 256 * d:256 * d + 256], sel[:, d * H + h], gates["M"][:, 512:TOK],
                                          start=True, stop=True)
                mm.then_inc(bc_done, 1)
                if h == 0:
                    pe.wait_ge(silu_done, 2 * H)
                for j in range(NT):
                    n = NT * h + j
                    t0, nt = seq_of(j)
                    if n >= 2:
                        pe.wait_ge(ws_ready, n - 1)
                    nc.tensor.matmul(ps[:, 3 + n % 2, 0:nt * P], mT[:, H + h, j * P:(j + 1) * P],
                                     mT[:, h, t0 * P:(t0 + nt) * P], start=True, stop=True).then_inc(s_done, 1)
                for t in range(NT):
                    m = NT * h + t
                    t0, nt = seq_of(t)
                    pe.wait_ge(ws_ready, NT * h + t0 + nt)
                    if m >= 2:
                        pe.wait_ge(num_used, m - 1)
                    ws = wsA if nt == 4 else wsB
                    i = t - t0
                    for d in range(2):
                        js = range(0, i + 1) if d == 0 else range(i, nt)
                        for j in js:
                            mm = nc.tensor.matmul(ps[:, 5 + 2 * (m % 2), d * 129:(d + 1) * 129],
                                                  ws[:, d, j, i * P:(i + 1) * P], vm[:, t0 + j, h, :],
                                                  start=(j == js[0]), stop=(j == js[-1]))
                    mm.then_inc(num_done, 1)

            def scores_of(m):
                h, t = divmod(m, NT)
                t0, nt = seq_of(t)
                if m >= 2:
                    pe.wait_ge(prob_exp, 2 * (m - 1))
                for c in range(2):
                    mm = nc.tensor.matmul(ps[:, 2 * (m % 2) + c, 0:nt * P], aT[QK * c:QK * c + QK, h, t * P:(t + 1) * P],
                                          aT[QK * c:QK * c + QK, H + h, t0 * P:(t0 + nt) * P], start=True, stop=True)
                mm.then_inc(sc_done, 1)

            def turn(m):
                nt = seq_of(m % NT)[1]
                pe.wait_ge(comb_done, m + 1)
                if m >= 2:
                    pe.wait_ge(combT_done, m - 1)
                for c in range(nt):
                    mm = nc.tensor.transpose(ps[:, 4 + m % 2, c * P:(c + 1) * P], comb[:, m % 2, c * P:(c + 1) * P], ident[:])
                mm.then_inc(ctr_done, 1)

            def values(m):
                h, t = divmod(m, NT)
                t0, nt = seq_of(t)
                pe.wait_ge(combT_done, m + 1)
                if m >= 2:
                    pe.wait_ge(att_done, m - 1)
                contract(ps[:, 6 + m % 2, 0:P], lambda c: combT[:, m % 2, c * P:(c + 1) * P],
                         lambda c: av[:, t0 + c, h * P:(h + 1) * P], nt).then_inc(att_mm, 1)

            pe.wait_ge(num_used, NT * H)
            pe.wait_ge(ws_ready, NT * H)
            MU = NT * H
            for m in range(MU + 2):
                if m < MU:
                    scores_of(m)
                if 1 <= m <= MU:
                    turn(m - 1)
                if m >= 2:
                    values(m - 2)

            for t in range(NT):
                pe.wait_ge(cnorm, 2 * (t + 1))
                if t >= 1:
                    pe.wait_ge(cat_done, 2 * t)
                for k, src in enumerate((att, mo)):
                    for h in range(H):
                        mm = nc.tensor.transpose(ps[:, k, h * P:(h + 1) * P], src[:, t, h * P:(h + 1) * P], ident[:])
                    mm.then_inc(ctrans, 1)
            pe.wait_ge(cat_done, 2 * NT)
            pe.wait_ge(att_done, NT * H)
            for i in range(2):
                n = NIN + i
                pe.wait_ge(w_ready[n % 2], 16 * (n // 2 + 1))
                for t in range(NT):
                    g = NT * i + t
                    if g >= 4:
                        pe.wait_ge(out_added, g - 3)
                    mm = contract(ps[:, 2 + g % 4, :], lambda c: catT[:, c, t * P:(t + 1) * P], lambda c: W[:, n % 2, c, :])
                    mm.then_inc(out_done, 1)

            norm_transposes("ffn")
            pe.wait_ge(N["ffn"]["hT"], 2 * NT)
            pe.wait_ge(subk_ready, 16)
            for q in range(2 * PH):
                n = PQ0 + q // 4
                if q % 4 == 0:
                    pe.wait_ge(w_ready[n % 2], 16 * (n // 2 + 1))
                if q >= 2:
                    pe.wait_ge(pq_copied, q - 1)
                for t0, nt in SEQS:
                    b = 2 + 2 * (q % 2) + (t0 > 0)
                    mm = contract(ps[:, b, 0:nt * P], lambda c: W[:, n % 2, c, (q % 4) * P:(q % 4 + 1) * P],
                                  lambda c: hT[:, c, t0 * P:(t0 + nt) * P])
                mm.then_inc(pq_done, 1)

                def score(q):
                    pe.wait_ge(pq_copied, q + 1)
                    if q >= 1:
                        pe.wait_ge(ps_copied, q)
                    for t in range(NT):
                        mm = nc.tensor.matmul(ps[:, 6 + t // 4, (t % 4) * P:(t % 4 + 1) * P], qT[:, q % 2, t * P:(t + 1) * P],
                                              subk[:, q, :], start=True, stop=True)
                    mm.then_inc(ps_done, 1)
                if q >= 1:
                    score(q - 1)
            score(2 * PH - 1)

            norm_transposes("ple")
            pe.wait_ge(N["ple"]["hT"], 2 * NT)
            pe.wait_ge(ple_ready, 48)
            for i in range(2):
                n = PG0 + i
                pe.wait_ge(w_ready[n % 2], 16 * (n // 2 + 1))
                for t in range(NT):
                    g = NT * i + t
                    if g >= 2:
                        pe.wait_ge(pp_used, g - 1)
                    contract(ps[:, 2 + 2 * (g % 2), :], lambda c: hT[:, c, t * P:(t + 1) * P], lambda c: W[:, n % 2, c, :])
                    contract(ps[:, 3 + 2 * (g % 2), :], lambda c: pT[:, c, t * P:(t + 1) * P],
                             lambda c: wp[:, c, 512 * i:512 * i + 512], 2).then_inc(pg_done, 1)

        @block.scalar
        def _(act):
            a = nc.scalar

            def norm(k):
                for t in range(NT):
                    if k == "mix":
                        act.wait_ge(x_ready[t], 16)
                    j = junk if k == "mix" else junk2
                    if t >= 1:
                        act.wait_ge(N[k]["ssq"], t)
                    a.activation(j, X[:, t], ACT.Square, accum_out=ssq[:, t:t + 1]).then_inc(N[k]["ssq"], 1)
                act.wait_ge(N[k]["var"], 1)
                a.activation(rstd, var, ACT.Sqrt).then_inc(N[k]["rstd"], 1)

            def norm_copies(k):
                for n in range(2 * NT):
                    t, half = divmod(n, 2)
                    act.wait_ge(N[k]["trans"], n + 1)
                    a.activation(hT[:, 4 * half:4 * half + 4, t * P:(t + 1) * P],
                                 ps[:, half, :].rearrange("p (c n) -> p c n", c=4), ACT.Copy).then_inc(N[k]["hT"], 1)

            norm("mix")
            norm_copies("mix")

            def qk_copy(u):
                act.wait_ge(qk_trans, u + 1)
                t, part = u % NT, u // NT
                a.activation(aT[:, H * part:H * part + H, t * P:(t + 1) * P],
                             ps[:, 6 + u % 2, :].rearrange("p (c n) -> p c n", c=4), ACT.Copy).then_inc(qk_copied, 1)

            grp = 0
            units = 0
            for name, _ in BLOCKS:
                if name in ("mq", "mk"):
                    for f in range(4):
                        for (t0, nt), dst in zip(SEQS, (preA, preB)):
                            act.wait_ge(proj_done, grp + 1)
                            c = f + (4 if name == "mk" else 0)
                            a.activation(dst[:, c, 2:2 + nt * P], ps[:, 2 + grp % 4, 0:nt * P], ACT.Copy).then_inc(proj_copied, 1)
                            grp += 1
                    if name == "mq":
                        act.wait_ge(gate_abs, 1)
                        a.activation(gates["e"], gates["e"], ACT.Exp, scale=-1.0).then_inc(gate_exp, 1)
                        act.wait_ge(gate_exp, 1)
                        a.activation(gates["e"], gates["e"], ACT.Ln, bias=1.0).then_inc(gate_ln, 1)
                        act.wait_ge(lam_sum, 2)
                        a.activation(lexp, lsum, ACT.Exp).then_inc(lam_exp, 1)
                    continue
                for t in range(NT):
                    act.wait_ge(proj_done, grp + 1)
                    src = ps[:, 2 + grp % 4, :]
                    if name == "mv":
                        a.activation(vm[:, t, :, 0:P], src.rearrange("p (h e) -> p h e", h=H), ACT.Copy).then_inc(proj_copied, 1)
                    elif name == "mo":
                        a.activation(mo[:, t], src, ACT.Sigmoid).then_inc(proj_copied, 1)
                    elif name == "av":
                        a.activation(av[:, t], src, ACT.Copy).then_inc(proj_copied, 1)
                    else:
                        if units >= 2:
                            act.wait_ge(qk_trans, units - 1)
                        a.activation(stg[:, units % 2], src, ACT.Copy).then_inc(proj_copied, 1)
                        if units == 0:
                            for c in range(2 * H):
                                act.wait_ge(conv_done, c + 1)
                                a.activation(mT[:, c, :], mT[:, c, :], ACT.Silu).then_inc(silu_done, 1)
                        if units >= 1:
                            qk_copy(units - 1)
                        units += 1
                    grp += 1
                    if name == "av" and t == 0:
                        qk_copy(units - 1)
            act.wait_ge(cols_trans, 1)
            a.activation(acol.rearrange("p t n -> p (t n)"), ps[:, 6, 0:NT * 36], ACT.Copy).then_inc(cols_done, 1)
            a.activation(floor.rearrange("p t n -> p (t n)"), ps[:, 7, 0:NT * 36], ACT.Exp, scale=-1.0).then_inc(cols_done, 1)
            act.wait_ge(cols_done, 2)
            for h in range(H):
                act.wait_ge(bc_done, h + 1)
                if h >= 1:
                    act.wait_ge(num_done, NT * h)
                for j in range(NT):
                    t0, nt = seq_of(j)
                    i = j - t0
                    for d in range(2):
                        lo, hi = (i * P, nt * P) if d == 0 else (0, (i + 1) * P)
                        if nt == 4:
                            src, dst = ps[:, 2 * d, lo:hi], wsA[:, d, i, lo:hi]
                        else:
                            src, dst = ps[:, 1, 256 * d + lo:256 * d + hi], wsB[:, d, i, lo:hi]
                        r = 32 * d + h
                        a.activation(dst, src, ACT.Exp, bias=acol[:, j, r:r + 1]).then_inc(w_exp, 1)
            MU = NT * H

            def exps(m):
                nt = seq_of(m % NT)[1]
                act.wait_ge(nm_done, m + 1)
                if m >= 2:
                    act.wait_ge(comb_done, m - 1)
                else:
                    act.wait_ge(num_done, MU)
                for c in range(2):
                    a.activation(prob[:, m % 2, c, 0:nt * P], ps[:, 2 * (m % 2) + c, 0:nt * P], ACT.Exp,
                                 bias=nmax[:, m % 2, c:c + 1], scale=QK ** -0.5,
                                 accum_out=z[:, m % 2, c:c + 1]).then_inc(prob_exp, 1)

            def copy_turned(m):
                nt = seq_of(m % NT)[1]
                act.wait_ge(ctr_done, m + 1)
                if m >= 2:
                    act.wait_ge(att_mm, m - 1)
                a.activation(combT[:, m % 2, 0:nt * P], ps[:, 4 + m % 2, 0:nt * P], ACT.Copy).then_inc(combT_done, 1)

            def take_att(m):
                h, t = divmod(m, NT)
                act.wait_ge(att_mm, m + 1)
                a.activation(att[:, t, h * P:(h + 1) * P], ps[:, 6 + m % 2, 0:P], ACT.Copy)
                if m >= 1:
                    act.wait_ge(att_done, m)
                a.activation(junk_sq, ps[:, 6 + m % 2, 0:P], ACT.Square,
                             accum_out=ass_[:, t * H + h:t * H + h + 1]).then_inc(att_done, 1)

            for m in range(MU + 2):
                if m < MU:
                    exps(m)
                if 1 <= m <= MU:
                    copy_turned(m - 1)
                if m >= 2:
                    take_att(m - 2)
            act.wait_ge(cvar, 2)
            a.activation(ars, ars, ACT.Sqrt).then_inc(crstd, 1)
            a.activation(mrs, mrs, ACT.Sqrt).then_inc(crstd, 1)
            for t in range(NT):
                act.wait_ge(ctrans, 2 * t + 1)
                a.activation(catT[:, 0:H, t * P:(t + 1) * P], ps[:, 0, :].rearrange("p (c n) -> p c n", c=4), ACT.Copy,
                             scale=again08).then_inc(cat_done, 1)
                act.wait_ge(ctrans, 2 * t + 2)
                for h in range(H):
                    ins = a.activation(catT[:, H + h, t * P:(t + 1) * P], ps[:, 1, h * P:(h + 1) * P], ACT.Copy,
                                       scale=mgain[:, h:h + 1])
                ins.then_inc(cat_done, 1)

            act.wait_ge(out_added, 2 * NT)
            norm("ffn")
            norm_copies("ffn")
            for q in range(2 * PH):
                act.wait_ge(pq_done, q + 1)
                if q >= 2:
                    act.wait_ge(ps_done, q - 1)
                a.activation(qT[:, q % 2, 0:512], ps[:, 2 + 2 * (q % 2), :], ACT.Copy)
                a.activation(qT[:, q % 2, 512:TOK], ps[:, 3 + 2 * (q % 2), 0:256], ACT.Copy).then_inc(pq_copied, 1)
            with act.Fori(0, NT) as t:
                act.wait_ge(best_ready, t + 1)
                a.activation(gate, bestv.rearrange("p a b -> p (a b)"), ACT.Exp).then_inc(gate_e, 1)
                act.wait_ge(dots_done, t + 1)
                a.activation(coef, dots, ACT.Gelu).then_inc(gelu_done, 1)
            act.wait_ge(x_done, NT)
            norm("ple")
            norm_copies("ple")
            for g in range(2 * NT):
                act.wait_ge(pg_done, g + 1)
                if g >= 2:
                    act.wait_ge(pp_used, g - 1)
                a.activation(sig[:, g % 2], ps[:, 2 + 2 * (g % 2), :], ACT.Sigmoid).then_inc(pg_sig, 1)
            act.wait_ge(pp_used, 2 * NT)
            norm("fin")

        @block.vector
        def _(dve):
            v = nc.vector
            steps = [0]

            def link(ins):
                steps[0] += 1
                ins.then_inc(dve_step, 1)
                dve.wait_ge(dve_step, steps[0])

            def norm(k, gain, loads):
                dve.wait_ge(N[k]["ssq"], NT)
                link(v.tensor_scalar(var, ssq, 1.0 / D, EPS, ALU.mult, ALU.add))
                v.reciprocal(var, var).then_inc(N[k]["var"], 1)
                dve.wait_ge(N[k]["rstd"], 1)
                dve.wait_ge(wbc_ready, 16 * loads)
                for t in range(NT):
                    if k == "fin":
                        if t >= 2:
                            dve.wait_ge(y_out[t % 2], 16 * (t // 2))
                    elif t >= 2:
                        dve.wait_ge(N[k]["trans"], 2 * (t - 1))
                    v.scalar_tensor_tensor((hn if k == "mix" else hn2)[:, t % 2], X[:, t], rstd[:, t:t + 1], gain,
                                           ALU.mult, ALU.mult).then_inc(y_ready if k == "fin" else N[k]["hn"], 1)

            norm("mix", wbc, 1)

            dve.wait_ge(consts_ready, 16 * 6)
            for kind, name in enumerate(("i", "f")):
                dve.wait_ge(gates_done, kind + 1)
                v.tensor_scalar(gates[name][:, 0:512], ps[0:36, 2 + kind, :], gb[0:36, kind:kind + 1], None,
                                ALU.add).then_inc(gates_copied, 1)
                v.tensor_scalar(gates[name][:, 512:TOK], ps[0:36, 4 + kind, 0:256], gb[0:36, kind:kind + 1], None,
                                ALU.add).then_inc(gates_copied, 1)
            dve.wait_ge(gates_copied, 4)
            v.scalar_tensor_tensor(gates["e"], gates["f"], -1.0, gates["f"], ALU.mult, ALU.max).then_inc(gate_abs, 1)
            dve.wait_ge(lam_ready, 16)
            for i in range(2):
                if i:
                    dve.wait_ge(lam_sum, 1)
                v.tensor_tensor_reduce(junk_sq[:, 0:QK], lq[:, 2 * i], lq[:, 2 * i + 1], 1.0, 0.0, ALU.mult, ALU.add,
                                       lsum[:, i:i + 1]).then_inc(lam_sum, 1)
            v.tensor_scalar(again08, again, 1.0 - LAM_INIT, None, ALU.mult).then_inc(lam_done, 1)

            def convolve(c):
                dve.wait_ge(proj_copied, 2 * (c + 1))
                for k in range(5):
                    for src, dst, n in ((preA, mT[:, c, 0:512], 512), (preB, mT[:, c, 512:TOK], 256)):
                        w = convw[:, c, k:k + 1]
                        if k == 0:
                            ins = v.tensor_scalar(dst, src[:, c, 0:n], w, None, ALU.mult)
                        else:
                            ins = v.scalar_tensor_tensor(dst, src[:, c, k:k + n], w, dst, ALU.mult, ALU.add)
                    if k < 4:
                        link(ins)
                ins.then_inc(conv_done, 1)

            dve.wait_ge(made, 6)
            for c in range(H):
                convolve(c)
            dve.wait_ge(gate_ln, 1)
            link(v.scalar_tensor_tensor(gates["f"], gates["f"], 0.0, gates["e"], ALU.min, ALU.subtract))

            def scan(dst, src, op):
                for t0, nt in SEQS:
                    cols = slice(t0 * P, (t0 + nt) * P)
                    v.tensor_tensor_scan(dst[0:32, cols], src[0:32, cols], src[0:32, cols], 0.0, op, ALU.bypass)
                    ins = v.tensor_tensor_scan(dst[32:36, cols][:, ::-1], src[32:36, cols][:, ::-1],
                                               src[32:36, cols][:, ::-1], 0.0, op, ALU.bypass)
                link(ins)
            scan(gates["B"], gates["f"], ALU.add)
            link(v.tensor_tensor(gates["i"], gates["i"], gates["B"], ALU.subtract))
            scan(gates["M"], gates["i"], ALU.max)
            v.tensor_tensor(gates["f"], gates["B"], gates["M"], ALU.add).then_inc(rows_done, 1)
            dve.wait_ge(lam_exp, 1)
            v.tensor_scalar(nlam, lexp[:, 1:2], lexp[:, 0:1], LAM_INIT, ALU.subtract, ALU.subtract).then_inc(lam_done, 1)
            for c in range(H, 2 * H):
                convolve(c)

            for u in range(2 * NT):
                t = u % NT
                i = t - seq_of(t)[0]
                dve.wait_ge(proj_copied, PROJ_ENDS[3] + u + 1)
                x = stg[:, u % 2].rearrange("p (g n) -> p g n", g=8)
                x1, x2 = x[:, :, 0:HALF], x[:, :, HALF:2 * HALF]
                cos, sin = (ropet[:, i, j:j + 1, :].to_broadcast([P, 8, HALF]) for j in range(2))
                if u:
                    dve.wait_ge(rope_done, u)
                v.tensor_tensor(rot[:, 0], x1, cos, ALU.mult)
                v.tensor_tensor(rot[:, 1], x2, sin, ALU.mult)
                v.tensor_tensor(rot[:, 2], x2, cos, ALU.mult)
                link(v.tensor_tensor(rot[:, 3], x1, sin, ALU.mult))
                v.tensor_tensor(x1, rot[:, 0], rot[:, 1], ALU.subtract)
                v.tensor_tensor(x2, rot[:, 2], rot[:, 3], ALU.add).then_inc(rope_done, 1)

            KSCALE = float(P) ** -0.5
            dve.wait_ge(cols_done, 2)
            for h in range(H):
                for j in range(NT):
                    n = NT * h + j
                    t0, nt = seq_of(j)
                    i = j - t0
                    dve.wait_ge(s_done, n + 1)
                    dve.wait_ge(w_mask, 2 * n + 2)
                    for d in range(2):
                        lo, hi = (i * P, nt * P) if d == 0 else (0, (i + 1) * P)
                        w = (wsA if nt == 4 else wsB)[:, d, i, lo:hi]
                        ins = v.scalar_tensor_tensor(w, ps[:, 3 + n % 2, lo:hi], KSCALE, w, ALU.mult, ALU.mult)
                    ins.then_inc(ws_ready, 1)
                for t in range(NT):
                    m = NT * h + t
                    dve.wait_ge(num_done, m + 1)
                    num = ps[:, 5 + 2 * (m % 2), 0:2 * (P + 1)].rearrange("p (d n) -> p d n", d=2)
                    link(v.tensor_tensor(den, num[:, :, P], floor[:, t, h:h + 33:32], ALU.max))
                    link(v.scalar_tensor_tensor(den, num[:, :, P], -1.0, den, ALU.mult, ALU.max))
                    link(v.reciprocal(rden, den))
                    hs = hsum[:, m % 2]
                    if m >= 2:
                        dve.wait_ge(mem_squared, m - 1)
                    link(v.tensor_scalar(hs, num[:, 0, 0:P], rden[:, 0:1], None, ALU.mult))
                    ins = v.scalar_tensor_tensor(hs, num[:, 1, 0:P], rden[:, 1:2], hs, ALU.mult, ALU.add)
                    ins.then_inc(num_used, 1)
                    dve.wait_ge(num_used, m + 1)
                    o = mo[:, t, h * P:(h + 1) * P]
                    link(v.tensor_tensor(o, o, hs, ALU.mult))
                    v.tensor_tensor_reduce(hs, o, o, 1.0, 0.0, ALU.mult, ALU.add, mss[:, t * H + h:t * H + h + 1]).then_inc(mem_squared, 1)

            MU = NT * H

            def maxima(m):
                nt = seq_of(m % NT)[1]
                dve.wait_ge(sc_done, m + 1)
                b = 2 * (m % 2)
                link(v.tensor_reduce(nmax[:, m % 2], ps[:, b:b + 2, 0:nt * P], AX.X, ALU.max, negate=True))
                v.tensor_scalar(nmax[:, m % 2], nmax[:, m % 2], QK ** -0.5, None, ALU.mult).then_inc(nm_done, 1)

            def combine(m):
                nt = seq_of(m % NT)[1]
                s = m % 2
                dve.wait_ge(prob_exp, 2 * (m + 1))
                if m:
                    dve.wait_ge(comb_done, m)
                link(v.reciprocal(rz, z[:, s]))
                p0, p1 = prob[:, s, 0, 0:nt * P], prob[:, s, 1, 0:nt * P]
                v.tensor_scalar(p0, p0, rz[:, 0:1], None, ALU.mult)
                link(v.tensor_scalar(nl, rz[:, 1:2], nlam, None, ALU.mult))
                if m >= 2:
                    dve.wait_ge(ctr_done, m - 1)
                v.scalar_tensor_tensor(comb[:, s, 0:nt * P], p1, nl, p0, ALU.mult, ALU.add).then_inc(comb_done, 1)

            dve.wait_ge(lam_done, 2)
            for m in range(MU + 1):
                if m < MU:
                    maxima(m)
                if m >= 1:
                    combine(m - 1)

            dve.wait_ge(mem_squared, MU)
            link(v.tensor_scalar(mrs, mss, 1.0 / P, EPS, ALU.mult, ALU.add))
            v.reciprocal(mrs, mrs).then_inc(cvar, 1)
            dve.wait_ge(att_done, MU)
            link(v.tensor_scalar(ars, ass_, 1.0 / P, EPS, ALU.mult, ALU.add))
            v.reciprocal(ars, ars).then_inc(cvar, 1)
            dve.wait_ge(crstd, 2)
            for t in range(NT):
                for arr, r in ((att, ars), (mo, mrs)):
                    x = arr[:, t].rearrange("p (h n) -> p h n", h=H)
                    v.tensor_tensor(x, x, r[:, t * H:(t + 1) * H].unsqueeze(2).to_broadcast([P, H, P]),
                                    ALU.mult).then_inc(cnorm, 1)

            for g in range(2 * NT):
                i, t = divmod(g, NT)
                dve.wait_ge(out_done, g + 1)
                dve.wait_ge(x_ready[t], 32)
                x = X[:, t, 512 * i:512 * i + 512]
                v.tensor_tensor(x, ps[:, 2 + g % 4, :], x, ALU.add).then_inc(out_added, 1)

            dve.wait_ge(out_added, 2 * NT)
            norm("ffn", wbc2, 2)
            for q in range(2 * PH):
                dve.wait_ge(ps_done, q + 1)
                v.tensor_copy(scores[:, 0:4, q, :], ps[:, 6, :].rearrange("p (t n) -> p t n", t=4))
                v.tensor_copy(scores[:, 4:6, q, :], ps[:, 7, 0:256].rearrange("p (t n) -> p t n", t=2)).then_inc(ps_copied, 1)
            dve.wait_ge(ps_copied, 2 * PH)
            v.memset(acc, 0.0).then_inc(row_used, RING)
            dve.wait_ge(mk, 2)

            def wait_for(signal, value):
                dve.wait_ge(signal, value)
                if not isinstance(value, int):
                    dve.sem_inc(dve_held, 1)

            def choose(t):
                k = [0]

                def tlink(ins):
                    k[0] += 1
                    ins.then_inc(topk_step, 1)
                    wait_for(topk_step, t * TOPK_STEPS + k[0])

                def top16(vals, inds, src):
                    tlink(v.max(vals[:, 0:8], src))
                    v.max_index(inds[:, 0:8], vals[:, 0:8], src)
                    tlink(v.match_replace(src, vals[:, 0:8], src, NEG))
                    tlink(v.max(vals[:, 8:16], src))
                    return v.max_index(inds[:, 8:16], vals[:, 8:16], src)

                tlink(v.tensor_copy(now, scores_flat[:, bass.ds(t * (2 * PH * P), 2 * PH * P)]))
                for h in range(PH):
                    for half in range(2):
                        last = top16(topv[:, h, half], topi[:, h, half], now[:, (2 * h + half) * P:(2 * h + half + 1) * P])
                tlink(last)
                tlink(v.tensor_copy(topf, topi))
                tlink(v.tensor_tensor(cand.rearrange("p h (i j) -> p h i j", i=K16),
                                      topv[:, :, 0].unsqueeze(3).to_broadcast([P, PH, K16, K16]),
                                      topv[:, :, 1].unsqueeze(2).to_broadcast([P, PH, K16, K16]), ALU.add))
                for h in range(PH):
                    last = top16(bestv[:, h], bestc[:, h], cand[:, h])
                tlink(last)
                for shift, half, e in ((True, 0, e1), (False, 1, e2)):
                    c = bestc.rearrange("p a b -> p (a b)")
                    if shift:
                        tlink(v.tensor_scalar(rank_u, c, 4, None, ALU.logical_shift_right))
                    else:
                        tlink(v.tensor_scalar(rank_u, c, 15, None, ALU.bitwise_and))
                    tlink(v.tensor_copy(rank, rank_u))
                    tlink(v.tensor_tensor(onehot, rank.unsqueeze(2).to_broadcast([P, NSLOT, K16]),
                                          iota16.unsqueeze(1).to_broadcast([P, NSLOT, K16]), ALU.is_equal))
                    oh = onehot.rearrange("p (h j) r -> p h j r", h=PH)
                    tlink(v.tensor_tensor(oh, oh, topf[:, :, half].unsqueeze(2).to_broadcast([P, PH, K16, K16]), ALU.mult))
                    tlink(v.tensor_reduce(e, onehot, AX.X, ALU.add))
                tlink(v.scalar_tensor_tensor(e1, e1, float(P), e2, ALU.mult, ALU.add))
                v.tensor_copy(idx[:, bass.ds(t * NSLOT, NSLOT)], e1).then_inc(idx_ready, 1)
                tlink(v.tensor_copy(gsum, bestv[:, :, 0]))
                v.tensor_tensor(bestv, bestv, gsum.unsqueeze(2).to_broadcast([P, PH, K16]), ALU.subtract).then_inc(best_ready, 1)
                wait_for(gate_e, t + 1)
                g3 = gate.rearrange("p (h n) -> p h n", h=PH)
                tlink(v.tensor_reduce(gsum, g3, AX.X, ALU.add))
                tlink(v.reciprocal(gsum, gsum))
                tlink(v.tensor_tensor(g3, g3, gsum.unsqueeze(2).to_broadcast([P, PH, K16]), ALU.mult))
                assert k[0] == TOPK_STEPS, k[0]

            def dots_of(t):
                v.scalar_tensor_tensor(xn, arena[:, bass.ds(t * D, D)], rstd[:, bass.ds(t, 1)], wbc2,
                                       ALU.mult, ALU.mult).then_inc(xn_step, 1)
                wait_for(xn_step, t + 1)
                with dve.Fori(0, NSLOT // RING) as b:
                    n = t * (2 * NSLOT // RING) + b
                    for s in range(RING):
                        wait_for(row_ready[s], n * 16 + 16)
                        v.tensor_tensor_reduce(rows[:, s], rows[:, s], xn, 1.0, 0.0, ALU.mult, ALU.add,
                                               dots_now[:, s:s + 1]).then_inc(row_used, 1)
                    wait_for(row_used, n * RING + 2 * RING)
                    v.tensor_copy(dots[:, bass.ds(b * RING, RING)], dots_now).then_inc(dots_copied, 1)
                    wait_for(dots_copied, t * (NSLOT // RING) + b + 1)
                v.memset(acc, 0.0).then_inc(dots_done, 1)
                wait_for(gelu_done, t + 1)
                v.tensor_tensor(coef, coef, gate, ALU.mult).then_inc(coef_done, 1)

            def sum_of(t):
                wait_for(coef_done, t + 1)
                with dve.Fori(0, NSLOT // RING) as b:
                    n = t * (2 * NSLOT // RING) + NSLOT // RING + b
                    for s in range(RING):
                        wait_for(row_ready[s], n * 16 + 16)
                        wait_for(row_used, n * RING + RING + s)
                        v.scalar_tensor_tensor(acc, rows[:, s], coef[:, bass.ds(b * RING + s, 1)], acc,
                                               ALU.mult, ALU.add).then_inc(row_used, 1)
                wait_for(row_used, (t + 1) * (2 * NSLOT) + RING)
                x = arena[:, bass.ds(t * D, D)]
                v.tensor_tensor(x, x, acc, ALU.add).then_inc(x_done, 1)
                wait_for(x_done, t + 1)

            choose(0)
            with dve.Fori(0, NT - 1) as t:
                dots_of(t)
                choose(t + 1)
                sum_of(t)
            dots_of(NT - 1)
            sum_of(NT - 1)

            norm("ple", wbc2, 3)
            for g in range(2 * NT):
                i, t = divmod(g, NT)
                dve.wait_ge(pg_sig, g + 1)
                if g >= 2:
                    dve.wait_ge(pp_used, g - 1)
                link(v.tensor_tensor(plp[:, g % 2], ps[:, 3 + 2 * (g % 2), :], sig[:, g % 2], ALU.mult))
                x = X[:, t, 512 * i:512 * i + 512]
                v.tensor_tensor(x, x, plp[:, g % 2], ALU.add).then_inc(pp_used, 1)
            dve.wait_ge(pp_used, 2 * NT)
            norm("fin", wbc2, 4)


def kernel(**inputs):
    import numpy as np
    import concourse.bacc as bacc
    from concourse.bass_utils import run_bass_kernel_spmd

    def arr(name):
        return np.ascontiguousarray(inputs[name])

    w_in = arr("w_in")[0]
    gb = arr("gate_bias")[0]
    gate_w = np.zeros((D, 2, 36), w_in.dtype)
    gate_b = np.zeros((36, 2), gb.dtype)
    for d in range(2):
        for kind in range(2):
            c = 8 * d + 4 * kind
            gate_w[:, kind, 32 * d:32 * d + H] = w_in[:, GATE0 + c:GATE0 + c + H]
            gate_b[32 * d:32 * d + H, kind] = gb[c:c + H]
    half = np.arange(0, 2 * HALF, 2, dtype=np.float32) / np.float32(2 * HALF)
    inv = np.float32(500000.0) ** -half
    ang = np.arange(SEQS[0][1] * P, dtype=np.float32)[:, None] * inv[None, :]
    rope = np.stack([np.cos(ang), np.sin(ang)], axis=1).astype(np.float32)
    arrays = {
        "x_a": arr("x_prompt")[0], "x_b": arr("x_sample")[0],
        "pT_a": arr("p_prompt")[0, 0].T, "pT_b": arr("p_sample")[0, 0].T,
        "norm_mix": arr("norm_mix")[0], "w_in": w_in,
        "gate_w": gate_w, "gate_b": gate_b,
        "conv_w": arr("conv_qk")[0].T.reshape(2 * H, P, 5).transpose(1, 0, 2),
        "lambda_qk": arr("lambda_qk")[0], "attn_gain": arr("attn_gain")[0][:, None],
        "mlstm_gain": arr("mlstm_gain")[0].reshape(H, P).T,
        "w_out": arr("w_out")[0], "norm_ffn": arr("norm_ffn")[0], "peer_wq": arr("peer_wq")[0],
        "subkeysT": arr("peer_subkeys")[0].reshape(2 * PH, P, P).transpose(2, 0, 1),
        "peer_u": arr("peer_u")[0], "peer_v": arr("peer_v")[0], "norm_ple": arr("norm_ple")[0],
        "ple_w_gate": arr("ple_w_gate")[0], "ple_w_proj": arr("ple_w_proj")[0],
        "norm_final": arr("norm_final"), "rope": rope,
    }
    arrays = {k: np.ascontiguousarray(a) for k, a in arrays.items()}
    nc = bacc.Bacc("TRN2", target_bir_lowering=False, num_devices=1)
    args = [nc.dram_tensor(k, a.shape, mybir.dt.from_np(a.dtype), kind="ExternalInput").ap() for k, a in arrays.items()]
    args += [nc.dram_tensor(k, (n, D), F32, kind="ExternalOutput").ap() for k, n in (("y_a", 4 * P), ("y_b", 2 * P))]
    hymba_layer(nc, *args)
    got = run_bass_kernel_spmd(nc, [arrays], core_ids=[0]).results[0]
    return got["y_a"].reshape(1, 4 * P, D), got["y_b"].reshape(1, 2 * P, D)
```

```python
from contextlib import ExitStack

import concourse.bass as bass
from concourse import mybir

ALU = mybir.AluOpType
ACT = mybir.ActivationFunctionType
AX = mybir.AxisListType
F32 = mybir.dt.float32
U32 = mybir.dt.uint32
BF16 = mybir.dt.bfloat16

P = 128
D = 1024
DC = D // P
NT = 6
TOK = NT * P
SEQS = [(0, 4), (4, 2)]
H = 4
HALF = 8
QK = 64
NGATE = 16
PH = 8
K16 = 16
NSLOT = PH * K16
EPS = 1e-6
LAM_INIT = 0.2
NEG = -3.0e38
NK = 128
TU = 8
ND = NT - 1
DTOK = ND * P
HALF_T = DTOK // 2
UNITS = P // TU
RING = 2
TAIL_ROWS = 6
NBANK = 5
GRP = 4
NGRP = NK // GRP
U_FIRST = 4
TOPK_STEPS = 48 + 2 + 25 + 10 + 1 + 2

BLOCKS = [("mq", 1536), ("mk", 2048), ("mv", 2560), ("mo", 3072), ("aq", 0), ("ak", 512), ("av", 1024)]
GATE0 = 3584
NIN = len(BLOCKS)


def hymba_layer(nc, x_a, x_b, pT_a, pT_b, norm_mix, w_in, gate_w, gate_b, conv_w, lambda_qk, attn_gain,
                mlstm_gain, w_out, norm_ffn, peer_wq, subkeysT, uT, peer_u, peer_v, norm_ple,
                ple_w_gate, ple_w_proj, norm_final, rope, y_a, y_b):
    ctx = ExitStack()
    with ctx:
        def sb(name, shape, dt=F32):
            return ctx.enter_context(nc.sbuf_tensor(name, shape, dt))

        def sem(name):
            return ctx.enter_context(nc.semaphore(name))


        WORDS = 48640
        arena = sb("arena", [P, WORDS])

        def view(at, *dims):
            n = 1
            for d in dims:
                n *= d
            assert at + n <= WORDS, (at, dims)
            v = arena[:, at:at + n]
            if len(dims) == 2:
                return v.rearrange("p (a b) -> p a b", a=dims[0])
            if len(dims) == 3:
                return v.rearrange("p (a b c) -> p a b c", a=dims[0], b=dims[1])
            return v

        X = view(0, NT, D)
        HT_AT = NT * D
        hT = view(HT_AT, DC, TOK)
        catT = hT
        W_AT = HT_AT + DC * TOK
        W = view(W_AT, 2, DC, 512)
        FREE = W_AT + 2 * DC * 512

        preA = view(FREE, 2 * H, 516)
        preB = view(FREE + 2 * H * 516, 2 * H, 260)
        aT = view(FREE, 2 * H, TOK)
        at = FREE + 2 * H * (516 + 260)
        mT = view(at, 2 * H, TOK)
        att = view(at, NT, H * P)
        at += 2 * H * TOK
        vm = view(at, NT, H, P + 1)
        at += NT * H * (P + 1)
        mo = view(at, NT, H * P)
        at += NT * H * P
        av = view(at, NT, H * P)
        at += NT * H * P
        wsA = view(at, 2, 4, 512)
        wsB = view(at + 4096, 2, 2, 256)
        hn = view(at, 2, D)
        junk = view(at + 2 * D, D)
        stg = view(at + 3 * D, 2, 512)
        prob = view(at, 2, 2, 512)
        comb = view(at + 2048, 2, 512)
        combT = view(at + 3072, 2, 512)
        at += 2 * 4 * 512 + 2 * 2 * 256
        wbc = view(at, D)
        at += D
        junk_sq = wbc[:, 0:P]
        rot = wbc[:, P:P + 256].rearrange("p (a g n) -> p a g n", a=4, g=8)
        lq = wbc[:, 512:768].rearrange("p (a b) -> p a b", a=4)
        gates = {}
        for i, name in enumerate(("i", "f", "e", "B", "M")):
            gates[name] = arena[0:36, i * TOK:(i + 1) * TOK]
        sel = view(4 * D, 2 * H, P)[0:36]
        assert at <= WORDS, at

        R1 = HT_AT
        uf = view(R1, 4, DC * NK)
        ubf = arena[:, R1 + 4 * D:R1 + 6 * D].bitcast(BF16)
        uh = [ubf[:, (2 * i) * D:(2 * i + 1) * D].rearrange("p (c n) -> p c n", c=DC) for i in range(2)]
        ul = [ubf[:, (2 * i + 1) * D:(2 * i + 2) * D].rearrange("p (c n) -> p c n", c=DC) for i in range(2)]
        G_AT = R1 + 6 * D
        gst = view(G_AT, NK, P)
        X_AT = G_AT + NK * P
        xbf = arena[:, X_AT:X_AT + DC * DTOK].bitcast(BF16)
        xh = xbf[:, 0:DC * DTOK].rearrange("p (c n) -> p c n", c=DC)
        xl = xbf[:, DC * DTOK:2 * DC * DTOK].rearrange("p (c n) -> p c n", c=DC)
        S_AT = X_AT + DC * TOK
        now = view(S_AT, 2 * PH * P)
        cand = view(S_AT + 2048, PH, K16 * K16)
        onehot = view(S_AT + 4096, NSLOT, K16)
        hn2 = view(S_AT, 2, D)
        junk2 = view(S_AT + 2 * D, D)
        wbc2 = view(S_AT + 3 * D, D)
        O_AT = S_AT + 6144
        oh = view(O_AT, 2 * TU, 2, NK)
        gst_a = view(O_AT + 4096, 2, DTOK)
        E_AT = O_AT + 4096 + 2 * DTOK
        xn = view(E_AT, D)
        rows = [view(E_AT + D, D), view(X_AT + DC * DTOK, D)]
        assert E_AT + 2 * D <= WORDS
        subk = view(O_AT, 2 * PH, P)
        qT = view(O_AT + 2048, 2, TOK)
        sst = view(O_AT + 3584, 2, NT, P)
        assert X_AT + DC * DTOK + D <= S_AT

        vf = view(G_AT, 2, GRP, D)
        vbf = arena[:, G_AT + 2 * GRP * D:G_AT + 4 * GRP * D].bitcast(BF16).rearrange(
            "p (s a k n) -> p s a k n", s=2, a=2, k=GRP)
        af = [view(at, GRP, DTOK) for at in (S_AT, X_AT)]
        gf = [view(at + GRP * DTOK, GRP, DTOK) for at in (S_AT, X_AT)]
        assert X_AT + 2 * GRP * DTOK <= X_AT + DC * DTOK
        abf = arena[:, O_AT:O_AT + 2 * GRP * DTOK].bitcast(BF16).rearrange(
            "p (s a k n) -> p s a k n", s=2, a=2, k=GRP)
        assert O_AT + 2 * GRP * DTOK <= E_AT

        pT = view(X_AT, 2, TOK)
        wp = view(X_AT + 2 * TOK, 2, D)
        sig = view(O_AT, 2, 512)
        plp = view(O_AT + 1024, 2, 512)

        small = sb("small", [P, 1024])
        spos = [0]

        def tiny(*dims, dt=F32):
            n = 1
            for d in dims:
                n *= d
            v = small[:, spos[0]:spos[0] + n]
            spos[0] += n
            assert spos[0] <= 1024
            if dt != F32:
                v = v.bitcast(dt)
            if len(dims) == 2:
                v = v.rearrange("p (a b) -> p a b", a=dims[0])
            elif len(dims) == 3:
                v = v.rearrange("p (a b c) -> p a b c", a=dims[0], b=dims[1])
            return v

        ident = sb("ident", [P, P])
        gw = sb("gw", [P, DC, 2, 36])
        gb = tiny(2)
        convw = tiny(2 * H, 5)
        again = tiny(1)
        again08 = tiny(1)
        mgain = tiny(H)
        ropet = tiny(4, 2, HALF)
        ssq = tiny(NT)
        var = tiny(NT)
        rstd = tiny(NT)
        lsum = tiny(2)
        lexp = tiny(2)
        nlam = tiny(1)
        acol = tiny(NT, 36)
        floor = tiny(NT, 36)
        den = tiny(2)
        rden = tiny(2)
        hsum = tiny(2, P)
        mss = tiny(NT * H)
        ass_ = tiny(NT * H)
        mrs = tiny(NT * H)
        ars = tiny(NT * H)
        nmax = tiny(2, 2)
        z = tiny(2, 2)
        rz = tiny(2)
        nl = tiny(1)
        pk = sb("pk", [P, 2740])
        kp = [0]

        def peer_tiny(*dims, dt=F32):
            n = 1
            for d in dims:
                n *= d
            v = pk[:, kp[0]:kp[0] + n]
            kp[0] += n
            assert kp[0] <= 2740
            if dt != F32:
                v = v.bitcast(dt)
            if len(dims) == 2:
                v = v.rearrange("p (a b) -> p a b", a=dims[0])
            elif len(dims) == 3:
                v = v.rearrange("p (a b c) -> p a b c", a=dims[0], b=dims[1])
            return v

        topv = peer_tiny(PH, 2, K16)
        topi = peer_tiny(PH, 2, K16, dt=U32)
        topf = peer_tiny(PH, 2, K16)
        bestv = peer_tiny(PH, K16)
        bestc = peer_tiny(PH, K16, dt=U32)
        rank_u = peer_tiny(NSLOT, dt=U32)
        rank = peer_tiny(NSLOT)
        e1 = peer_tiny(NSLOT)
        e2 = peer_tiny(NSLOT)
        gate = peer_tiny(NSLOT)
        eT = peer_tiny(3, P)
        iota_f = peer_tiny(NK)
        idx = peer_tiny(NSLOT, dt=U32)
        idx_now = peer_tiny(RING, dt=U32)
        gate0 = peer_tiny(NSLOT)
        dots = peer_tiny(NSLOT)
        coef = peer_tiny(NSLOT)
        dots_now = peer_tiny(UNITS)
        gsum = peer_tiny(PH)
        iota16 = peer_tiny(K16)

        ps = ctx.enter_context(nc.psum_tensor("ps", [P, 8, 512], F32))

        x_ready = [sem(f"x_ready{t}") for t in range(NT)]
        w_ready = [sem(f"w_ready{i}") for i in range(2)]
        lam_ready = sem("lam_ready")
        consts_ready = sem("consts_ready")
        wbc_ready = sem("wbc_ready")
        made = sem("made")
        mk = sem("mk")
        N = {k: {e: sem(f"{k}_{e}") for e in ("ssq", "var", "rstd", "hn", "trans", "hT")}
             for k in ("mix", "ffn", "ple", "fin")}
        gates_done, gates_copied = sem("gates_done"), sem("gates_copied")
        proj_done, proj_copied = sem("proj_done"), sem("proj_copied")
        rope_done, qk_trans, qk_copied = sem("rope_done"), sem("qk_trans"), sem("qk_copied")
        conv_done, silu_done = sem("conv_done"), sem("silu_done")
        gate_abs, gate_exp, gate_ln = sem("gate_abs"), sem("gate_exp"), sem("gate_ln")
        rows_done, cols_trans, cols_done = sem("rows_done"), sem("cols_trans"), sem("cols_done")
        bc_done, w_exp, w_mask = sem("bc_done"), sem("w_exp"), sem("w_mask")
        s_done, ws_ready = sem("s_done"), sem("ws_ready")
        num_done, num_used = sem("num_done"), sem("num_used")
        mem_squared = sem("mem_squared")
        lam_sum, lam_exp, lam_done = sem("lam_sum"), sem("lam_exp"), sem("lam_done")
        sc_done, nm_done, prob_exp = sem("sc_done"), sem("nm_done"), sem("prob_exp")
        comb_done, ctr_done, combT_done = sem("comb_done"), sem("ctr_done"), sem("combT_done")
        att_mm, att_done = sem("att_mm"), sem("att_done")
        cvar, crstd, cnorm, ctrans, cat_done = (sem(n) for n in ("cvar", "crstd", "cnorm", "ctrans", "cat_done"))
        out_done, out_added = sem("out_done"), sem("out_added")
        subk_ready = sem("subk_ready")
        pq_done, pq_copied, ps_done, ps_copied = (sem(n) for n in ("pq_done", "pq_copied", "ps_done", "ps_copied"))
        dve_step = sem("dve_step")
        topk_step = sem("topk_step")
        best_ready, gate_e = sem("best_ready"), sem("gate_e")
        score_ready, score_out, now_ready = sem("score_ready"), [sem("score_out0"), sem("score_out1")], sem("now_ready")
        x_split = sem("x_split")
        u_ready = [sem(f"u_ready{i}") for i in range(4)]
        uh_done, u_split = sem("uh_done"), sem("u_split")
        up_done = sem("up_done")
        gelu_done = sem("gelu_done")
        ga_out = [sem("ga_out0"), sem("ga_out1")]
        chosen, tab_trans, tab_done, gate_ready = sem("chosen"), sem("tab_trans"), sem("tab_done"), sem("gate_ready")
        oh_ready = sem("oh_ready")
        g_mm, g_evac = sem("g_mm"), sem("g_evac")
        g_out = sem("g_out")
        x_done, weighed = sem("x_done"), sem("weighed")
        held = {e: sem(f"held_{e}") for e in ("dve", "pool", "act")}
        idx_ready, idx_staged = sem("idx_ready"), sem("idx_staged")
        row_ready = [sem("row_ready0"), sem("row_ready1")]
        row_used = sem("row_used")
        dots_copied, dots_done, coef_gelu, coef_done, xn_done = (sem(n) for n in (
            "dots_copied", "dots_done", "coef_gelu", "coef_done", "xn_done"))
        v_ready = [sem("v_ready0"), sem("v_ready1")]
        ga_ready = [sem("ga_ready0"), sem("ga_ready1")]
        vh_done = sem("vh_done")
        vl_done = sem("vl_done")
        act_done = sem("act_done")
        dn_done = sem("dn_done")
        add_done = sem("add_done")
        ple_ready = sem("ple_ready")
        pg_done, pg_sig, pp_used = sem("pg_done"), sem("pg_sig"), sem("pp_used")
        y_ready, y_out = sem("y_ready"), [sem("y_out0"), sem("y_out1")]

        block = ctx.enter_context(nc.Block())

        def seq_of(t):
            return SEQS[0] if t < 4 else SEQS[1]

        def x_rows(t):
            src = x_a if t < 4 else x_b
            r = (t - seq_of(t)[0]) * P
            return src[r:r + P, :]

        def row_of(w):
            return w.rearrange("(a n) -> a n", a=1).to_broadcast([P, D])

        scr_s = nc.dram_tensor("scr_scores", (NT, P, 2 * PH, P), F32, kind="Internal").ap()
        scr_a = nc.dram_tensor("scr_gelu", (NK, P, DTOK), F32, kind="Internal").ap()
        scr_g = nc.dram_tensor("scr_gates", (NK, P, DTOK), F32, kind="Internal").ap()
        v_rows = peer_v.rearrange("(a b) d -> a b d", b=NK)

        def wait_for(eng, signal, value):
            eng.wait_ge(signal, value)
            if not isinstance(value, int):
                eng.sem_inc(held[{nc.vector.engine: "dve", nc.gpsimd.engine: "pool", nc.scalar.engine: "act"}[eng.engine]], 1)

        w_blocks = [w_in[:, c:c + 512] for _, c in BLOCKS]
        w_blocks += [w_out[:, 512 * i:512 * i + 512] for i in range(2)]
        w_blocks += [peer_wq[:, 512 * i:512 * i + 512] for i in range(4)]
        PQ0 = NIN + 2
        PG0 = PQ0 + 4
        PROJ_ENDS = (8, 16, 22, 28, 34, 40, 46)

        def block_read(n):
            if n < NIN:
                return proj_done, PROJ_ENDS[n]
            if n < PQ0:
                return out_done, NT * (n - NIN + 1)
            return pq_done, 4 * (n - PQ0 + 1)
        w_blocks += [ple_w_gate[:, 512 * i:512 * i + 512] for i in range(2)]

        @block.sync
        def _(sp):
            def load_block(n):
                if 2 <= n < PG0:
                    sp.wait_ge(*block_read(n - 2))
                sp.dma_start(W[:, n % 2], w_blocks[n].rearrange("(c p) n -> p c n", p=P)).then_inc(w_ready[n % 2], 16)

            sp.dma_start(X[:, 0], x_rows(0)).then_inc(x_ready[0], 16)
            sp.dma_start(wbc, row_of(norm_mix)).then_inc(wbc_ready, 16)
            for t in range(1, NT):
                sp.dma_start(X[:, t], x_rows(t)).then_inc(x_ready[t], 16)
            sp.dma_start(gw[:], gate_w.rearrange("(c p) k n -> p c k n", p=P)).then_inc(consts_ready, 16)
            sp.dma_start(gb[0:36, :], gate_b).then_inc(consts_ready, 16)
            load_block(0)
            load_block(1)
            sp.dma_start(convw, conv_w).then_inc(consts_ready, 16)
            sp.dma_start(again, attn_gain).then_inc(consts_ready, 16)
            sp.dma_start(mgain, mlstm_gain).then_inc(consts_ready, 16)
            sp.dma_start(ropet, rope.rearrange("(t p) a b -> p t a b", p=P)).then_inc(consts_ready, 16)
            sp.wait_ge(N["mix"]["hn"], NT)
            sp.dma_start(lq, lambda_qk.rearrange("(o a) b -> o a b", o=1).to_broadcast([P, 4, QK])).then_inc(lam_ready, 16)
            for n in range(2, NIN + 2):
                load_block(n)
            sp.wait_ge(bc_done, H)
            for t in range(NT):
                sp.dma_start(X[:, t], x_rows(t)).then_inc(x_ready[t], 16)
            sp.wait_ge(att_done, NT * H)
            sp.wait_ge(cat_done, 2 * NT)
            sp.dma_start(wbc2, row_of(norm_ffn)).then_inc(wbc_ready, 16)
            sp.dma_start(subk, subkeysT).then_inc(subk_ready, 16)
            for n in range(NIN + 2, PG0):
                load_block(n)
            sp.wait_ge(ps_done, 2 * PH)
            sp.wait_ge(x_split, 2)
            with sp.Fori(0, NK // 4) as i:
                for k in range(4):
                    sp.wait_ge(u_split, i * 4 + k + 1)
                    sp.dma_start(uf[:, k], uT[bass.ds(i * 4 + k, 1)].rearrange("o p n -> (o p) n")).then_inc(u_ready[k], 16)
            def load_v(g, b):
                sp.wait_ge(vl_done, g * GRP + GRP)
                sp.dma_start(vf[:, b], v_rows[:, bass.ds(g * GRP, GRP), :]).then_inc(v_ready[b], 16)

            def load_weights(g, b):
                sp.wait_ge(act_done, g * GRP + GRP)
                sp.dma_start(af[b], scr_a[bass.ds(g * GRP, GRP)].rearrange("k p n -> p k n")).then_inc(ga_ready[b], 16)
                sp.dma_start(gf[b], scr_g[bass.ds(g * GRP, GRP)].rearrange("k p n -> p k n")).then_inc(ga_ready[b], 16)

            sp.wait_ge(g_out, 16 * ND + 16)
            load_v(0, 0)
            load_v(1, 1)
            for b in range(2):
                sp.wait_ge(ga_out[b], 16 * GRP // 2 + 16)
            load_weights(0, 0)
            sp.wait_ge(up_done, NK + 2)
            for b in range(2):
                sp.wait_ge(ga_out[b], 16 * NK // 2 + 16)
            load_weights(1, 1)
            with sp.Fori(1, NGRP // 2) as i:
                for b in range(2):
                    load_v(i * 2 + b, b)
                    load_weights(i * 2 + b, b)
            sp.wait_ge(x_done, 1)
            sp.dma_start(wbc2, row_of(norm_ple)).then_inc(wbc_ready, 16)
            sp.dma_start(pT[:, :, 0:512], pT_a.rearrange("(c p) n -> p c n", p=P)).then_inc(ple_ready, 16)
            sp.dma_start(pT[:, :, 512:TOK], pT_b.rearrange("(c p) n -> p c n", p=P)).then_inc(ple_ready, 16)
            sp.dma_start(wp, ple_w_proj.rearrange("(c p) n -> p c n", p=P)).then_inc(ple_ready, 16)
            load_block(PG0)
            load_block(PG0 + 1)
            sp.wait_ge(N["ple"]["hn"], NT)
            sp.dma_start(wbc2, row_of(norm_final)).then_inc(wbc_ready, 16)
            for t in range(NT):
                sp.wait_ge(y_ready, t + 1)
                dst = y_a if t < 4 else y_b
                r = (t - seq_of(t)[0]) * P
                sp.dma_start(dst[r:r + P, :], hn2[:, t % 2]).then_inc(y_out[t % 2], 16)
            for i in range(2):
                sp.wait_ge(y_out[i], 16 * (NT // 2))

        @block.gpsimd
        def _(pool):
            g = nc.gpsimd
            g.memset(ident[:], 0.0).then_inc(mk, 1)
            g.iota(iota16, pattern=[[1, K16]], base=0, channel_multiplier=0,
                   allow_small_or_imprecise_dtypes=True).then_inc(mk, 1)
            g.iota(iota_f, pattern=[[1, NK]], base=0, channel_multiplier=0,
                   allow_small_or_imprecise_dtypes=True).then_inc(mk, 1)
            pool.wait_ge(mk, 3)
            g.affine_select(out=ident[:], in_=ident[:], compare_op=ALU.not_equal, fill=1.0, base=0,
                            pattern=[[-1, P]], channel_multiplier=1).then_inc(made, 1)
            g.memset(preA[:, :, 0:2], 0.0).then_inc(made, 1)
            g.memset(preA[:, :, 514:516], 0.0).then_inc(made, 1)
            g.memset(preB[:, :, 0:2], 0.0).then_inc(made, 1)
            g.memset(preB[:, :, 258:260], 0.0).then_inc(made, 1)
            g.memset(vm[:, :, :, P:P + 1], 1.0).then_inc(made, 1)
            pool.wait_ge(N["mix"]["hn"], NT)
            pool.sem_inc(row_used, RING)
            g.memset(sel, 0.0).then_inc(mk, 1)
            pool.wait_ge(mk, 4)
            for i in range(2 * H):
                row = 32 * (i // H) + i % H
                g.affine_select(out=sel[:, i], in_=sel[:, i], compare_op=ALU.not_equal, fill=-1.0,
                                base=-row, pattern=[[0, P]], channel_multiplier=1).then_inc(made, 1)
            for h in range(H):
                for j in range(NT):
                    for d in range(2):
                        pool.wait_ge(w_exp, 2 * NT * h + 2 * j + d + 1)
                        t0, n = seq_of(j)
                        o = (j - t0) * P
                        w = (wsA if n == 4 else wsB)[:, d, j - t0, o:o + P]
                        sign = 1 if d == 0 else -1
                        g.affine_select(out=w, in_=w, compare_op=ALU.is_ge, fill=0.0, base=0,
                                        pattern=[[sign, P]], channel_multiplier=-sign).then_inc(w_mask, 1)
            for q in range(2 * PH):
                pool.wait_ge(ps_copied, q + 1)
                pool.dma_start(scr_s[:, :, q].rearrange("t p n -> p t n"), sst[:, q % 2]).then_inc(score_out[q % 2], 16)
            pool.sem_inc(u_split, 4)

            def split_u(i, k):
                n = i * 4 + k
                wait_for(pool, u_ready[k], i * 16 + 16)
                wait_for(pool, up_done, n + 1)
                src = uf[:, k].rearrange("p (c n) -> p c n", c=DC)
                g.tensor_copy(uh[k % 2], src).then_inc(uh_done, 1)
                wait_for(pool, uh_done, n + 1)
                g.tensor_tensor(ul[k % 2], src, uh[k % 2], ALU.subtract).then_inc(u_split, 1)

            def gather(table, r, slot, first):
                wait_for(pool, row_used, r + 1)
                g.tensor_copy(idx_now[:, slot:slot + 1], idx[:, bass.ds(r - first, 1)]).then_inc(idx_staged, 1)
                wait_for(pool, idx_staged, r + 1)
                g.indirect_dma_start(out=rows[slot], out_offset=None, in_=table,
                                     in_offset=bass.IndirectOffsetOnAxis(ap=idx_now[:, slot:slot + 1], axis=0),
                                     ).then_inc(row_ready[slot], 16)

            with pool.Fori(0, U_FIRST) as i:
                for k in range(4):
                    split_u(i, k)
            pool.wait_ge(idx_ready, 1)
            with pool.Fori(0, ND * UNITS // 4) as i:
                for k in range(4):
                    split_u(i + U_FIRST, k)
                    gather(peer_u, i * 4 + k, k % 2, 0)
            with pool.Fori(0, NK // 4 - U_FIRST - ND * UNITS // 4) as i:
                for k in range(4):
                    split_u(i + (U_FIRST + ND * UNITS // 4), k)
                    for j in ((0, 1), (2, 3), (4,), (5,))[k]:
                        gather(peer_u, i * TAIL_ROWS + (ND * UNITS + j), j % 2, 0)
            pool.sem_inc(vl_done, 2 * GRP)

            def split_v(n, b, k):
                wait_for(pool, vh_done, n + 1)
                g.tensor_tensor(vbf[:, b, 1, k], vf[:, b, k], vbf[:, b, 0, k], ALU.subtract).then_inc(vl_done, 1)

            for k in range(2):
                gather(peer_v, NSLOT + k, k, NSLOT)
            for k in range(GRP):
                split_v(k, 0, k)
            with pool.Fori(0, NGRP // 2 - 1) as i:
                for n in range(2 * GRP):
                    split_v(i * (2 * GRP) + (n + GRP), (n // GRP + 1) % 2, n % GRP)
                    gather(peer_v, i * (2 * GRP) + (n + NSLOT + 2), n % 2, NSLOT)
            for k in range(GRP):
                split_v(NK - GRP + k, 1, k)
            for n in range(NK - 2 * GRP + 2, NK):
                gather(peer_v, NSLOT + n, n % 2, NSLOT)

        @block.tensor
        def _(pe):
            def norm_transposes(k):
                for t in range(NT):
                    pe.wait_ge(N[k]["hn"], t + 1)
                    for half in range(2):
                        n = 2 * t + half
                        if n >= 2:
                            pe.wait_ge(N[k]["hT"], n - 1)
                        src = (hn if k == "mix" else hn2)[:, t % 2]
                        for c in range(4):
                            mm = nc.tensor.transpose(ps[:, half, c * P:(c + 1) * P],
                                                     src[:, (4 * half + c) * P:(4 * half + c + 1) * P], ident[:])
                        mm.then_inc(N[k]["trans"], 1)

            def contract(out, lhs, rhs, n=DC):
                for c in range(n):
                    mm = nc.tensor.matmul(out, lhs(c), rhs(c), start=(c == 0), stop=(c == n - 1))
                return mm

            pe.wait_ge(made, 1)
            norm_transposes("mix")
            pe.wait_ge(N["mix"]["hT"], 2 * NT)

            pe.wait_ge(consts_ready, 16 * 6)
            for kind in range(2):
                contract(ps[0:36, 2 + kind, :], lambda c: gw[:, c, kind, :], lambda c: hT[:, c, 0:512])
                contract(ps[0:36, 4 + kind, 0:256], lambda c: gw[:, c, kind, :],
                         lambda c: hT[:, c, 512:TOK]).then_inc(gates_done, 1)

            grp = 0
            units = 0

            def bank_free(g):
                if g < 4:
                    pe.wait_ge(gates_copied, 4)
                else:
                    pe.wait_ge(proj_copied, g - 3)

            def qk_transposes(u):
                pe.wait_ge(rope_done, u + 1)
                if u >= 2:
                    pe.wait_ge(qk_copied, u - 1)
                for c in range(4):
                    mm = nc.tensor.transpose(ps[:, 6 + u % 2, c * P:(c + 1) * P], stg[:, u % 2, c * P:(c + 1) * P], ident[:])
                mm.then_inc(qk_trans, 1)

            for n, (name, _) in enumerate(BLOCKS):
                pe.wait_ge(w_ready[n % 2], 16 * (n // 2 + 1))
                Wn = W[:, n % 2]
                if name in ("mq", "mk"):
                    for f in range(4):
                        for t0, nt in SEQS:
                            bank_free(grp)
                            mm = contract(ps[:, 2 + grp % 4, 0:nt * P], lambda c: Wn[:, c, f * P:(f + 1) * P],
                                          lambda c: hT[:, c, t0 * P:(t0 + nt) * P])
                            mm.then_inc(proj_done, 1)
                            grp += 1
                else:
                    for t in range(NT):
                        bank_free(grp)
                        mm = contract(ps[:, 2 + grp % 4, :], lambda c: hT[:, c, t * P:(t + 1) * P], lambda c: Wn[:, c, :])
                        mm.then_inc(proj_done, 1)
                        grp += 1
                        if name in ("aq", "ak"):
                            if units >= 1:
                                qk_transposes(units - 1)
                            units += 1
                        elif name == "av" and t == 0:
                            qk_transposes(units - 1)
                assert grp == PROJ_ENDS[n]

            pe.wait_ge(rows_done, 1)
            pe.wait_ge(qk_copied, 12)
            for t in range(NT):
                nc.tensor.transpose(ps[:, 6, t * 36:(t + 1) * 36], gates["i"][:, t * P:(t + 1) * P], ident[0:36, 0:36])
                mm = nc.tensor.transpose(ps[:, 7, t * 36:(t + 1) * 36], gates["f"][:, t * P:(t + 1) * P], ident[0:36, 0:36])
            mm.then_inc(cols_trans, 1)
            pe.wait_ge(cols_done, 2)
            pe.wait_ge(proj_copied, grp)
            pe.wait_ge(made, 1 + 2 * H + 5)
            for h in range(H):
                if h >= 1:
                    pe.wait_ge(w_exp, 2 * NT * h)
                for d in range(2):
                    nc.tensor.matmul(ps[:, 2 * d, :], sel[:, d * H + h], gates["M"][:, 0:512], start=True, stop=True)
                    mm = nc.tensor.matmul(ps[:, 1, 256 * d:256 * d + 256], sel[:, d * H + h], gates["M"][:, 512:TOK],
                                          start=True, stop=True)
                mm.then_inc(bc_done, 1)
                if h == 0:
                    pe.wait_ge(silu_done, 2 * H)
                for j in range(NT):
                    n = NT * h + j
                    t0, nt = seq_of(j)
                    if n >= 2:
                        pe.wait_ge(ws_ready, n - 1)
                    nc.tensor.matmul(ps[:, 3 + n % 2, 0:nt * P], mT[:, H + h, j * P:(j + 1) * P],
                                     mT[:, h, t0 * P:(t0 + nt) * P], start=True, stop=True).then_inc(s_done, 1)
                for t in range(NT):
                    m = NT * h + t
                    t0, nt = seq_of(t)
                    pe.wait_ge(ws_ready, NT * h + t0 + nt)
                    if m >= 2:
                        pe.wait_ge(num_used, m - 1)
                    ws = wsA if nt == 4 else wsB
                    i = t - t0
                    for d in range(2):
                        js = range(0, i + 1) if d == 0 else range(i, nt)
                        for j in js:
                            mm = nc.tensor.matmul(ps[:, 5 + 2 * (m % 2), d * 129:(d + 1) * 129],
                                                  ws[:, d, j, i * P:(i + 1) * P], vm[:, t0 + j, h, :],
                                                  start=(j == js[0]), stop=(j == js[-1]))
                    mm.then_inc(num_done, 1)

            def scores_of(m):
                h, t = divmod(m, NT)
                t0, nt = seq_of(t)
                if m >= 2:
                    pe.wait_ge(prob_exp, 2 * (m - 1))
                for c in range(2):
                    mm = nc.tensor.matmul(ps[:, 2 * (m % 2) + c, 0:nt * P], aT[QK * c:QK * c + QK, h, t * P:(t + 1) * P],
                                          aT[QK * c:QK * c + QK, H + h, t0 * P:(t0 + nt) * P], start=True, stop=True)
                mm.then_inc(sc_done, 1)

            def turn(m):
                nt = seq_of(m % NT)[1]
                pe.wait_ge(comb_done, m + 1)
                if m >= 2:
                    pe.wait_ge(combT_done, m - 1)
                for c in range(nt):
                    mm = nc.tensor.transpose(ps[:, 4 + m % 2, c * P:(c + 1) * P], comb[:, m % 2, c * P:(c + 1) * P], ident[:])
                mm.then_inc(ctr_done, 1)

            def values(m):
                h, t = divmod(m, NT)
                t0, nt = seq_of(t)
                pe.wait_ge(combT_done, m + 1)
                if m >= 2:
                    pe.wait_ge(att_done, m - 1)
                contract(ps[:, 6 + m % 2, 0:P], lambda c: combT[:, m % 2, c * P:(c + 1) * P],
                         lambda c: av[:, t0 + c, h * P:(h + 1) * P], nt).then_inc(att_mm, 1)

            pe.wait_ge(num_used, NT * H)
            pe.wait_ge(ws_ready, NT * H)
            MU = NT * H
            for m in range(MU + 2):
                if m < MU:
                    scores_of(m)
                if 1 <= m <= MU:
                    turn(m - 1)
                if m >= 2:
                    values(m - 2)

            for t in range(NT):
                pe.wait_ge(cnorm, 2 * (t + 1))
                if t >= 1:
                    pe.wait_ge(cat_done, 2 * t)
                for k, src in enumerate((att, mo)):
                    for h in range(H):
                        mm = nc.tensor.transpose(ps[:, k, h * P:(h + 1) * P], src[:, t, h * P:(h + 1) * P], ident[:])
                    mm.then_inc(ctrans, 1)
            pe.wait_ge(cat_done, 2 * NT)
            pe.wait_ge(att_done, NT * H)
            for i in range(2):
                n = NIN + i
                pe.wait_ge(w_ready[n % 2], 16 * (n // 2 + 1))
                for t in range(NT):
                    g = NT * i + t
                    if g >= 4:
                        pe.wait_ge(out_added, g - 3)
                    mm = contract(ps[:, 2 + g % 4, :], lambda c: catT[:, c, t * P:(t + 1) * P], lambda c: W[:, n % 2, c, :])
                    mm.then_inc(out_done, 1)

            norm_transposes("ffn")
            pe.wait_ge(N["ffn"]["hT"], 2 * NT)
            pe.wait_ge(subk_ready, 16)
            for q in range(2 * PH):
                n = PQ0 + q // 4
                if q % 4 == 0:
                    pe.wait_ge(w_ready[n % 2], 16 * (n // 2 + 1))
                if q >= 2:
                    pe.wait_ge(pq_copied, q - 1)
                for t0, nt in SEQS:
                    b = 2 + 2 * (q % 2) + (t0 > 0)
                    mm = contract(ps[:, b, 0:nt * P], lambda c: W[:, n % 2, c, (q % 4) * P:(q % 4 + 1) * P],
                                  lambda c: hT[:, c, t0 * P:(t0 + nt) * P])
                mm.then_inc(pq_done, 1)

                def score(q):
                    pe.wait_ge(pq_copied, q + 1)
                    if q >= 1:
                        pe.wait_ge(ps_copied, q)
                    for t in range(NT):
                        mm = nc.tensor.matmul(ps[:, 6 + t // 4, (t % 4) * P:(t % 4 + 1) * P], qT[:, q % 2, t * P:(t + 1) * P],
                                              subk[:, q, :], start=True, stop=True)
                    mm.then_inc(ps_done, 1)
                if q >= 1:
                    score(q - 1)
            score(2 * PH - 1)

            pe.sem_inc(up_done, 2)
            pe.sem_inc(g_mm, 2)

            def up(n, k):
                pe.wait_ge(u_split, n + 5)
                pe.wait_ge(gelu_done, n + 1)
                for c in range(DC):
                    for w, x in ((uh, xh), (uh, xl), (ul, xh)):
                        for b in range(2):
                            mm = nc.tensor.matmul(ps[:, 2 * (k % 2) + b, 0:HALF_T], w[k % 2][:, c, :],
                                                  x[:, c, b * HALF_T:(b + 1) * HALF_T],
                                                  start=(c == 0 and w is uh and x is xh),
                                                  stop=(c == DC - 1 and w is ul))
                mm.then_inc(up_done, 1)

            def gate_matrices(n, k):
                pe.wait_ge(oh_ready, n + 1)
                pe.wait_ge(g_evac, n + 1)
                for i in range(TU):
                    s = TU * (k % 2) + i
                    mm = nc.tensor.matmul(ps[:, 4 + 2 * (k % 2) + i // 4, (i % 4) * P:(i % 4 + 1) * P],
                                          oh[:, s, 0], oh[:, s, 1], start=True, stop=True)
                mm.then_inc(g_mm, 1)

            def turn_tables(t):
                pe.wait_ge(gate_ready, t + 2)
                for i, e in enumerate((e1, e2, gate)):
                    mm = nc.tensor.transpose(ps[:, 4, i * P:(i + 1) * P], e, ident[:])
                mm.then_inc(tab_trans, 1)

            pe.wait_ge(x_split, 2)
            with pe.Fori(0, U_FIRST) as i:
                for k in range(4):
                    up(i * 4 + k, k)
            with pe.Fori(0, ND) as t:
                pe.wait_ge(g_evac, t * 16 + 2)
                turn_tables(t)
                with pe.Fori(0, UNITS // 4) as i:
                    for k in range(4):
                        up(t * 16 + i * 4 + (k + 4 * U_FIRST), k)
                        gate_matrices(t * 16 + i * 4 + k, k)
            with pe.Fori(U_FIRST + 4 * ND, NK // 4) as i:
                for k in range(4):
                    up(i * 4 + k, k)

            pe.wait_ge(gelu_done, NK + 2)
            pe.wait_ge(g_evac, ND * UNITS + 2)
            pe.sem_inc(dn_done, 4 * ND)
            with pe.Fori(0, NGRP // 2) as i:
                for b in range(2):
                    pe.wait_ge(vl_done, i * (2 * GRP) + (b * GRP + 3 * GRP))
                    pe.wait_ge(act_done, i * (2 * GRP) + (b * GRP + 3 * GRP))
                    for o in range(2 * ND):
                        t, half = divmod(o, 2)
                        n = i * (4 * ND) + (b * 2 * ND + o)
                        pe.wait_ge(add_done, n + (2 * ND - NBANK + 1))
                        for k in range(GRP):
                            for pa, pv in ((0, 0), (0, 1), (1, 0)):
                                mm = nc.tensor.matmul(ps[:, o % NBANK, :], abf[:, b, pa, k, t * P:(t + 1) * P],
                                                      vbf[:, b, pv, k, half * 512:half * 512 + 512],
                                                      start=(k == 0 and pa + pv == 0), stop=(k == GRP - 1 and pa == 1))
                        mm.then_inc(dn_done, 1)

            pe.wait_ge(x_done, 1)
            norm_transposes("ple")
            pe.wait_ge(N["ple"]["hT"], 2 * NT)
            pe.wait_ge(ple_ready, 48)
            for i in range(2):
                n = PG0 + i
                pe.wait_ge(w_ready[n % 2], 16 * (n // 2 + 1))
                for t in range(NT):
                    g = NT * i + t
                    if g >= 2:
                        pe.wait_ge(pp_used, g - 1)
                    contract(ps[:, 2 + 2 * (g % 2), :], lambda c: hT[:, c, t * P:(t + 1) * P], lambda c: W[:, n % 2, c, :])
                    contract(ps[:, 3 + 2 * (g % 2), :], lambda c: pT[:, c, t * P:(t + 1) * P],
                             lambda c: wp[:, c, 512 * i:512 * i + 512], 2).then_inc(pg_done, 1)

        @block.scalar
        def _(act):
            a = nc.scalar

            def norm(k):
                for t in range(NT):
                    if k == "mix":
                        act.wait_ge(x_ready[t], 16)
                    j = junk if k == "mix" else junk2
                    if t >= 1:
                        act.wait_ge(N[k]["ssq"], t)
                    a.activation(j, X[:, t], ACT.Square, accum_out=ssq[:, t:t + 1]).then_inc(N[k]["ssq"], 1)
                act.wait_ge(N[k]["var"], 1)
                a.activation(rstd, var, ACT.Sqrt).then_inc(N[k]["rstd"], 1)

            def norm_copies(k):
                for n in range(2 * NT):
                    t, half = divmod(n, 2)
                    act.wait_ge(N[k]["trans"], n + 1)
                    a.activation(hT[:, 4 * half:4 * half + 4, t * P:(t + 1) * P],
                                 ps[:, half, :].rearrange("p (c n) -> p c n", c=4), ACT.Copy).then_inc(N[k]["hT"], 1)

            norm("mix")
            norm_copies("mix")

            def qk_copy(u):
                act.wait_ge(qk_trans, u + 1)
                t, part = u % NT, u // NT
                a.activation(aT[:, H * part:H * part + H, t * P:(t + 1) * P],
                             ps[:, 6 + u % 2, :].rearrange("p (c n) -> p c n", c=4), ACT.Copy).then_inc(qk_copied, 1)

            grp = 0
            units = 0
            for name, _ in BLOCKS:
                if name in ("mq", "mk"):
                    for f in range(4):
                        for (t0, nt), dst in zip(SEQS, (preA, preB)):
                            act.wait_ge(proj_done, grp + 1)
                            c = f + (4 if name == "mk" else 0)
                            a.activation(dst[:, c, 2:2 + nt * P], ps[:, 2 + grp % 4, 0:nt * P], ACT.Copy).then_inc(proj_copied, 1)
                            grp += 1
                    if name == "mq":
                        act.wait_ge(gate_abs, 1)
                        a.activation(gates["e"], gates["e"], ACT.Exp, scale=-1.0).then_inc(gate_exp, 1)
                        act.wait_ge(gate_exp, 1)
                        a.activation(gates["e"], gates["e"], ACT.Ln, bias=1.0).then_inc(gate_ln, 1)
                        act.wait_ge(lam_sum, 2)
                        a.activation(lexp, lsum, ACT.Exp).then_inc(lam_exp, 1)
                    continue
                for t in range(NT):
                    act.wait_ge(proj_done, grp + 1)
                    src = ps[:, 2 + grp % 4, :]
                    if name == "mv":
                        a.activation(vm[:, t, :, 0:P], src.rearrange("p (h e) -> p h e", h=H), ACT.Copy).then_inc(proj_copied, 1)
                    elif name == "mo":
                        a.activation(mo[:, t], src, ACT.Sigmoid).then_inc(proj_copied, 1)
                    elif name == "av":
                        a.activation(av[:, t], src, ACT.Copy).then_inc(proj_copied, 1)
                    else:
                        if units >= 2:
                            act.wait_ge(qk_trans, units - 1)
                        a.activation(stg[:, units % 2], src, ACT.Copy).then_inc(proj_copied, 1)
                        if units == 0:
                            for c in range(2 * H):
                                act.wait_ge(conv_done, c + 1)
                                a.activation(mT[:, c, :], mT[:, c, :], ACT.Silu).then_inc(silu_done, 1)
                        if units >= 1:
                            qk_copy(units - 1)
                        units += 1
                    grp += 1
                    if name == "av" and t == 0:
                        qk_copy(units - 1)
            act.wait_ge(cols_trans, 1)
            a.activation(acol.rearrange("p t n -> p (t n)"), ps[:, 6, 0:NT * 36], ACT.Copy).then_inc(cols_done, 1)
            a.activation(floor.rearrange("p t n -> p (t n)"), ps[:, 7, 0:NT * 36], ACT.Exp, scale=-1.0).then_inc(cols_done, 1)
            act.wait_ge(cols_done, 2)
            for h in range(H):
                act.wait_ge(bc_done, h + 1)
                if h >= 1:
                    act.wait_ge(num_done, NT * h)
                for j in range(NT):
                    t0, nt = seq_of(j)
                    i = j - t0
                    for d in range(2):
                        lo, hi = (i * P, nt * P) if d == 0 else (0, (i + 1) * P)
                        if nt == 4:
                            src, dst = ps[:, 2 * d, lo:hi], wsA[:, d, i, lo:hi]
                        else:
                            src, dst = ps[:, 1, 256 * d + lo:256 * d + hi], wsB[:, d, i, lo:hi]
                        r = 32 * d + h
                        a.activation(dst, src, ACT.Exp, bias=acol[:, j, r:r + 1]).then_inc(w_exp, 1)
            MU = NT * H

            def exps(m):
                nt = seq_of(m % NT)[1]
                act.wait_ge(nm_done, m + 1)
                if m >= 2:
                    act.wait_ge(comb_done, m - 1)
                else:
                    act.wait_ge(num_done, MU)
                for c in range(2):
                    a.activation(prob[:, m % 2, c, 0:nt * P], ps[:, 2 * (m % 2) + c, 0:nt * P], ACT.Exp,
                                 bias=nmax[:, m % 2, c:c + 1], scale=QK ** -0.5,
                                 accum_out=z[:, m % 2, c:c + 1]).then_inc(prob_exp, 1)

            def copy_turned(m):
                nt = seq_of(m % NT)[1]
                act.wait_ge(ctr_done, m + 1)
                if m >= 2:
                    act.wait_ge(att_mm, m - 1)
                a.activation(combT[:, m % 2, 0:nt * P], ps[:, 4 + m % 2, 0:nt * P], ACT.Copy).then_inc(combT_done, 1)

            def take_att(m):
                h, t = divmod(m, NT)
                act.wait_ge(att_mm, m + 1)
                a.activation(att[:, t, h * P:(h + 1) * P], ps[:, 6 + m % 2, 0:P], ACT.Copy)
                if m >= 1:
                    act.wait_ge(att_done, m)
                a.activation(junk_sq, ps[:, 6 + m % 2, 0:P], ACT.Square,
                             accum_out=ass_[:, t * H + h:t * H + h + 1]).then_inc(att_done, 1)

            for m in range(MU + 2):
                if m < MU:
                    exps(m)
                if 1 <= m <= MU:
                    copy_turned(m - 1)
                if m >= 2:
                    take_att(m - 2)
            act.wait_ge(cvar, 2)
            a.activation(ars, ars, ACT.Sqrt).then_inc(crstd, 1)
            a.activation(mrs, mrs, ACT.Sqrt).then_inc(crstd, 1)
            for t in range(NT):
                act.wait_ge(ctrans, 2 * t + 1)
                a.activation(catT[:, 0:H, t * P:(t + 1) * P], ps[:, 0, :].rearrange("p (c n) -> p c n", c=4), ACT.Copy,
                             scale=again08).then_inc(cat_done, 1)
                act.wait_ge(ctrans, 2 * t + 2)
                for h in range(H):
                    ins = a.activation(catT[:, H + h, t * P:(t + 1) * P], ps[:, 1, h * P:(h + 1) * P], ACT.Copy,
                                       scale=mgain[:, h:h + 1])
                ins.then_inc(cat_done, 1)

            act.wait_ge(out_added, 2 * NT)
            norm("ffn")
            norm_copies("ffn")
            for q in range(2 * PH):
                act.wait_ge(pq_done, q + 1)
                if q >= 2:
                    act.wait_ge(ps_done, q - 1)
                a.activation(qT[:, q % 2, 0:512], ps[:, 2 + 2 * (q % 2), :], ACT.Copy)
                a.activation(qT[:, q % 2, 512:TOK], ps[:, 3 + 2 * (q % 2), 0:256], ACT.Copy).then_inc(pq_copied, 1)
            act.sem_inc(gelu_done, 2)
            for b in range(2):
                act.sem_inc(ga_out[b], 16)
            act.sem_inc(g_out, 16)
            act.sem_inc(g_evac, 2)

            def evacuate(n, k, i):
                wait_for(act, g_mm, n + 3)
                for b in range(2):
                    ins = a.activation(gst[:, :, bass.ds(i * (4 * TU) + (TU * k + 4 * b), 4)].rearrange("p k t -> p t k"),
                                       ps[:, 4 + 2 * (k % 2) + b, :].rearrange("p (t k) -> p t k", t=4), ACT.Copy)
                ins.then_inc(g_evac, 1)

            def gelu(n, k, pairs):
                wait_for(act, ga_out[k % 2], pairs * 16 + 16)
                wait_for(act, up_done, n + 3)
                a.activation(gst_a[:, k % 2].rearrange("p (b n) -> p b n", b=2),
                             ps[:, 2 * (k % 2):2 * (k % 2) + 2, 0:HALF_T], ACT.Gelu).then_inc(gelu_done, 1)
                wait_for(act, gelu_done, n + 3)
                act.dma_start(scr_a[bass.ds(n, 1)].rearrange("o p n -> (o p) n"), gst_a[:, k % 2]).then_inc(ga_out[k % 2], 16)

            def gate_exps(t):
                wait_for(act, best_ready, t + 1)
                a.activation(gate, bestv.rearrange("p a b -> p (a b)"), ACT.Exp).then_inc(gate_e, 1)

            def load_scores(t):
                wait_for(act, chosen, t)
                act.dma_start(now, scr_s[bass.ds(t, 1)].rearrange("o p q n -> (o p) (q n)")).then_inc(now_ready, 16)

            for q in range(2):
                act.wait_ge(score_out[q], 16 * PH)
            act.wait_ge(x_split, 2)
            act.dma_start(now, scr_s[0].rearrange("p q n -> p (q n)")).then_inc(now_ready, 16)
            for part in range(2):
                with act.Fori(part * U_FIRST // 2, (part + 1) * U_FIRST // 2) as i:
                    for k in range(4):
                        gelu(i * 4 + k, k, i * 2 + k // 2)
                gate_exps(part)
                if part == 0:
                    load_scores(1)
            QT = UNITS // 4

            def tile_gelus(t, more):
                if more:
                    load_scores(t + 2)
                wait_for(act, g_out, t * 16 + 16)
                for lo, hi in ((0, QT - 1), (QT - 1, QT)):
                    with act.Fori(lo, hi) as i:
                        for k in range(4):
                            gelu(t * 16 + i * 4 + (k + 4 * U_FIRST), k, t * 8 + i * 2 + (k // 2 + 2 * U_FIRST))
                            evacuate(t * 16 + i * 4 + k, k, i)
                    if more and lo == 0:
                        gate_exps(t + 2)
                wait_for(act, g_evac, t * 16 + 18)
                act.dma_start(scr_g[:, :, bass.ds(t * P, P)].rearrange("k p n -> p k n"), gst).then_inc(g_out, 16)

            with act.Fori(0, ND - 1) as t:
                tile_gelus(t, True)
            tile_gelus(ND - 1, False)

            def first_part_of_v(i, b):
                wait_for(act, v_ready[b], i * 16 + 16)
                for k in range(GRP):
                    a.activation(vbf[:, b, 0, k], vf[:, b, k], ACT.Copy).then_inc(vh_done, 1)

            with act.Fori(U_FIRST + 4 * ND, NK // 4 - 1) as i:
                for k in range(4):
                    gelu(i * 4 + k, k, i * 2 + k // 2)
            first_part_of_v(0, 0)
            for k in range(4):
                gelu(NK - 4 + k, k, NK // 2 - 2 + k // 2)
            act.wait_ge(dots_done, 1)
            a.activation(coef, dots, ACT.Gelu).then_inc(coef_gelu, 1)
            first_part_of_v(0, 1)
            with act.Fori(1, NGRP // 2) as i:
                for b in range(2):
                    wait_for(act, dn_done, i * (4 * ND) + (b + 1) * 2 * ND)
                    first_part_of_v(i, b)
            act.wait_ge(x_done, 1)
            norm("ple")
            norm_copies("ple")
            for g in range(2 * NT):
                act.wait_ge(pg_done, g + 1)
                if g >= 2:
                    act.wait_ge(pp_used, g - 1)
                a.activation(sig[:, g % 2], ps[:, 2 + 2 * (g % 2), :], ACT.Sigmoid).then_inc(pg_sig, 1)
            act.wait_ge(pp_used, 2 * NT)
            norm("fin")

        @block.vector
        def _(dve):
            v = nc.vector
            steps = [0]

            def link(ins):
                steps[0] += 1
                ins.then_inc(dve_step, 1)
                dve.wait_ge(dve_step, steps[0])

            def norm(k, gain, loads):
                dve.wait_ge(N[k]["ssq"], NT)
                link(v.tensor_scalar(var, ssq, 1.0 / D, EPS, ALU.mult, ALU.add))
                v.reciprocal(var, var).then_inc(N[k]["var"], 1)
                dve.wait_ge(N[k]["rstd"], 1)
                dve.wait_ge(wbc_ready, 16 * loads)
                for t in range(NT):
                    if k == "fin":
                        if t >= 2:
                            dve.wait_ge(y_out[t % 2], 16 * (t // 2))
                    elif t >= 2:
                        dve.wait_ge(N[k]["trans"], 2 * (t - 1))
                    v.scalar_tensor_tensor((hn if k == "mix" else hn2)[:, t % 2], X[:, t], rstd[:, t:t + 1], gain,
                                           ALU.mult, ALU.mult).then_inc(y_ready if k == "fin" else N[k]["hn"], 1)

            norm("mix", wbc, 1)

            dve.wait_ge(consts_ready, 16 * 6)
            for kind, name in enumerate(("i", "f")):
                dve.wait_ge(gates_done, kind + 1)
                v.tensor_scalar(gates[name][:, 0:512], ps[0:36, 2 + kind, :], gb[0:36, kind:kind + 1], None,
                                ALU.add).then_inc(gates_copied, 1)
                v.tensor_scalar(gates[name][:, 512:TOK], ps[0:36, 4 + kind, 0:256], gb[0:36, kind:kind + 1], None,
                                ALU.add).then_inc(gates_copied, 1)
            dve.wait_ge(gates_copied, 4)
            v.scalar_tensor_tensor(gates["e"], gates["f"], -1.0, gates["f"], ALU.mult, ALU.max).then_inc(gate_abs, 1)
            dve.wait_ge(lam_ready, 16)
            for i in range(2):
                if i:
                    dve.wait_ge(lam_sum, 1)
                v.tensor_tensor_reduce(junk_sq[:, 0:QK], lq[:, 2 * i], lq[:, 2 * i + 1], 1.0, 0.0, ALU.mult, ALU.add,
                                       lsum[:, i:i + 1]).then_inc(lam_sum, 1)
            v.tensor_scalar(again08, again, 1.0 - LAM_INIT, None, ALU.mult).then_inc(lam_done, 1)

            def convolve(c):
                dve.wait_ge(proj_copied, 2 * (c + 1))
                for k in range(5):
                    for src, dst, n in ((preA, mT[:, c, 0:512], 512), (preB, mT[:, c, 512:TOK], 256)):
                        w = convw[:, c, k:k + 1]
                        if k == 0:
                            ins = v.tensor_scalar(dst, src[:, c, 0:n], w, None, ALU.mult)
                        else:
                            ins = v.scalar_tensor_tensor(dst, src[:, c, k:k + n], w, dst, ALU.mult, ALU.add)
                    if k < 4:
                        link(ins)
                ins.then_inc(conv_done, 1)

            dve.wait_ge(made, 6)
            for c in range(H):
                convolve(c)
            dve.wait_ge(gate_ln, 1)
            link(v.scalar_tensor_tensor(gates["f"], gates["f"], 0.0, gates["e"], ALU.min, ALU.subtract))

            def scan(dst, src, op):
                for t0, nt in SEQS:
                    cols = slice(t0 * P, (t0 + nt) * P)
                    v.tensor_tensor_scan(dst[0:32, cols], src[0:32, cols], src[0:32, cols], 0.0, op, ALU.bypass)
                    ins = v.tensor_tensor_scan(dst[32:36, cols][:, ::-1], src[32:36, cols][:, ::-1],
                                               src[32:36, cols][:, ::-1], 0.0, op, ALU.bypass)
                link(ins)
            scan(gates["B"], gates["f"], ALU.add)
            link(v.tensor_tensor(gates["i"], gates["i"], gates["B"], ALU.subtract))
            scan(gates["M"], gates["i"], ALU.max)
            v.tensor_tensor(gates["f"], gates["B"], gates["M"], ALU.add).then_inc(rows_done, 1)
            dve.wait_ge(lam_exp, 1)
            v.tensor_scalar(nlam, lexp[:, 1:2], lexp[:, 0:1], LAM_INIT, ALU.subtract, ALU.subtract).then_inc(lam_done, 1)
            for c in range(H, 2 * H):
                convolve(c)

            for u in range(2 * NT):
                t = u % NT
                i = t - seq_of(t)[0]
                dve.wait_ge(proj_copied, PROJ_ENDS[3] + u + 1)
                x = stg[:, u % 2].rearrange("p (g n) -> p g n", g=8)
                x1, x2 = x[:, :, 0:HALF], x[:, :, HALF:2 * HALF]
                cos, sin = (ropet[:, i, j:j + 1, :].to_broadcast([P, 8, HALF]) for j in range(2))
                if u:
                    dve.wait_ge(rope_done, u)
                v.tensor_tensor(rot[:, 0], x1, cos, ALU.mult)
                v.tensor_tensor(rot[:, 1], x2, sin, ALU.mult)
                v.tensor_tensor(rot[:, 2], x2, cos, ALU.mult)
                link(v.tensor_tensor(rot[:, 3], x1, sin, ALU.mult))
                v.tensor_tensor(x1, rot[:, 0], rot[:, 1], ALU.subtract)
                v.tensor_tensor(x2, rot[:, 2], rot[:, 3], ALU.add).then_inc(rope_done, 1)

            KSCALE = float(P) ** -0.5
            dve.wait_ge(cols_done, 2)
            for h in range(H):
                for j in range(NT):
                    n = NT * h + j
                    t0, nt = seq_of(j)
                    i = j - t0
                    dve.wait_ge(s_done, n + 1)
                    dve.wait_ge(w_mask, 2 * n + 2)
                    for d in range(2):
                        lo, hi = (i * P, nt * P) if d == 0 else (0, (i + 1) * P)
                        w = (wsA if nt == 4 else wsB)[:, d, i, lo:hi]
                        ins = v.scalar_tensor_tensor(w, ps[:, 3 + n % 2, lo:hi], KSCALE, w, ALU.mult, ALU.mult)
                    ins.then_inc(ws_ready, 1)
                for t in range(NT):
                    m = NT * h + t
                    dve.wait_ge(num_done, m + 1)
                    num = ps[:, 5 + 2 * (m % 2), 0:2 * (P + 1)].rearrange("p (d n) -> p d n", d=2)
                    link(v.tensor_tensor(den, num[:, :, P], floor[:, t, h:h + 33:32], ALU.max))
                    link(v.scalar_tensor_tensor(den, num[:, :, P], -1.0, den, ALU.mult, ALU.max))
                    link(v.reciprocal(rden, den))
                    hs = hsum[:, m % 2]
                    if m >= 2:
                        dve.wait_ge(mem_squared, m - 1)
                    link(v.tensor_scalar(hs, num[:, 0, 0:P], rden[:, 0:1], None, ALU.mult))
                    ins = v.scalar_tensor_tensor(hs, num[:, 1, 0:P], rden[:, 1:2], hs, ALU.mult, ALU.add)
                    ins.then_inc(num_used, 1)
                    dve.wait_ge(num_used, m + 1)
                    o = mo[:, t, h * P:(h + 1) * P]
                    link(v.tensor_tensor(o, o, hs, ALU.mult))
                    v.tensor_tensor_reduce(hs, o, o, 1.0, 0.0, ALU.mult, ALU.add, mss[:, t * H + h:t * H + h + 1]).then_inc(mem_squared, 1)

            MU = NT * H

            def maxima(m):
                nt = seq_of(m % NT)[1]
                dve.wait_ge(sc_done, m + 1)
                b = 2 * (m % 2)
                link(v.tensor_reduce(nmax[:, m % 2], ps[:, b:b + 2, 0:nt * P], AX.X, ALU.max, negate=True))
                v.tensor_scalar(nmax[:, m % 2], nmax[:, m % 2], QK ** -0.5, None, ALU.mult).then_inc(nm_done, 1)

            def combine(m):
                nt = seq_of(m % NT)[1]
                s = m % 2
                dve.wait_ge(prob_exp, 2 * (m + 1))
                if m:
                    dve.wait_ge(comb_done, m)
                link(v.reciprocal(rz, z[:, s]))
                p0, p1 = prob[:, s, 0, 0:nt * P], prob[:, s, 1, 0:nt * P]
                v.tensor_scalar(p0, p0, rz[:, 0:1], None, ALU.mult)
                link(v.tensor_scalar(nl, rz[:, 1:2], nlam, None, ALU.mult))
                if m >= 2:
                    dve.wait_ge(ctr_done, m - 1)
                v.scalar_tensor_tensor(comb[:, s, 0:nt * P], p1, nl, p0, ALU.mult, ALU.add).then_inc(comb_done, 1)

            dve.wait_ge(lam_done, 2)
            for m in range(MU + 1):
                if m < MU:
                    maxima(m)
                if m >= 1:
                    combine(m - 1)

            dve.wait_ge(mem_squared, MU)
            link(v.tensor_scalar(mrs, mss, 1.0 / P, EPS, ALU.mult, ALU.add))
            v.reciprocal(mrs, mrs).then_inc(cvar, 1)
            dve.wait_ge(att_done, MU)
            link(v.tensor_scalar(ars, ass_, 1.0 / P, EPS, ALU.mult, ALU.add))
            v.reciprocal(ars, ars).then_inc(cvar, 1)
            dve.wait_ge(crstd, 2)
            for t in range(NT):
                for arr, r in ((att, ars), (mo, mrs)):
                    x = arr[:, t].rearrange("p (h n) -> p h n", h=H)
                    v.tensor_tensor(x, x, r[:, t * H:(t + 1) * H].unsqueeze(2).to_broadcast([P, H, P]),
                                    ALU.mult).then_inc(cnorm, 1)

            for g in range(2 * NT):
                i, t = divmod(g, NT)
                dve.wait_ge(out_done, g + 1)
                dve.wait_ge(x_ready[t], 32)
                x = X[:, t, 512 * i:512 * i + 512]
                v.tensor_tensor(x, ps[:, 2 + g % 4, :], x, ALU.add).then_inc(out_added, 1)

            dve.wait_ge(out_added, 2 * NT)
            norm("ffn", wbc2, 2)
            for q in range(2 * PH):
                dve.wait_ge(ps_done, q + 1)
                if q >= 2:
                    dve.wait_ge(score_out[q % 2], 16 * (q // 2))
                v.tensor_copy(sst[:, q % 2, 0:4], ps[:, 6, :].rearrange("p (t n) -> p t n", t=4))
                v.tensor_copy(sst[:, q % 2, 4:6], ps[:, 7, 0:256].rearrange("p (t n) -> p t n", t=2)).then_inc(ps_copied, 1)
                if q == 1:
                    dve.wait_ge(N["ffn"]["hT"], 2 * NT)
                    v.tensor_copy(xh, hT[:, :, P:TOK]).then_inc(x_split, 1)
                    dve.wait_ge(x_split, 1)
                    v.tensor_tensor(xl, hT[:, :, P:TOK], xh, ALU.subtract).then_inc(x_split, 1)
                    v.scalar_tensor_tensor(xn, X[:, 0], rstd[:, 0:1], wbc2, ALU.mult, ALU.mult).then_inc(xn_done, 1)
            dve.wait_ge(mk, 3)

            def choose(t):
                k = [0]

                def tlink(ins):
                    k[0] += 1
                    ins.then_inc(topk_step, 1)
                    wait_for(dve, topk_step, t * TOPK_STEPS + k[0])

                def top16(vals, inds, src):
                    tlink(v.max(vals[:, 0:8], src))
                    v.max_index(inds[:, 0:8], vals[:, 0:8], src)
                    tlink(v.match_replace(src, vals[:, 0:8], src, NEG))
                    tlink(v.max(vals[:, 8:16], src))
                    return v.max_index(inds[:, 8:16], vals[:, 8:16], src)

                wait_for(dve, now_ready, t * 16 + 16)
                for h in range(PH):
                    for half in range(2):
                        last = top16(topv[:, h, half], topi[:, h, half], now[:, (2 * h + half) * P:(2 * h + half + 1) * P])
                        yield
                last.then_inc(chosen, 1)
                wait_for(dve, chosen, t + 1)
                tlink(v.tensor_copy(topf, topi))
                tlink(v.tensor_tensor(cand.rearrange("p h (i j) -> p h i j", i=K16),
                                      topv[:, :, 0].unsqueeze(3).to_broadcast([P, PH, K16, K16]),
                                      topv[:, :, 1].unsqueeze(2).to_broadcast([P, PH, K16, K16]), ALU.add))
                for h in range(PH):
                    last = top16(bestv[:, h], bestc[:, h], cand[:, h])
                    yield
                tlink(last)
                for shift, half, e in ((True, 0, e1), (False, 1, e2)):
                    c = bestc.rearrange("p a b -> p (a b)")
                    if shift:
                        tlink(v.tensor_scalar(rank_u, c, 4, None, ALU.logical_shift_right))
                    else:
                        tlink(v.tensor_scalar(rank_u, c, 15, None, ALU.bitwise_and))
                    tlink(v.tensor_copy(rank, rank_u))
                    yield
                    tlink(v.tensor_tensor(onehot, rank.unsqueeze(2).to_broadcast([P, NSLOT, K16]),
                                          iota16.unsqueeze(1).to_broadcast([P, NSLOT, K16]), ALU.is_equal))
                    yield
                    oh4 = onehot.rearrange("p (h j) r -> p h j r", h=PH)
                    tlink(v.tensor_tensor(oh4, oh4, topf[:, :, half].unsqueeze(2).to_broadcast([P, PH, K16, K16]), ALU.mult))
                    yield
                    tlink(v.tensor_reduce(e, onehot, AX.X, ALU.add))
                    yield
                if isinstance(t, int) and t == 0:
                    link(v.scalar_tensor_tensor(rank, e1, float(NK), e2, ALU.mult, ALU.add))
                    v.tensor_copy(idx, rank).then_inc(idx_ready, 1)
                tlink(v.tensor_copy(gsum, bestv[:, :, 0]))
                v.tensor_tensor(bestv, bestv, gsum.unsqueeze(2).to_broadcast([P, PH, K16]), ALU.subtract).then_inc(best_ready, 1)
                yield "exp"
                wait_for(dve, gate_e, t + 1)
                g3 = gate.rearrange("p (h n) -> p h n", h=PH)
                tlink(v.tensor_reduce(gsum, g3, AX.X, ALU.add))
                tlink(v.reciprocal(gsum, gsum))
                (v.tensor_tensor(g3, g3, gsum.unsqueeze(2).to_broadcast([P, PH, K16]), ALU.mult)).then_inc(gate_ready, 1)
                assert k[0] == TOPK_STEPS, k[0]

            def tables(t):
                wait_for(dve, tab_trans, t + 1)
                v.tensor_copy(eT.rearrange("p a n -> p (a n)"), ps[:, 4, 0:3 * P]).then_inc(tab_done, 1)
                wait_for(dve, tab_done, t + 1)

            def dot(pairs, r, col):
                wait_for(dve, row_ready[r % 2], pairs * 16 + 16)
                x = rows[r % 2]
                v.tensor_tensor_reduce(x, x, xn, 1.0, 0.0, ALU.mult, ALU.add, dots_now[:, col:col + 1]).then_inc(row_used, 1)

            def keep_dots(at, n, used, turn):
                wait_for(dve, row_used, used)
                v.tensor_copy(dots[:, bass.ds(at, n)], dots_now[:, 0:n]).then_inc(dots_copied, 1)
                wait_for(dve, dots_copied, turn + 1)

            def build(n, j):
                wait_for(dve, g_mm, n + 1)
                for i in range(TU):
                    col, s = TU * j + i, TU * (j % 2) + i
                    v.tensor_scalar(oh[:, s, 0], iota_f, eT[:, 0, col:col + 1], None, ALU.is_equal)
                    ins = v.tensor_scalar(oh[:, s, 1], iota_f, eT[:, 1, col:col + 1], eT[:, 2, col:col + 1],
                                          ALU.is_equal, ALU.mult)
                ins.then_inc(oh_ready, 1)

            def tile_gates(t, following):
                tables(t)
                steps = following
                at_exp, left = False, 4
                for j in range(P // TU):
                    build(t * 16 + j, j)
                    while steps is not None and j >= 1 and (at_exp is False or j == 13):
                        stop = next(steps, "end")
                        left -= 1
                        at_exp = at_exp or stop == "exp"
                        if stop == "end" or (j < 12 and left == 0) or (at_exp and j < 13):
                            break
                    left = 4
                    dot(t * 8 + j // 2, j, j)
                keep_dots(t * UNITS, UNITS, t * UNITS + (UNITS + 2), t)

            dve.wait_ge(xn_done, 1)
            for _ in choose(0):
                pass
            dve.wait_ge(gate_ready, 1)
            link(v.tensor_copy(gate0, gate))
            for _ in choose(1):
                pass
            with dve.Fori(0, ND - 1) as t:
                tile_gates(t, choose(t + 2))
            tile_gates(ND - 1, None)
            with dve.Fori(0, NK // 4 - U_FIRST - ND * UNITS // 4) as i:
                for j in range(TAIL_ROWS):
                    dot(i * (TAIL_ROWS // 2) + (ND * UNITS // 2 + j // 2), j, j)
                keep_dots(i * TAIL_ROWS + ND * UNITS, TAIL_ROWS, i * TAIL_ROWS + (ND * UNITS + TAIL_ROWS + 2), i + ND)
            v.memset(rz, 0.0).then_inc(dots_done, 1)

            v.sem_inc(act_done, 2 * GRP)
            v.sem_inc(add_done, 2 * ND)

            def weigh(n, b, k, i):
                if k == 0:
                    wait_for(dve, ga_ready[b], i * 32 + 32)
                x = af[b][:, k]
                v.tensor_tensor(x, x, gf[b][:, k], ALU.mult).then_inc(weighed, 1)
                dve.wait_ge(weighed, n * 2 + 1)
                v.tensor_copy(abf[:, b, 0, k], x).then_inc(weighed, 1)
                dve.wait_ge(weighed, n * 2 + 2)
                v.tensor_tensor(abf[:, b, 1, k], x, abf[:, b, 0, k], ALU.subtract).then_inc(act_done, 1)

            def add_banks(n0, outs):
                for o in outs:
                    t, half = divmod(o, 2)
                    dve.wait_ge(dn_done, n0 + (o + 1 + 4 * ND))
                    dve.wait_ge(add_done, n0 + (o + 1))
                    x = X[:, t + 1, half * 512:half * 512 + 512]
                    v.tensor_tensor(x, ps[:, o % NBANK, :], x, ALU.add).then_inc(add_done, 1)

            def add_row(pairs, n, k):
                wait_for(dve, row_ready[k % 2], pairs * 16 + 16)
                wait_for(dve, row_used, n + (NSLOT + 2))
                v.scalar_tensor_tensor(X[:, 0], rows[k % 2], coef[:, bass.ds(n, 1)], X[:, 0],
                                       ALU.mult, ALU.add).then_inc(row_used, 1)

            OUTS = ((0, 1, 2), (3, 4, 5), (6, 7), (8, 9))

            def group(i, b, more):
                for k in range(GRP):
                    if more:
                        if b == 0:
                            if k == 0:
                                wait_for(dve, dn_done, i * (4 * ND) + 4 * ND)
                            weigh(i * (2 * GRP) + (GRP + k), 1, k, i)
                        else:
                            if k == 0:
                                wait_for(dve, dn_done, i * (4 * ND) + 6 * ND)
                            weigh(i * (2 * GRP) + (2 * GRP + k), 0, k, i + 1)
                    add_row(i * GRP + (b * GRP // 2 + k // 2 + NSLOT // 2), i * (2 * GRP) + (b * GRP + k), k)
                    add_banks(i * (4 * ND) + b * 2 * ND, OUTS[k])

            for k in range(GRP):
                weigh(k, 0, k, 0)
            dve.wait_ge(coef_gelu, 1)
            v.tensor_tensor(coef, coef, gate0, ALU.mult).then_inc(coef_done, 1)
            dve.wait_ge(coef_done, 1)
            dve.wait_ge(gelu_done, NK + 2)
            for b in range(2):
                dve.wait_ge(ga_out[b], 16 * NK // 2 + 16)
            with dve.Fori(0, NGRP // 2 - 1) as i:
                group(i, 0, True)
                group(i, 1, True)
            group(NGRP // 2 - 1, 0, True)
            group(NGRP // 2 - 1, 1, False)
            dve.wait_ge(add_done, NGRP * 2 * ND + 2 * ND)
            dve.wait_ge(row_used, 2 * NSLOT + 2)
            v.memset(rz, 0.0).then_inc(x_done, 1)

            norm("ple", wbc2, 3)
            for g in range(2 * NT):
                i, t = divmod(g, NT)
                dve.wait_ge(pg_sig, g + 1)
                if g >= 2:
                    dve.wait_ge(pp_used, g - 1)
                link(v.tensor_tensor(plp[:, g % 2], ps[:, 3 + 2 * (g % 2), :], sig[:, g % 2], ALU.mult))
                x = X[:, t, 512 * i:512 * i + 512]
                v.tensor_tensor(x, x, plp[:, g % 2], ALU.add).then_inc(pp_used, 1)
            dve.wait_ge(pp_used, 2 * NT)
            norm("fin", wbc2, 4)


def kernel(**inputs):
    import numpy as np
    import concourse.bacc as bacc
    from concourse.bass_utils import run_bass_kernel_spmd

    def arr(name):
        return np.ascontiguousarray(inputs[name])

    w_in = arr("w_in")[0]
    gb = arr("gate_bias")[0]
    gate_w = np.zeros((D, 2, 36), w_in.dtype)
    gate_b = np.zeros((36, 2), gb.dtype)
    for d in range(2):
        for kind in range(2):
            c = 8 * d + 4 * kind
            gate_w[:, kind, 32 * d:32 * d + H] = w_in[:, GATE0 + c:GATE0 + c + H]
            gate_b[32 * d:32 * d + H, kind] = gb[c:c + H]
    half = np.arange(0, 2 * HALF, 2, dtype=np.float32) / np.float32(2 * HALF)
    inv = np.float32(500000.0) ** -half
    ang = np.arange(SEQS[0][1] * P, dtype=np.float32)[:, None] * inv[None, :]
    rope = np.stack([np.cos(ang), np.sin(ang)], axis=1).astype(np.float32)
    arrays = {
        "x_a": arr("x_prompt")[0], "x_b": arr("x_sample")[0],
        "pT_a": arr("p_prompt")[0, 0].T, "pT_b": arr("p_sample")[0, 0].T,
        "norm_mix": arr("norm_mix")[0], "w_in": w_in,
        "gate_w": gate_w, "gate_b": gate_b,
        "conv_w": arr("conv_qk")[0].T.reshape(2 * H, P, 5).transpose(1, 0, 2),
        "lambda_qk": arr("lambda_qk")[0], "attn_gain": arr("attn_gain")[0][:, None],
        "mlstm_gain": arr("mlstm_gain")[0].reshape(H, P).T,
        "w_out": arr("w_out")[0], "norm_ffn": arr("norm_ffn")[0], "peer_wq": arr("peer_wq")[0],
        "subkeysT": arr("peer_subkeys")[0].reshape(2 * PH, P, P).transpose(2, 0, 1),
        "uT": arr("peer_u")[0].reshape(NK, NK, DC, P).transpose(1, 3, 2, 0).reshape(NK, P, DC * NK),
        "peer_u": arr("peer_u")[0], "peer_v": arr("peer_v")[0], "norm_ple": arr("norm_ple")[0],
        "ple_w_gate": arr("ple_w_gate")[0], "ple_w_proj": arr("ple_w_proj")[0],
        "norm_final": arr("norm_final"), "rope": rope,
    }
    arrays = {k: np.ascontiguousarray(a) for k, a in arrays.items()}
    nc = bacc.Bacc("TRN2", target_bir_lowering=False, num_devices=1)
    args = [nc.dram_tensor(k, a.shape, mybir.dt.from_np(a.dtype), kind="ExternalInput").ap() for k, a in arrays.items()]
    args += [nc.dram_tensor(k, (n, D), F32, kind="ExternalOutput").ap() for k, n in (("y_a", 4 * P), ("y_b", 2 * P))]
    hymba_layer(nc, *args)
    got = run_bass_kernel_spmd(nc, [arrays], core_ids=[0]).results[0]
    return got["y_a"].reshape(1, 4 * P, D), got["y_b"].reshape(1, 2 * P, D)
```

```python
from contextlib import ExitStack

import concourse.bass as bass
from concourse import mybir

ALU = mybir.AluOpType
ACT = mybir.ActivationFunctionType
AX = mybir.AxisListType
F32 = mybir.dt.float32
U32 = mybir.dt.uint32
BF16 = mybir.dt.bfloat16

P = 128
D = 1024
DC = D // P
NT = 6
TOK = NT * P
SEQS = [(0, 4), (4, 2)]
H = 4
HALF = 8
QK = 64
NGATE = 16
PH = 8
K16 = 16
NSLOT = PH * K16
EPS = 1e-6
LAM_INIT = 0.2
NEG = -3.0e38
NK = 128
TU = 8
ND = NT - 1
DTOK = ND * P
HALF_T = DTOK // 2
UNITS = P // TU
RING = 4
PART = 4 * TU
NBANK = 5
GRP = 4
NGRP = NK // GRP
U_FIRST = 4
PARTS = P // PART
TILE_STEPS = PARTS + 1
GATED_ROWS, PLAIN_ROWS = 5, 4
TILE_ROWS = PARTS * GATED_ROWS + PLAIN_ROWS
LAST_STEPS = NK // 4 - U_FIRST - ND * TILE_STEPS - 1
assert ND * TILE_ROWS + LAST_STEPS * PLAIN_ROWS == NSLOT
KEY_STEPS = 3 * 2 * PH
TOPK_STEPS = KEY_STEPS + 2 + 25 + 10 + 1 + 2

BLOCKS = [("mq", 1536), ("mk", 2048), ("mv", 2560), ("mo", 3072), ("aq", 0), ("ak", 512), ("av", 1024)]
GATE0 = 3584
NIN = len(BLOCKS)


def hymba_layer(nc, x_a, x_b, pT_a, pT_b, norm_mix, w_in, gate_w, gate_b, conv_w, lambda_qk, attn_gain,
                mlstm_gain, w_out, norm_ffn, peer_wq, subkeysT, uT, peer_u, peer_v, norm_ple,
                ple_w_gate, ple_w_proj, norm_final, rope, y_a, y_b):
    ctx = ExitStack()
    with ctx:
        def sb(name, shape, dt=F32):
            return ctx.enter_context(nc.sbuf_tensor(name, shape, dt))

        def sem(name):
            return ctx.enter_context(nc.semaphore(name))


        WORDS = 48640
        arena = sb("arena", [P, WORDS])

        def view(at, *dims):
            n = 1
            for d in dims:
                n *= d
            assert at + n <= WORDS, (at, dims)
            v = arena[:, at:at + n]
            if len(dims) == 2:
                return v.rearrange("p (a b) -> p a b", a=dims[0])
            if len(dims) == 3:
                return v.rearrange("p (a b c) -> p a b c", a=dims[0], b=dims[1])
            return v

        X = view(0, NT, D)
        HT_AT = NT * D
        hT = view(HT_AT, DC, TOK)
        catT = hT
        W_AT = HT_AT + DC * TOK
        W = view(W_AT, 2, DC, 512)
        FREE = W_AT + 2 * DC * 512

        preA = view(FREE, 2 * H, 516)
        preB = view(FREE + 2 * H * 516, 2 * H, 260)
        aT = view(FREE, 2 * H, TOK)
        at = FREE + 2 * H * (516 + 260)
        mT = view(at, 2 * H, TOK)
        att = view(at, NT, H * P)
        at += 2 * H * TOK
        vm = view(at, NT, H, P + 1)
        at += NT * H * (P + 1)
        mo = view(at, NT, H * P)
        at += NT * H * P
        av = view(at, NT, H * P)
        at += NT * H * P
        wsA = view(at, 2, 4, 512)
        wsB = view(at + 4096, 2, 2, 256)
        hn = view(at, 2, D)
        junk = view(at + 2 * D, D)
        stg = view(5 * D, 2, 512)
        prob = view(at, 2, 2, 512)
        comb = view(at + 2048, 2, 512)
        combT = view(at + 3072, 2, 512)
        at += 2 * 4 * 512 + 2 * 2 * 256
        wbc = view(at, D)
        at += D
        junk_sq = wbc[:, 0:P]
        rot = wbc[:, P:P + 256].rearrange("p (a g n) -> p a g n", a=4, g=8)
        lq = wbc[:, 512:768].rearrange("p (a b) -> p a b", a=4)
        gates = {}
        for i, name in enumerate(("i", "f", "e", "B", "M")):
            gates[name] = arena[0:36, i * TOK:(i + 1) * TOK]
        sel = view(4 * D, 2 * H, P)[0:36]
        assert at <= WORDS, at

        R1 = HT_AT
        uf = view(R1, 4, DC * NK)
        ubf = arena[:, R1 + 4 * D:R1 + 6 * D].bitcast(BF16)
        uh = [ubf[:, (2 * i) * D:(2 * i + 1) * D].rearrange("p (c n) -> p c n", c=DC) for i in range(2)]
        ul = [ubf[:, (2 * i + 1) * D:(2 * i + 2) * D].rearrange("p (c n) -> p c n", c=DC) for i in range(2)]
        G_AT = R1 + 6 * D
        gst = [view(G_AT + (2 + i) * NK * PART, NK, PART) for i in range(2)]
        X_AT = G_AT + NK * P
        xbf = arena[:, X_AT:X_AT + DC * DTOK].bitcast(BF16)
        xh = xbf[:, 0:DC * DTOK].rearrange("p (c n) -> p c n", c=DC)
        xl = xbf[:, DC * DTOK:2 * DC * DTOK].rearrange("p (c n) -> p c n", c=DC)
        S_AT = X_AT + DC * TOK
        now = view(S_AT, 2 * PH * P)
        cand = view(S_AT + 2048, PH, K16 * K16)
        onehot = view(S_AT + 4096, NSLOT, K16)
        hn2 = view(S_AT, 2, D)
        junk2 = view(S_AT + 2 * D, D)
        wbc2 = view(S_AT + 3 * D, D)
        O_AT = S_AT + 6144
        oh = arena[:, O_AT:O_AT + 4 * TU * NK].bitcast(BF16).rearrange("p (s a t n) -> p s a t n", s=2, a=4, t=TU)
        gst_a = view(O_AT + 4096, 2, DTOK)
        E_AT = O_AT + 4096 + 2 * DTOK
        xn = view(E_AT, D)
        rows = [view(E_AT + D, D), view(X_AT + DC * DTOK, D)]
        u_rows = rows + [view(G_AT + (GRP + i) * D, D) for i in range(2)]
        v_rows_now = rows + [view(R1 + i * D, D) for i in range(2)]
        assert E_AT + 2 * D <= WORDS
        subk = view(O_AT, 2 * PH, P)
        qT = view(O_AT + 2048, 2, TOK)
        sst = view(O_AT + 3584, 2, NT, P)
        assert X_AT + DC * DTOK + D <= S_AT

        vf = view(G_AT, 2, GRP, D)
        vbf = arena[:, G_AT + 2 * GRP * D:G_AT + 4 * GRP * D].bitcast(BF16).rearrange(
            "p (s a k n) -> p s a k n", s=2, a=2, k=GRP)
        af = [view(at, GRP, DTOK) for at in (S_AT, X_AT)]
        gf = [view(at + GRP * DTOK, ND * PARTS, GRP * PART) for at in (S_AT, X_AT)]
        assert X_AT + 2 * GRP * DTOK <= X_AT + DC * DTOK
        abf = arena[:, O_AT:O_AT + 2 * GRP * DTOK].bitcast(BF16).rearrange(
            "p (s a k n) -> p s a k n", s=2, a=2, k=GRP)
        assert O_AT + 2 * GRP * DTOK <= E_AT

        pT = view(X_AT, 2, TOK)
        wp = view(X_AT + 2 * TOK, 2, D)
        sig = view(O_AT, 2, 512)
        plp = view(O_AT + 1024, 2, 512)

        small = sb("small", [P, 1024])
        spos = [0]

        def tiny(*dims, dt=F32):
            n = 1
            for d in dims:
                n *= d
            v = small[:, spos[0]:spos[0] + n]
            spos[0] += n
            assert spos[0] <= 1024
            if dt != F32:
                v = v.bitcast(dt)
            if len(dims) == 2:
                v = v.rearrange("p (a b) -> p a b", a=dims[0])
            elif len(dims) == 3:
                v = v.rearrange("p (a b c) -> p a b c", a=dims[0], b=dims[1])
            return v

        ident = sb("ident", [P, P])
        gw = sb("gw", [P, DC, 2, 36])
        gb = tiny(2)
        convw = tiny(2 * H, 5)
        again = tiny(1)
        again08 = tiny(1)
        mgain = tiny(H)
        ropet = tiny(4, 2, HALF)
        ssq = tiny(NT)
        var = tiny(NT)
        rstd = tiny(NT)
        lsum = tiny(2)
        lexp = tiny(2)
        nlam = tiny(1)
        acol = tiny(NT, 36)
        floor = tiny(NT, 36)
        den = tiny(2)
        rden = tiny(2)
        hsum = tiny(2, P)
        mss = tiny(NT * H)
        ass_ = tiny(NT * H)
        mrs = tiny(NT * H)
        ars = tiny(NT * H)
        nmax = tiny(2, 2)
        z = tiny(2, 2)
        rz = tiny(2)
        nl = tiny(1)
        pk = sb("pk", [P, 2740])
        kp = [0]

        def peer_tiny(*dims, dt=F32):
            n = 1
            for d in dims:
                n *= d
            v = pk[:, kp[0]:kp[0] + n]
            kp[0] += n
            assert kp[0] <= 2740
            if dt != F32:
                v = v.bitcast(dt)
            if len(dims) == 2:
                v = v.rearrange("p (a b) -> p a b", a=dims[0])
            elif len(dims) == 3:
                v = v.rearrange("p (a b c) -> p a b c", a=dims[0], b=dims[1])
            return v

        topv = peer_tiny(PH, 2, K16)
        topi = peer_tiny(PH, 2, K16, dt=U32)
        topf = peer_tiny(PH, 2, K16)
        bestv = peer_tiny(PH, K16)
        bestc = peer_tiny(PH, K16, dt=U32)
        rank_u = peer_tiny(NSLOT, dt=U32)
        rank = peer_tiny(NSLOT)
        e1 = peer_tiny(NSLOT)
        e2 = peer_tiny(NSLOT)
        gate = peer_tiny(NSLOT)
        eT = peer_tiny(P).bitcast(BF16).rearrange("p (a n) -> p a n", a=2)
        iota_keys = peer_tiny(NK // 2).bitcast(BF16)
        gT = peer_tiny(P).bitcast(BF16).rearrange("p (a n) -> p a n", a=2)
        iota_f = peer_tiny(NK)
        idx = peer_tiny(NSLOT, dt=U32)
        idx_now = peer_tiny(RING, dt=U32)
        gate0 = peer_tiny(NSLOT)
        dots = peer_tiny(NSLOT)
        coef = peer_tiny(NSLOT)
        dots_now = peer_tiny(PARTS * GATED_ROWS)
        gsum = peer_tiny(PH)
        iota16 = peer_tiny(K16)

        ps = ctx.enter_context(nc.psum_tensor("ps", [P, 8, 512], F32))

        x_ready = [sem(f"x_ready{t}") for t in range(NT)]
        w_ready = [sem(f"w_ready{i}") for i in range(2)]
        lam_ready = sem("lam_ready")
        consts_ready = sem("consts_ready")
        wbc_ready = sem("wbc_ready")
        made = sem("made")
        mk = sem("mk")
        N = {k: {e: sem(f"{k}_{e}") for e in ("ssq", "var", "rstd", "hn", "trans", "hT")}
             for k in ("mix", "ffn", "ple", "fin")}
        gates_done, gates_copied = sem("gates_done"), sem("gates_copied")
        proj_done, proj_copied = sem("proj_done"), sem("proj_copied")
        rope_done, qk_trans, qk_copied = sem("rope_done"), sem("qk_trans"), sem("qk_copied")
        conv_done, silu_done = sem("conv_done"), sem("silu_done")
        gate_abs, gate_exp, gate_ln = sem("gate_abs"), sem("gate_exp"), sem("gate_ln")
        rows_done, cols_trans, cols_done = sem("rows_done"), sem("cols_trans"), sem("cols_done")
        bc_done, w_exp, w_mask = sem("bc_done"), sem("w_exp"), sem("w_mask")
        s_done, ws_ready = sem("s_done"), sem("ws_ready")
        num_done, num_used = sem("num_done"), sem("num_used")
        mem_squared = sem("mem_squared")
        lam_sum, lam_exp, lam_done = sem("lam_sum"), sem("lam_exp"), sem("lam_done")
        sc_done, nm_done, prob_exp = sem("sc_done"), sem("nm_done"), sem("prob_exp")
        comb_done, ctr_done, combT_done = sem("comb_done"), sem("ctr_done"), sem("combT_done")
        att_mm, att_done = sem("att_mm"), sem("att_done")
        cvar, crstd, cnorm, ctrans, cat_done = (sem(n) for n in ("cvar", "crstd", "cnorm", "ctrans", "cat_done"))
        out_done, out_added = sem("out_done"), sem("out_added")
        subk_ready = sem("subk_ready")
        pq_done, pq_copied, ps_done, ps_copied = (sem(n) for n in ("pq_done", "pq_copied", "ps_done", "ps_copied"))
        dve_step = sem("dve_step")
        topk_step = sem("topk_step")
        best_ready, gate_e = sem("best_ready"), sem("gate_e")
        score_out, now_ready = [sem("score_out0"), sem("score_out1")], sem("now_ready")
        x_split = sem("x_split")
        u_ready = [sem(f"u_ready{i}") for i in range(4)]
        uh_done, u_split = sem("uh_done"), sem("u_split")
        up_done = sem("up_done")
        gelu_done = sem("gelu_done")
        ga_out = [sem("ga_out0"), sem("ga_out1")]
        chosen, tab_trans, tab_done, gate_ready = sem("chosen"), sem("tab_trans"), sem("tab_done"), sem("gate_ready")
        oh_step, oh_ready = sem("oh_step"), sem("oh_ready")
        g_mm, g_evac = sem("g_mm"), sem("g_evac")
        g_out = [sem("g_out0"), sem("g_out1")]
        x_done, weighed = sem("x_done"), sem("weighed")
        held = {e: sem(f"held_{e}") for e in ("dve", "pool", "act")}
        idx_ready, idx_staged = sem("idx_ready"), sem("idx_staged")
        row_ready = [sem(f"row_ready{i}") for i in range(RING)]
        row_used = sem("row_used")
        dots_copied, dots_done, coef_gelu, coef_done, xn_done = (sem(n) for n in (
            "dots_copied", "dots_done", "coef_gelu", "coef_done", "xn_done"))
        v_ready = [sem("v_ready0"), sem("v_ready1")]
        ga_ready = [sem("ga_ready0"), sem("ga_ready1")]
        vh_done = sem("vh_done")
        vl_done = sem("vl_done")
        act_done = sem("act_done")
        dn_done = sem("dn_done")
        add_done = sem("add_done")
        ple_ready = sem("ple_ready")
        pg_done, pg_sig, pp_used = sem("pg_done"), sem("pg_sig"), sem("pp_used")
        y_ready, y_out = sem("y_ready"), [sem("y_out0"), sem("y_out1")]

        block = ctx.enter_context(nc.Block())

        def seq_of(t):
            return SEQS[0] if t < 4 else SEQS[1]

        def x_rows(t):
            src = x_a if t < 4 else x_b
            r = (t - seq_of(t)[0]) * P
            return src[r:r + P, :]

        def row_of(w):
            return w.rearrange("(a n) -> a n", a=1).to_broadcast([P, D])

        scr_s = nc.dram_tensor("scr_scores", (NT, P, 2 * PH, P), F32, kind="Internal").ap()
        scr_a = nc.dram_tensor("scr_gelu", (NK, P, DTOK), F32, kind="Internal").ap()
        scr_g = nc.dram_tensor("scr_gates", (ND * PARTS, P, NK, PART), F32, kind="Internal").ap()
        v_rows = peer_v.rearrange("(a b) d -> a b d", b=NK)

        def wait_for(eng, signal, value):
            eng.wait_ge(signal, value)
            if not isinstance(value, int):
                eng.sem_inc(held[{nc.vector.engine: "dve", nc.gpsimd.engine: "pool", nc.scalar.engine: "act"}[eng.engine]], 1)

        w_blocks = [w_in[:, c:c + 512] for _, c in BLOCKS]
        w_blocks += [w_out[:, 512 * i:512 * i + 512] for i in range(2)]
        w_blocks += [peer_wq[:, 512 * i:512 * i + 512] for i in range(4)]
        PQ0 = NIN + 2
        PG0 = PQ0 + 4
        PROJ_ENDS = (8, 16, 22, 28, 34, 40, 46)

        def block_read(n):
            if n < NIN:
                return proj_done, PROJ_ENDS[n]
            if n < PQ0:
                return out_done, NT * (n - NIN + 1)
            return pq_done, 4 * (n - PQ0 + 1)

        MIX0 = PROJ_ENDS[3]
        mlstm_steps = []
        for h in range(H + 1):
            last_outs = [("out", h - 1, t) for t in (4, 5)] if h else [None, None]
            if h == H:
                mlstm_steps += last_outs
                continue
            mlstm_steps += [("bc", h, 0), ("weights", h, 0), last_outs[0], ("weights", h, 1), last_outs[1]]
            mlstm_steps += [("weights", h, j) for j in (2, 3, 4)]
            mlstm_steps += [("out", h, 0), ("weights", h, 5), ("out", h, 1), ("out", h, 2), ("out", h, 3)]
        mlstm_steps = [step for step in mlstm_steps if step]
        n_slots = PROJ_ENDS[-1] - MIX0
        slots = [mlstm_steps[len(mlstm_steps) * i // n_slots:len(mlstm_steps) * (i + 1) // n_slots] for i in range(n_slots)]
        w_blocks += [ple_w_gate[:, 512 * i:512 * i + 512] for i in range(2)]

        @block.sync
        def _(sp):
            def load_block(n):
                if 2 <= n < PG0:
                    sp.wait_ge(*block_read(n - 2))
                sp.dma_start(W[:, n % 2], w_blocks[n].rearrange("(c p) n -> p c n", p=P)).then_inc(w_ready[n % 2], 16)

            sp.dma_start(X[:, 0], x_rows(0)).then_inc(x_ready[0], 16)
            sp.dma_start(wbc, row_of(norm_mix)).then_inc(wbc_ready, 16)
            for t in range(1, NT):
                sp.dma_start(X[:, t], x_rows(t)).then_inc(x_ready[t], 16)
            sp.dma_start(gw[:], gate_w.rearrange("(c p) k n -> p c k n", p=P)).then_inc(consts_ready, 16)
            sp.dma_start(gb[0:36, :], gate_b).then_inc(consts_ready, 16)
            load_block(0)
            load_block(1)
            sp.dma_start(convw, conv_w).then_inc(consts_ready, 16)
            sp.dma_start(again, attn_gain).then_inc(consts_ready, 16)
            sp.dma_start(mgain, mlstm_gain).then_inc(consts_ready, 16)
            sp.dma_start(ropet, rope.rearrange("(t p) a b -> p t a b", p=P)).then_inc(consts_ready, 16)
            sp.wait_ge(N["mix"]["hn"], NT)
            sp.dma_start(lq, lambda_qk.rearrange("(o a) b -> o a b", o=1).to_broadcast([P, 4, QK])).then_inc(lam_ready, 16)
            for n in range(2, NIN + 2):
                load_block(n)
            sp.wait_ge(bc_done, H)
            for t in range(NT):
                if t == 5:
                    sp.wait_ge(qk_trans, 2 * NT)
                sp.dma_start(X[:, t], x_rows(t)).then_inc(x_ready[t], 16)
            sp.wait_ge(att_done, NT * H)
            sp.wait_ge(cat_done, 2 * NT)
            sp.dma_start(wbc2, row_of(norm_ffn)).then_inc(wbc_ready, 16)
            sp.dma_start(subk, subkeysT).then_inc(subk_ready, 16)
            for n in range(NIN + 2, PG0):
                load_block(n)
            sp.wait_ge(ps_done, 2 * PH)
            sp.wait_ge(x_split, 2)
            with sp.Fori(0, NK // 4) as i:
                for k in range(4):
                    sp.wait_ge(u_split, i * 4 + k + 1)
                    sp.dma_start(uf[:, k], uT[bass.ds(i * 4 + k, 1)].rearrange("o p n -> (o p) n")).then_inc(u_ready[k], 16)
            def load_v(g, b):
                sp.wait_ge(vl_done, g * GRP + GRP)
                sp.dma_start(vf[:, b], v_rows[:, bass.ds(g * GRP, GRP), :]).then_inc(v_ready[b], 16)

            def load_weights(g, b):
                sp.wait_ge(act_done, g * GRP + GRP)
                sp.dma_start(af[b], scr_a[bass.ds(g * GRP, GRP)].rearrange("k p n -> p k n")).then_inc(ga_ready[b], 16)
                sp.dma_start(gf[b], scr_g[:, :, bass.ds(g * GRP, GRP)].rearrange("s p k n -> p s (k n)")).then_inc(ga_ready[b], 16)

            load_v(0, 0)
            sp.wait_ge(dots_done, 1)
            load_v(1, 1)
            for b in range(2):
                sp.wait_ge(g_out[b], 8 * ND * PARTS + 16)
            for b in range(2):
                sp.wait_ge(ga_out[b], 16 * GRP // 2 + 16)
            load_weights(0, 0)
            sp.wait_ge(up_done, NK + 2)
            for b in range(2):
                sp.wait_ge(ga_out[b], 16 * NK // 2 + 16)
            load_weights(1, 1)
            with sp.Fori(1, NGRP // 2) as i:
                for b in range(2):
                    load_v(i * 2 + b, b)
                    load_weights(i * 2 + b, b)
            sp.wait_ge(x_done, 1)
            sp.dma_start(wbc2, row_of(norm_ple)).then_inc(wbc_ready, 16)
            sp.dma_start(pT[:, :, 0:512], pT_a.rearrange("(c p) n -> p c n", p=P)).then_inc(ple_ready, 16)
            sp.dma_start(pT[:, :, 512:TOK], pT_b.rearrange("(c p) n -> p c n", p=P)).then_inc(ple_ready, 16)
            sp.dma_start(wp, ple_w_proj.rearrange("(c p) n -> p c n", p=P)).then_inc(ple_ready, 16)
            load_block(PG0)
            load_block(PG0 + 1)
            sp.wait_ge(N["ple"]["hn"], NT)
            sp.dma_start(wbc2, row_of(norm_final)).then_inc(wbc_ready, 16)
            for t in range(NT):
                sp.wait_ge(y_ready, t + 1)
                dst = y_a if t < 4 else y_b
                r = (t - seq_of(t)[0]) * P
                sp.dma_start(dst[r:r + P, :], hn2[:, t % 2]).then_inc(y_out[t % 2], 16)
            for i in range(2):
                sp.wait_ge(y_out[i], 16 * (NT // 2))

        @block.gpsimd
        def _(pool):
            g = nc.gpsimd
            g.memset(ident[:], 0.0).then_inc(mk, 1)
            g.iota(iota16, pattern=[[1, K16]], base=0, channel_multiplier=0,
                   allow_small_or_imprecise_dtypes=True).then_inc(mk, 1)
            g.iota(iota_f, pattern=[[1, NK]], base=0, channel_multiplier=0,
                   allow_small_or_imprecise_dtypes=True).then_inc(mk, 1)
            pool.wait_ge(mk, 3)
            g.tensor_copy(iota_keys, iota_f).then_inc(mk, 1)
            g.affine_select(out=ident[:], in_=ident[:], compare_op=ALU.not_equal, fill=1.0, base=0,
                            pattern=[[-1, P]], channel_multiplier=1).then_inc(made, 1)
            g.memset(preA[:, :, 0:2], 0.0).then_inc(made, 1)
            g.memset(preA[:, :, 514:516], 0.0).then_inc(made, 1)
            g.memset(preB[:, :, 0:2], 0.0).then_inc(made, 1)
            g.memset(preB[:, :, 258:260], 0.0).then_inc(made, 1)
            g.memset(vm[:, :, :, P:P + 1], 1.0).then_inc(made, 1)
            pool.wait_ge(N["mix"]["hn"], NT)
            pool.sem_inc(row_used, RING)
            g.memset(sel, 0.0).then_inc(mk, 1)
            pool.wait_ge(mk, 5)
            for i in range(2 * H):
                row = 32 * (i // H) + i % H
                g.affine_select(out=sel[:, i], in_=sel[:, i], compare_op=ALU.not_equal, fill=-1.0,
                                base=-row, pattern=[[0, P]], channel_multiplier=1).then_inc(made, 1)
            for h in range(H):
                for j in range(NT):
                    for d in range(2):
                        pool.wait_ge(w_exp, 2 * NT * h + 2 * j + d + 1)
                        t0, n = seq_of(j)
                        o = (j - t0) * P
                        w = (wsA if n == 4 else wsB)[:, d, j - t0, o:o + P]
                        sign = 1 if d == 0 else -1
                        g.affine_select(out=w, in_=w, compare_op=ALU.is_ge, fill=0.0, base=0,
                                        pattern=[[sign, P]], channel_multiplier=-sign).then_inc(w_mask, 1)
            for q in range(2 * PH):
                pool.wait_ge(ps_copied, q + 1)
                pool.dma_start(scr_s[:, :, q].rearrange("t p n -> p t n"), sst[:, q % 2]).then_inc(score_out[q % 2], 16)
            pool.sem_inc(u_split, 4)
            pool.sem_inc(vl_done, 2 * GRP)

            def split_u(i, k):
                n = i * 4 + k
                wait_for(pool, uh_done, n + 1)
                src = uf[:, k].rearrange("p (c n) -> p c n", c=DC)
                g.tensor_tensor(ul[k % 2], src, uh[k % 2], ALU.subtract).then_inc(u_split, 1)

            def gather(table, into, r, slot, first):
                wait_for(pool, row_used, r + 1)
                g.tensor_copy(idx_now[:, slot:slot + 1], idx[:, bass.ds(r - first, 1)]).then_inc(idx_staged, 1)
                wait_for(pool, idx_staged, r + 1)
                g.indirect_dma_start(out=into[slot], out_offset=None, in_=table,
                                     in_offset=bass.IndirectOffsetOnAxis(ap=idx_now[:, slot:slot + 1], axis=0),
                                     ).then_inc(row_ready[slot], 16)

            with pool.Fori(0, U_FIRST) as i:
                for k in range(4):
                    split_u(i, k)
            pool.wait_ge(idx_ready, 1)

            def step(i, row, first_slot, n_rows):
                for k in range(4):
                    split_u(i, k)
                    for j in range(k * n_rows // 4, (k + 1) * n_rows // 4):
                        gather(peer_u, u_rows, row + j, (first_slot + j) % RING, 0)

            with pool.Fori(0, ND) as t:
                for p in range(PARTS):
                    at = p * GATED_ROWS
                    step(t * TILE_STEPS + (p + U_FIRST), t * TILE_ROWS + at, at, GATED_ROWS)
                step(t * TILE_STEPS + (U_FIRST + PARTS), t * TILE_ROWS + PARTS * GATED_ROWS, 0, PLAIN_ROWS)
            with pool.Fori(0, LAST_STEPS) as i:
                step(i + (U_FIRST + ND * TILE_STEPS), i * PLAIN_ROWS + ND * TILE_ROWS, 0, PLAIN_ROWS)
            for k in range(4):
                split_u(NK // 4 - 1, k)

            def split_v(n, b, k):
                wait_for(pool, vh_done, n + 1)
                g.tensor_tensor(vbf[:, b, 1, k], vf[:, b, k], vbf[:, b, 0, k], ALU.subtract).then_inc(vl_done, 1)

            for k in range(GRP):
                split_v(k, 0, k)
            pool.wait_ge(up_done, NK + 2)
            for k in range(RING):
                gather(peer_v, v_rows_now, NSLOT + k, k, NSLOT)
            with pool.Fori(0, NGRP // 2 - 1) as i:
                for n in range(2 * GRP):
                    split_v(i * (2 * GRP) + (n + GRP), (n // GRP + 1) % 2, n % GRP)
                    gather(peer_v, v_rows_now, i * (2 * GRP) + (n + NSLOT + RING), n % RING, NSLOT)
            for k in range(GRP):
                split_v(NK - GRP + k, 1, k)
            for n in range(NK - 2 * GRP + RING, NK):
                gather(peer_v, v_rows_now, NSLOT + n, n % RING, NSLOT)

        @block.tensor
        def _(pe):
            def norm_transposes(k):
                for t in range(NT):
                    pe.wait_ge(N[k]["hn"], t + 1)
                    for half in range(2):
                        n = 2 * t + half
                        if n >= 2:
                            pe.wait_ge(N[k]["hT"], n - 1)
                        src = (hn if k == "mix" else hn2)[:, t % 2]
                        for c in range(4):
                            mm = nc.tensor.transpose(ps[:, half, c * P:(c + 1) * P],
                                                     src[:, (4 * half + c) * P:(4 * half + c + 1) * P], ident[:])
                        mm.then_inc(N[k]["trans"], 1)

            def contract(out, lhs, rhs, n=DC):
                for c in range(n):
                    mm = nc.tensor.matmul(out, lhs(c), rhs(c), start=(c == 0), stop=(c == n - 1))
                return mm

            pe.wait_ge(made, 1)
            norm_transposes("mix")
            pe.wait_ge(N["mix"]["hT"], 2 * NT)

            pe.wait_ge(consts_ready, 16 * 6)
            for kind in range(2):
                contract(ps[0:36, 2 + kind, :], lambda c: gw[:, c, kind, :], lambda c: hT[:, c, 0:512])
                contract(ps[0:36, 4 + kind, 0:256], lambda c: gw[:, c, kind, :],
                         lambda c: hT[:, c, 512:TOK]).then_inc(gates_done, 1)

            grp = 0

            def bank_free(g):
                if g < 4:
                    pe.wait_ge(gates_copied, 4)
                else:
                    pe.wait_ge(proj_copied, g - 3)

            def qk_transposes(u):
                pe.wait_ge(rope_done, u + 1)
                if u >= 1:
                    pe.wait_ge(qk_copied, u)
                for c in range(4):
                    mm = nc.tensor.transpose(ps[:, 5, c * P:(c + 1) * P], stg[:, u % 2, c * P:(c + 1) * P], ident[:])
                mm.then_inc(qk_trans, 1)

            for n, (name, _) in enumerate(BLOCKS[:4]):
                pe.wait_ge(w_ready[n % 2], 16 * (n // 2 + 1))
                Wn = W[:, n % 2]
                if name in ("mq", "mk"):
                    for f in range(4):
                        for t0, nt in SEQS:
                            bank_free(grp)
                            mm = contract(ps[:, 2 + grp % 4, 0:nt * P], lambda c: Wn[:, c, f * P:(f + 1) * P],
                                          lambda c: hT[:, c, t0 * P:(t0 + nt) * P])
                            mm.then_inc(proj_done, 1)
                            grp += 1
                else:
                    for t in range(NT):
                        bank_free(grp)
                        mm = contract(ps[:, 2 + grp % 4, :], lambda c: hT[:, c, t * P:(t + 1) * P], lambda c: Wn[:, c, :])
                        mm.then_inc(proj_done, 1)
                        grp += 1
                assert grp == PROJ_ENDS[n]

            pe.wait_ge(rows_done, 1)
            for t in range(NT):
                nc.tensor.transpose(ps[:, 6, t * 36:(t + 1) * 36], gates["i"][:, t * P:(t + 1) * P], ident[0:36, 0:36])
                mm = nc.tensor.transpose(ps[:, 7, t * 36:(t + 1) * 36], gates["f"][:, t * P:(t + 1) * P], ident[0:36, 0:36])
            mm.then_inc(cols_trans, 1)
            pe.wait_ge(cols_done, 2)
            pe.wait_ge(proj_copied, MIX0)
            pe.wait_ge(made, 1 + 2 * H + 5)

            def broadcast(h):
                if h >= 1:
                    pe.wait_ge(w_exp, 2 * NT * h)
                for d in range(2):
                    nc.tensor.matmul(ps[:, 2 * d, :], sel[:, d * H + h], gates["M"][:, 0:512], start=True, stop=True)
                    mm = nc.tensor.matmul(ps[:, 1, 256 * d:256 * d + 256], sel[:, d * H + h], gates["M"][:, 512:TOK],
                                          start=True, stop=True)
                mm.then_inc(bc_done, 1)

            def products(h, j):
                n = NT * h + j
                t0, nt = seq_of(j)
                if n == 0:
                    pe.wait_ge(silu_done, 2 * H)
                else:
                    pe.wait_ge(ws_ready, n)
                nc.tensor.matmul(ps[:, 3, 0:nt * P], mT[:, H + h, j * P:(j + 1) * P],
                                 mT[:, h, t0 * P:(t0 + nt) * P], start=True, stop=True).then_inc(s_done, 1)

            def weighted_sums(h, t):
                m = NT * h + t
                t0, nt = seq_of(t)
                pe.wait_ge(ws_ready, NT * h + t0 + nt)
                if m >= 1:
                    pe.wait_ge(num_used, m)
                ws = wsA if nt == 4 else wsB
                i = t - t0
                for d in range(2):
                    js = range(0, i + 1) if d == 0 else range(i, nt)
                    for j in js:
                        mm = nc.tensor.matmul(ps[:, 4, d * 129:(d + 1) * 129],
                                              ws[:, d, j, i * P:(i + 1) * P], vm[:, t0 + j, h, :],
                                              start=(j == js[0]), stop=(j == js[-1]))
                mm.then_inc(num_done, 1)

            for slot, between in enumerate(slots):
                grp = MIX0 + slot
                n, t = 4 + slot // NT, slot % NT
                if t == 0:
                    pe.wait_ge(w_ready[n % 2], 16 * (n // 2 + 1))
                if slot >= 2:
                    pe.wait_ge(proj_copied, grp - 1)
                done = 0
                for i, (kind, h, j) in enumerate(between):
                    share = DC * (i + 1) // (len(between) + 1)
                    for c in range(done, share):
                        nc.tensor.matmul(ps[:, 6 + grp % 2, :], hT[:, c, t * P:(t + 1) * P], W[:, n % 2, c, :],
                                         start=(c == 0), stop=False)
                    done = share
                    if kind == "bc":
                        broadcast(h)
                    elif kind == "weights":
                        products(h, j)
                    else:
                        weighted_sums(h, j)
                for c in range(done, DC):
                    mm = nc.tensor.matmul(ps[:, 6 + grp % 2, :], hT[:, c, t * P:(t + 1) * P], W[:, n % 2, c, :],
                                          start=(c == 0), stop=(c == DC - 1))
                mm.then_inc(proj_done, 1)
                if 1 <= slot <= 2 * NT:
                    qk_transposes(slot - 1)

            def scores_of(m):
                h, t = divmod(m, NT)
                t0, nt = seq_of(t)
                if m >= 2:
                    pe.wait_ge(prob_exp, 2 * (m - 1))
                for c in range(2):
                    mm = nc.tensor.matmul(ps[:, 2 * (m % 2) + c, 0:nt * P], aT[QK * c:QK * c + QK, h, t * P:(t + 1) * P],
                                          aT[QK * c:QK * c + QK, H + h, t0 * P:(t0 + nt) * P], start=True, stop=True)
                mm.then_inc(sc_done, 1)

            def turn(m):
                nt = seq_of(m % NT)[1]
                pe.wait_ge(comb_done, m + 1)
                if m >= 2:
                    pe.wait_ge(combT_done, m - 1)
                for c in range(nt):
                    mm = nc.tensor.transpose(ps[:, 4 + m % 2, c * P:(c + 1) * P], comb[:, m % 2, c * P:(c + 1) * P], ident[:])
                mm.then_inc(ctr_done, 1)

            def values(m):
                h, t = divmod(m, NT)
                t0, nt = seq_of(t)
                pe.wait_ge(combT_done, m + 1)
                if m >= 2:
                    pe.wait_ge(att_done, m - 1)
                contract(ps[:, 6 + m % 2, 0:P], lambda c: combT[:, m % 2, c * P:(c + 1) * P],
                         lambda c: av[:, t0 + c, h * P:(h + 1) * P], nt).then_inc(att_mm, 1)

            pe.wait_ge(num_used, NT * H)
            pe.wait_ge(ws_ready, NT * H)
            pe.wait_ge(proj_copied, PROJ_ENDS[-1])
            pe.wait_ge(qk_copied, 2 * NT)
            MU = NT * H
            scores_of(0)
            for m in range(MU + 2):
                if m + 1 < MU:
                    scores_of(m + 1)
                if 1 <= m <= MU:
                    turn(m - 1)
                if m >= 2:
                    values(m - 2)

            for t in range(NT):
                pe.wait_ge(cnorm, 2 * (t + 1))
                if t >= 1:
                    pe.wait_ge(cat_done, 2 * t)
                for k, src in enumerate((att, mo)):
                    for h in range(H):
                        mm = nc.tensor.transpose(ps[:, k, h * P:(h + 1) * P], src[:, t, h * P:(h + 1) * P], ident[:])
                    mm.then_inc(ctrans, 1)
            pe.wait_ge(cat_done, 2 * NT)
            pe.wait_ge(att_done, NT * H)
            for i in range(2):
                n = NIN + i
                pe.wait_ge(w_ready[n % 2], 16 * (n // 2 + 1))
                for t in range(NT):
                    g = NT * i + t
                    if g >= 4:
                        pe.wait_ge(out_added, g - 3)
                    mm = contract(ps[:, 2 + g % 4, :], lambda c: catT[:, c, t * P:(t + 1) * P], lambda c: W[:, n % 2, c, :])
                    mm.then_inc(out_done, 1)

            norm_transposes("ffn")
            pe.wait_ge(N["ffn"]["hT"], 2 * NT)
            pe.wait_ge(subk_ready, 16)
            for q in range(2 * PH):
                n = PQ0 + q // 4
                if q % 4 == 0:
                    pe.wait_ge(w_ready[n % 2], 16 * (n // 2 + 1))
                if q >= 2:
                    pe.wait_ge(pq_copied, q - 1)
                for t0, nt in SEQS:
                    b = 2 + 2 * (q % 2) + (t0 > 0)
                    mm = contract(ps[:, b, 0:nt * P], lambda c: W[:, n % 2, c, (q % 4) * P:(q % 4 + 1) * P],
                                  lambda c: hT[:, c, t0 * P:(t0 + nt) * P])
                mm.then_inc(pq_done, 1)

                def score(q):
                    pe.wait_ge(pq_copied, q + 1)
                    if q >= 1:
                        pe.wait_ge(ps_copied, q)
                    for t in range(NT):
                        mm = nc.tensor.matmul(ps[:, 6 + t // 4, (t % 4) * P:(t % 4 + 1) * P], qT[:, q % 2, t * P:(t + 1) * P],
                                              subk[:, q, :], start=True, stop=True)
                    mm.then_inc(ps_done, 1)
                if q >= 1:
                    score(q - 1)
            score(2 * PH - 1)

            pe.sem_inc(up_done, 2)
            pe.sem_inc(g_mm, 2)

            def up(n, k):
                pe.wait_ge(u_split, n + 5)
                pe.wait_ge(gelu_done, n + 1)
                for c in range(DC):
                    for w, x in ((uh, xh), (uh, xl), (ul, xh)):
                        for b in range(2):
                            mm = nc.tensor.matmul(ps[:, 2 * (k % 2) + b, 0:HALF_T], w[k % 2][:, c, :],
                                                  x[:, c, b * HALF_T:(b + 1) * HALF_T],
                                                  start=(c == 0 and w is uh and x is xh),
                                                  stop=(c == DC - 1 and w is ul))
                mm.then_inc(up_done, 1)

            def gate_matrices(n, k):
                pe.wait_ge(oh_ready, n * 3 + 3)
                pe.wait_ge(g_evac, n + 1)
                for i in range(TU):
                    for part in range(2):
                        mm = nc.tensor.matmul(ps[:, 4 + 2 * (k % 2) + i // 4, (i % 4) * P:(i % 4 + 1) * P],
                                              oh[:, k % 2, 0, i], oh[:, k % 2, 2 + part, i],
                                              start=(part == 0), stop=(part == 1))
                mm.then_inc(g_mm, 1)

            def turn_tables(t):
                pe.wait_ge(gate_ready, t + 2)
                pe.wait_ge(g_evac, t * 16 + 2)
                for i, e in enumerate((e1, e2, gate)):
                    mm = nc.tensor.transpose(ps[:, 4, i * P:(i + 1) * P], e, ident[:])
                mm.then_inc(tab_trans, 1)

            pe.wait_ge(x_split, 2)
            with pe.Fori(0, U_FIRST) as i:
                for k in range(4):
                    up(i * 4 + k, k)
            with pe.Fori(0, ND) as t:
                turn_tables(t)
                with pe.Fori(0, PARTS) as i:
                    for k in range(4):
                        up(t * (4 * TILE_STEPS) + i * 4 + (k + 4 * U_FIRST), k)
                        gate_matrices(t * 16 + i * 4 + k, k)
                for k in range(4):
                    up(t * (4 * TILE_STEPS) + (4 * U_FIRST + UNITS + k), k)
            with pe.Fori(U_FIRST + ND * TILE_STEPS, NK // 4) as i:
                for k in range(4):
                    up(i * 4 + k, k)

            pe.wait_ge(gelu_done, NK + 2)
            pe.wait_ge(g_evac, ND * UNITS + 2)
            pe.sem_inc(dn_done, 4 * ND)
            with pe.Fori(0, NGRP // 2) as i:
                for b in range(2):
                    pe.wait_ge(vl_done, i * (2 * GRP) + (b * GRP + 3 * GRP))
                    pe.wait_ge(act_done, i * (2 * GRP) + (b * GRP + 3 * GRP))
                    for o in range(2 * ND):
                        t, half = divmod(o, 2)
                        n = i * (4 * ND) + (b * 2 * ND + o)
                        pe.wait_ge(add_done, n + (2 * ND - NBANK + 1))
                        for k in range(GRP):
                            for pa, pv in ((0, 0), (0, 1), (1, 0)):
                                mm = nc.tensor.matmul(ps[:, o % NBANK, :], abf[:, b, pa, k, t * P:(t + 1) * P],
                                                      vbf[:, b, pv, k, half * 512:half * 512 + 512],
                                                      start=(k == 0 and pa + pv == 0), stop=(k == GRP - 1 and pa == 1))
                        mm.then_inc(dn_done, 1)

            pe.wait_ge(x_done, 1)
            norm_transposes("ple")
            pe.wait_ge(N["ple"]["hT"], 2 * NT)
            pe.wait_ge(ple_ready, 48)
            for i in range(2):
                n = PG0 + i
                pe.wait_ge(w_ready[n % 2], 16 * (n // 2 + 1))
                for t in range(NT):
                    g = NT * i + t
                    if g >= 2:
                        pe.wait_ge(pp_used, g - 1)
                    contract(ps[:, 2 + 2 * (g % 2), :], lambda c: hT[:, c, t * P:(t + 1) * P], lambda c: W[:, n % 2, c, :])
                    contract(ps[:, 3 + 2 * (g % 2), :], lambda c: pT[:, c, t * P:(t + 1) * P],
                             lambda c: wp[:, c, 512 * i:512 * i + 512], 2).then_inc(pg_done, 1)

        @block.scalar
        def _(act):
            a = nc.scalar

            def norm(k):
                for t in range(NT):
                    if k == "mix":
                        act.wait_ge(x_ready[t], 16)
                    j = junk if k == "mix" else junk2
                    if t >= 1:
                        act.wait_ge(N[k]["ssq"], t)
                    a.activation(j, X[:, t], ACT.Square, accum_out=ssq[:, t:t + 1]).then_inc(N[k]["ssq"], 1)
                act.wait_ge(N[k]["var"], 1)
                a.activation(rstd, var, ACT.Sqrt).then_inc(N[k]["rstd"], 1)

            def norm_copies(k):
                for n in range(2 * NT):
                    t, half = divmod(n, 2)
                    act.wait_ge(N[k]["trans"], n + 1)
                    a.activation(hT[:, 4 * half:4 * half + 4, t * P:(t + 1) * P],
                                 ps[:, half, :].rearrange("p (c n) -> p c n", c=4), ACT.Copy).then_inc(N[k]["hT"], 1)

            norm("mix")
            norm_copies("mix")

            def qk_copy(u):
                act.wait_ge(qk_trans, u + 1)
                t, part = u % NT, u // NT
                a.activation(aT[:, H * part:H * part + H, t * P:(t + 1) * P],
                             ps[:, 5, :].rearrange("p (c n) -> p c n", c=4), ACT.Copy).then_inc(qk_copied, 1)

            grp = 0
            for name, _ in BLOCKS[:4]:
                if name in ("mq", "mk"):
                    for f in range(4):
                        for (t0, nt), dst in zip(SEQS, (preA, preB)):
                            act.wait_ge(proj_done, grp + 1)
                            c = f + (4 if name == "mk" else 0)
                            a.activation(dst[:, c, 2:2 + nt * P], ps[:, 2 + grp % 4, 0:nt * P], ACT.Copy).then_inc(proj_copied, 1)
                            grp += 1
                    if name == "mq":
                        act.wait_ge(gate_abs, 1)
                        a.activation(gates["e"], gates["e"], ACT.Exp, scale=-1.0).then_inc(gate_exp, 1)
                        act.wait_ge(gate_exp, 1)
                        a.activation(gates["e"], gates["e"], ACT.Ln, bias=1.0).then_inc(gate_ln, 1)
                        act.wait_ge(lam_sum, 2)
                        a.activation(lexp, lsum, ACT.Exp).then_inc(lam_exp, 1)
                    continue
                for t in range(NT):
                    act.wait_ge(proj_done, grp + 1)
                    src = ps[:, 2 + grp % 4, :]
                    if name == "mv":
                        a.activation(vm[:, t, :, 0:P], src.rearrange("p (h e) -> p h e", h=H), ACT.Copy).then_inc(proj_copied, 1)
                    elif name == "mo":
                        a.activation(mo[:, t], src, ACT.Sigmoid).then_inc(proj_copied, 1)
                    grp += 1
            for c in range(2 * H):
                act.wait_ge(conv_done, c + 1)
                a.activation(mT[:, c, :], mT[:, c, :], ACT.Silu).then_inc(silu_done, 1)
            act.wait_ge(cols_trans, 1)
            a.activation(acol.rearrange("p t n -> p (t n)"), ps[:, 6, 0:NT * 36], ACT.Copy).then_inc(cols_done, 1)
            a.activation(floor.rearrange("p t n -> p (t n)"), ps[:, 7, 0:NT * 36], ACT.Exp, scale=-1.0).then_inc(cols_done, 1)
            act.wait_ge(cols_done, 2)

            def mlstm_exps(h, j):
                t0, nt = seq_of(j)
                i = j - t0
                act.wait_ge(bc_done, h + 1)
                if h >= 1 and i == 0:
                    act.wait_ge(num_done, NT * (h - 1) + t0 + nt)
                for d in range(2):
                    lo, hi = (i * P, nt * P) if d == 0 else (0, (i + 1) * P)
                    if nt == 4:
                        src, dst = ps[:, 2 * d, lo:hi], wsA[:, d, i, lo:hi]
                    else:
                        src, dst = ps[:, 1, 256 * d + lo:256 * d + hi], wsB[:, d, i, lo:hi]
                    r = 32 * d + h
                    a.activation(dst, src, ACT.Exp, bias=acol[:, j, r:r + 1]).then_inc(w_exp, 1)

            for slot, between in enumerate(slots):
                for kind, h, j in between:
                    if kind == "weights":
                        mlstm_exps(h, j)
                grp = MIX0 + slot
                t = slot % NT
                act.wait_ge(proj_done, grp + 1)
                src = ps[:, 6 + grp % 2, :]
                if slot < 2 * NT:
                    if slot >= 2:
                        act.wait_ge(qk_trans, slot - 1)
                    elif slot == 0:
                        act.wait_ge(conv_done, 2 * H)
                    a.activation(stg[:, slot % 2], src, ACT.Copy).then_inc(proj_copied, 1)
                else:
                    a.activation(av[:, t], src, ACT.Copy).then_inc(proj_copied, 1)
                if 1 <= slot <= 2 * NT:
                    qk_copy(slot - 1)
            MU = NT * H

            def exps(m):
                nt = seq_of(m % NT)[1]
                act.wait_ge(nm_done, m + 1)
                if m >= 2:
                    act.wait_ge(comb_done, m - 1)
                else:
                    act.wait_ge(num_done, MU)
                for c in range(2):
                    a.activation(prob[:, m % 2, c, 0:nt * P], ps[:, 2 * (m % 2) + c, 0:nt * P], ACT.Exp,
                                 bias=nmax[:, m % 2, c:c + 1], scale=QK ** -0.5,
                                 accum_out=z[:, m % 2, c:c + 1]).then_inc(prob_exp, 1)

            def copy_turned(m):
                nt = seq_of(m % NT)[1]
                act.wait_ge(ctr_done, m + 1)
                if m >= 2:
                    act.wait_ge(att_mm, m - 1)
                a.activation(combT[:, m % 2, 0:nt * P], ps[:, 4 + m % 2, 0:nt * P], ACT.Copy).then_inc(combT_done, 1)

            def take_att(m):
                h, t = divmod(m, NT)
                act.wait_ge(att_mm, m + 1)
                a.activation(att[:, t, h * P:(h + 1) * P], ps[:, 6 + m % 2, 0:P], ACT.Copy)
                if m >= 1:
                    act.wait_ge(att_done, m)
                a.activation(junk_sq, ps[:, 6 + m % 2, 0:P], ACT.Square,
                             accum_out=ass_[:, t * H + h:t * H + h + 1]).then_inc(att_done, 1)

            for m in range(MU + 2):
                if m < MU:
                    exps(m)
                if 1 <= m <= MU:
                    copy_turned(m - 1)
                if m >= 2:
                    take_att(m - 2)
            act.wait_ge(cvar, 2)
            a.activation(ars, ars, ACT.Sqrt).then_inc(crstd, 1)
            a.activation(mrs, mrs, ACT.Sqrt).then_inc(crstd, 1)
            for t in range(NT):
                act.wait_ge(ctrans, 2 * t + 1)
                a.activation(catT[:, 0:H, t * P:(t + 1) * P], ps[:, 0, :].rearrange("p (c n) -> p c n", c=4), ACT.Copy,
                             scale=again08).then_inc(cat_done, 1)
                act.wait_ge(ctrans, 2 * t + 2)
                for h in range(H):
                    ins = a.activation(catT[:, H + h, t * P:(t + 1) * P], ps[:, 1, h * P:(h + 1) * P], ACT.Copy,
                                       scale=mgain[:, h:h + 1])
                ins.then_inc(cat_done, 1)

            act.wait_ge(out_added, 2 * NT)
            norm("ffn")
            norm_copies("ffn")
            for q in range(2 * PH):
                act.wait_ge(pq_done, q + 1)
                if q >= 2:
                    act.wait_ge(ps_done, q - 1)
                a.activation(qT[:, q % 2, 0:512], ps[:, 2 + 2 * (q % 2), :], ACT.Copy)
                a.activation(qT[:, q % 2, 512:TOK], ps[:, 3 + 2 * (q % 2), 0:256], ACT.Copy).then_inc(pq_copied, 1)
            act.sem_inc(gelu_done, 2)
            for b in range(2):
                act.sem_inc(ga_out[b], 16)
                act.sem_inc(g_out[b], 16)
            act.sem_inc(g_evac, 2)

            def evacuate(n, k, p):
                wait_for(act, g_mm, n + 3)
                for b in range(2):
                    ins = a.activation(gst[p % 2][:, :, TU * k + 4 * b:TU * k + 4 * b + 4].rearrange("p k t -> p t k"),
                                       ps[:, 4 + 2 * (k % 2) + b, :].rearrange("p (t k) -> p t k", t=4), ACT.Copy)
                ins.then_inc(g_evac, 1)

            def first_part_of_u(steps, k):
                wait_for(act, u_ready[k], steps * 16 + 16)
                a.activation(uh[k % 2], uf[:, k].rearrange("p (c n) -> p c n", c=DC), ACT.Copy).then_inc(uh_done, 1)

            def gelu(step, k, cast=True):
                n, pairs = step * 4 + k, step * 2 + k // 2
                wait_for(act, ga_out[k % 2], pairs * 16 + 16)
                wait_for(act, up_done, n + 3)
                a.activation(gst_a[:, k % 2].rearrange("p (b n) -> p b n", b=2),
                             ps[:, 2 * (k % 2):2 * (k % 2) + 2, 0:HALF_T], ACT.Gelu).then_inc(gelu_done, 1)
                if cast:
                    first_part_of_u(step if k < 2 else step + 1, (k + 2) % 4)
                wait_for(act, gelu_done, n + 3)
                act.dma_start(scr_a[bass.ds(n, 1)].rearrange("o p n -> (o p) n"), gst_a[:, k % 2]).then_inc(ga_out[k % 2], 16)

            def gate_exps(t):
                wait_for(act, best_ready, t + 1)
                a.activation(gate, bestv.rearrange("p a b -> p (a b)"), ACT.Exp).then_inc(gate_e, 1)

            def load_scores(t):
                wait_for(act, chosen, t)
                act.dma_start(now, scr_s[bass.ds(t, 1)].rearrange("o p q n -> (o p) (q n)")).then_inc(now_ready, 16)

            for q in range(2):
                act.wait_ge(score_out[q], 16 * PH)
            act.wait_ge(x_split, 2)
            act.dma_start(now, scr_s[0].rearrange("p q n -> p (q n)")).then_inc(now_ready, 16)
            for k in range(2):
                first_part_of_u(0, k)
            for part in range(2):
                with act.Fori(part * U_FIRST // 2, (part + 1) * U_FIRST // 2) as i:
                    for k in range(4):
                        gelu(i, k)
                gate_exps(part)
                if part == 0:
                    load_scores(1)

            def tile_gelus(t, more, load=False):
                for p in range(PARTS):
                    if load and p == 1:
                        load_scores(t + 3)
                    wait_for(act, g_out[p % 2], t * (16 * PARTS // 2) + 16 * (p // 2 + 1))
                    for k in range(4):
                        gelu(t * TILE_STEPS + (p + U_FIRST), k)
                        evacuate(t * UNITS + (4 * p + k), k, p)
                    if more and p == PARTS - 2:
                        gate_exps(t + 2)
                    wait_for(act, g_evac, t * UNITS + (4 * p + 6))
                    act.dma_start(scr_g[bass.ds(t * PARTS + p, 1)].rearrange("o p k n -> (o p) k n"), gst[p % 2],
                                  ).then_inc(g_out[p % 2], 16)

            def plain_gelus(t):
                for k in range(4):
                    gelu(t * TILE_STEPS + (U_FIRST + PARTS), k)

            load_scores(2)
            tile_gelus(0, True)
            load_scores(3)
            plain_gelus(0)
            with act.Fori(1, ND - 2) as t:
                tile_gelus(t, True, load=True)
                plain_gelus(t)
            tile_gelus(ND - 2, True)
            plain_gelus(ND - 2)
            tile_gelus(ND - 1, False)
            plain_gelus(ND - 1)

            def first_part_of_v(i, b):
                wait_for(act, v_ready[b], i * 16 + 16)
                for k in range(GRP):
                    a.activation(vbf[:, b, 0, k], vf[:, b, k], ACT.Copy).then_inc(vh_done, 1)

            with act.Fori(U_FIRST + ND * TILE_STEPS, NK // 4 - 1) as i:
                for k in range(4):
                    gelu(i, k)
            for b in range(2):
                act.wait_ge(g_out[b], 8 * ND * PARTS + 16)
            first_part_of_v(0, 0)
            for k in range(4):
                gelu(NK // 4 - 1, k, cast=k < 2)
            act.wait_ge(dots_done, 1)
            a.activation(coef, dots, ACT.Gelu).then_inc(coef_gelu, 1)
            first_part_of_v(0, 1)
            with act.Fori(1, NGRP // 2) as i:
                for b in range(2):
                    wait_for(act, dn_done, i * (4 * ND) + (b + 1) * 2 * ND)
                    first_part_of_v(i, b)
            act.wait_ge(x_done, 1)
            norm("ple")
            norm_copies("ple")
            for g in range(2 * NT):
                act.wait_ge(pg_done, g + 1)
                if g >= 2:
                    act.wait_ge(pp_used, g - 1)
                a.activation(sig[:, g % 2], ps[:, 2 + 2 * (g % 2), :], ACT.Sigmoid).then_inc(pg_sig, 1)
            act.wait_ge(pp_used, 2 * NT)
            norm("fin")

        @block.vector
        def _(dve):
            v = nc.vector
            steps = [0]

            def link(ins):
                steps[0] += 1
                ins.then_inc(dve_step, 1)
                dve.wait_ge(dve_step, steps[0])

            def norm(k, gain, loads):
                dve.wait_ge(N[k]["ssq"], NT)
                link(v.tensor_scalar(var, ssq, 1.0 / D, EPS, ALU.mult, ALU.add))
                v.reciprocal(var, var).then_inc(N[k]["var"], 1)
                dve.wait_ge(N[k]["rstd"], 1)
                dve.wait_ge(wbc_ready, 16 * loads)
                for t in range(NT):
                    if k == "fin":
                        if t >= 2:
                            dve.wait_ge(y_out[t % 2], 16 * (t // 2))
                    elif t >= 2:
                        dve.wait_ge(N[k]["trans"], 2 * (t - 1))
                    v.scalar_tensor_tensor((hn if k == "mix" else hn2)[:, t % 2], X[:, t], rstd[:, t:t + 1], gain,
                                           ALU.mult, ALU.mult).then_inc(y_ready if k == "fin" else N[k]["hn"], 1)

            norm("mix", wbc, 1)

            dve.wait_ge(consts_ready, 16 * 6)
            for kind, name in enumerate(("i", "f")):
                dve.wait_ge(gates_done, kind + 1)
                v.tensor_scalar(gates[name][:, 0:512], ps[0:36, 2 + kind, :], gb[0:36, kind:kind + 1], None,
                                ALU.add).then_inc(gates_copied, 1)
                v.tensor_scalar(gates[name][:, 512:TOK], ps[0:36, 4 + kind, 0:256], gb[0:36, kind:kind + 1], None,
                                ALU.add).then_inc(gates_copied, 1)
            dve.wait_ge(gates_copied, 4)
            v.scalar_tensor_tensor(gates["e"], gates["f"], -1.0, gates["f"], ALU.mult, ALU.max).then_inc(gate_abs, 1)
            dve.wait_ge(lam_ready, 16)
            for i in range(2):
                if i:
                    dve.wait_ge(lam_sum, 1)
                v.tensor_tensor_reduce(junk_sq[:, 0:QK], lq[:, 2 * i], lq[:, 2 * i + 1], 1.0, 0.0, ALU.mult, ALU.add,
                                       lsum[:, i:i + 1]).then_inc(lam_sum, 1)
            v.tensor_scalar(again08, again, 1.0 - LAM_INIT, None, ALU.mult).then_inc(lam_done, 1)

            def convolve(c):
                dve.wait_ge(proj_copied, 2 * (c + 1))
                for k in range(5):
                    for src, dst, n in ((preA, mT[:, c, 0:512], 512), (preB, mT[:, c, 512:TOK], 256)):
                        w = convw[:, c, k:k + 1]
                        if k == 0:
                            ins = v.tensor_scalar(dst, src[:, c, 0:n], w, None, ALU.mult)
                        else:
                            ins = v.scalar_tensor_tensor(dst, src[:, c, k:k + n], w, dst, ALU.mult, ALU.add)
                    if k < 4:
                        link(ins)
                ins.then_inc(conv_done, 1)

            dve.wait_ge(made, 6)
            for c in range(H):
                convolve(c)
            dve.wait_ge(gate_ln, 1)
            link(v.scalar_tensor_tensor(gates["f"], gates["f"], 0.0, gates["e"], ALU.min, ALU.subtract))

            def scan(dst, src, op):
                for t0, nt in SEQS:
                    cols = slice(t0 * P, (t0 + nt) * P)
                    v.tensor_tensor_scan(dst[0:32, cols], src[0:32, cols], src[0:32, cols], 0.0, op, ALU.bypass)
                    ins = v.tensor_tensor_scan(dst[32:36, cols][:, ::-1], src[32:36, cols][:, ::-1],
                                               src[32:36, cols][:, ::-1], 0.0, op, ALU.bypass)
                link(ins)
            scan(gates["B"], gates["f"], ALU.add)
            link(v.tensor_tensor(gates["i"], gates["i"], gates["B"], ALU.subtract))
            scan(gates["M"], gates["i"], ALU.max)
            v.tensor_tensor(gates["f"], gates["B"], gates["M"], ALU.add).then_inc(rows_done, 1)
            dve.wait_ge(lam_exp, 1)
            v.tensor_scalar(nlam, lexp[:, 1:2], lexp[:, 0:1], LAM_INIT, ALU.subtract, ALU.subtract).then_inc(lam_done, 1)
            for c in range(H, 2 * H):
                convolve(c)

            def rotate(u):
                t = u % NT
                i = t - seq_of(t)[0]
                dve.wait_ge(proj_copied, PROJ_ENDS[3] + u + 1)
                x = stg[:, u % 2].rearrange("p (g n) -> p g n", g=8)
                x1, x2 = x[:, :, 0:HALF], x[:, :, HALF:2 * HALF]
                cos, sin = (ropet[:, i, j:j + 1, :].to_broadcast([P, 8, HALF]) for j in range(2))
                if u:
                    dve.wait_ge(rope_done, u)
                v.tensor_tensor(rot[:, 0], x1, cos, ALU.mult)
                v.tensor_tensor(rot[:, 1], x2, sin, ALU.mult)
                v.tensor_tensor(rot[:, 2], x2, cos, ALU.mult)
                link(v.tensor_tensor(rot[:, 3], x1, sin, ALU.mult))
                v.tensor_tensor(x1, rot[:, 0], rot[:, 1], ALU.subtract)
                v.tensor_tensor(x2, rot[:, 2], rot[:, 3], ALU.add).then_inc(rope_done, 1)

            KSCALE = float(P) ** -0.5

            def mlstm_weights(h, j):
                n = NT * h + j
                t0, nt = seq_of(j)
                i = j - t0
                dve.wait_ge(s_done, n + 1)
                dve.wait_ge(w_mask, 2 * n + 2)
                for d in range(2):
                    lo, hi = (i * P, nt * P) if d == 0 else (0, (i + 1) * P)
                    w = (wsA if nt == 4 else wsB)[:, d, i, lo:hi]
                    ins = v.scalar_tensor_tensor(w, ps[:, 3, lo:hi], KSCALE, w, ALU.mult, ALU.mult)
                ins.then_inc(ws_ready, 1)

            def mlstm_out(h, t):
                m = NT * h + t
                dve.wait_ge(num_done, m + 1)
                num = ps[:, 4, 0:2 * (P + 1)].rearrange("p (d n) -> p d n", d=2)
                link(v.tensor_tensor(den, num[:, :, P], floor[:, t, h:h + 33:32], ALU.max))
                link(v.scalar_tensor_tensor(den, num[:, :, P], -1.0, den, ALU.mult, ALU.max))
                link(v.reciprocal(rden, den))
                hs = hsum[:, m % 2]
                if m >= 2:
                    dve.wait_ge(mem_squared, m - 1)
                link(v.tensor_scalar(hs, num[:, 0, 0:P], rden[:, 0:1], None, ALU.mult))
                v.scalar_tensor_tensor(hs, num[:, 1, 0:P], rden[:, 1:2], hs, ALU.mult, ALU.add).then_inc(num_used, 1)
                dve.wait_ge(num_used, m + 1)
                o = mo[:, t, h * P:(h + 1) * P]
                link(v.tensor_tensor(o, o, hs, ALU.mult))
                v.tensor_tensor_reduce(hs, o, o, 1.0, 0.0, ALU.mult, ALU.add, mss[:, t * H + h:t * H + h + 1]).then_inc(mem_squared, 1)

            dve.wait_ge(cols_done, 2)
            for slot, between in enumerate(slots):
                if 1 <= slot <= 2 * NT:
                    rotate(slot - 1)
                for kind, h, j in between:
                    if kind == "weights":
                        mlstm_weights(h, j)
                    elif kind == "out":
                        mlstm_out(h, j)

            MU = NT * H

            def maxima(m):
                nt = seq_of(m % NT)[1]
                dve.wait_ge(sc_done, m + 1)
                b = 2 * (m % 2)
                link(v.tensor_reduce(nmax[:, m % 2], ps[:, b:b + 2, 0:nt * P], AX.X, ALU.max, negate=True))
                v.tensor_scalar(nmax[:, m % 2], nmax[:, m % 2], QK ** -0.5, None, ALU.mult).then_inc(nm_done, 1)

            def combine(m):
                nt = seq_of(m % NT)[1]
                s = m % 2
                dve.wait_ge(prob_exp, 2 * (m + 1))
                if m:
                    dve.wait_ge(comb_done, m)
                link(v.reciprocal(rz, z[:, s]))
                p0, p1 = prob[:, s, 0, 0:nt * P], prob[:, s, 1, 0:nt * P]
                v.tensor_scalar(p0, p0, rz[:, 0:1], None, ALU.mult)
                link(v.tensor_scalar(nl, rz[:, 1:2], nlam, None, ALU.mult))
                if m >= 2:
                    dve.wait_ge(ctr_done, m - 1)
                v.scalar_tensor_tensor(comb[:, s, 0:nt * P], p1, nl, p0, ALU.mult, ALU.add).then_inc(comb_done, 1)

            dve.wait_ge(lam_done, 2)
            for m in range(MU + 1):
                if m < MU:
                    maxima(m)
                if m >= 1:
                    combine(m - 1)

            dve.wait_ge(mem_squared, MU)
            link(v.tensor_scalar(mrs, mss, 1.0 / P, EPS, ALU.mult, ALU.add))
            v.reciprocal(mrs, mrs).then_inc(cvar, 1)
            dve.wait_ge(att_done, MU)
            link(v.tensor_scalar(ars, ass_, 1.0 / P, EPS, ALU.mult, ALU.add))
            v.reciprocal(ars, ars).then_inc(cvar, 1)
            dve.wait_ge(crstd, 2)
            for t in range(NT):
                for arr, r in ((att, ars), (mo, mrs)):
                    x = arr[:, t].rearrange("p (h n) -> p h n", h=H)
                    v.tensor_tensor(x, x, r[:, t * H:(t + 1) * H].unsqueeze(2).to_broadcast([P, H, P]),
                                    ALU.mult).then_inc(cnorm, 1)

            for g in range(2 * NT):
                i, t = divmod(g, NT)
                dve.wait_ge(out_done, g + 1)
                dve.wait_ge(x_ready[t], 32)
                x = X[:, t, 512 * i:512 * i + 512]
                v.tensor_tensor(x, ps[:, 2 + g % 4, :], x, ALU.add).then_inc(out_added, 1)

            dve.wait_ge(out_added, 2 * NT)
            norm("ffn", wbc2, 2)
            for q in range(2 * PH):
                dve.wait_ge(ps_done, q + 1)
                if q >= 2:
                    dve.wait_ge(score_out[q % 2], 16 * (q // 2))
                v.tensor_copy(sst[:, q % 2, 0:4], ps[:, 6, :].rearrange("p (t n) -> p t n", t=4))
                v.tensor_copy(sst[:, q % 2, 4:6], ps[:, 7, 0:256].rearrange("p (t n) -> p t n", t=2)).then_inc(ps_copied, 1)
                if q == 1:
                    dve.wait_ge(N["ffn"]["hT"], 2 * NT)
                    v.tensor_copy(xh, hT[:, :, P:TOK]).then_inc(x_split, 1)
                    dve.wait_ge(x_split, 1)
                    v.tensor_tensor(xl, hT[:, :, P:TOK], xh, ALU.subtract).then_inc(x_split, 1)
                    v.scalar_tensor_tensor(xn, X[:, 0], rstd[:, 0:1], wbc2, ALU.mult, ALU.mult).then_inc(xn_done, 1)
            dve.wait_ge(mk, 4)

            def best_keys(t):
                return choice(t, True)

            def best_experts(t):
                return choice(t, False)

            def choose(t):
                yield from best_keys(t)
                yield from best_experts(t)

            def choice(t, keys):
                k = [0 if keys else KEY_STEPS]

                def tlink(ins):
                    k[0] += 1
                    ins.then_inc(topk_step, 1)
                    wait_for(dve, topk_step, t * TOPK_STEPS + k[0])

                def top16(vals, inds, src):
                    tlink(v.max(vals[:, 0:8], src))
                    v.max_index(inds[:, 0:8], vals[:, 0:8], src)
                    tlink(v.match_replace(src, vals[:, 0:8], src, NEG))
                    tlink(v.max(vals[:, 8:16], src))
                    return v.max_index(inds[:, 8:16], vals[:, 8:16], src)

                if keys:
                    wait_for(dve, now_ready, t * 16 + 16)
                    for h in range(PH):
                        for half in range(2):
                            last = top16(topv[:, h, half], topi[:, h, half], now[:, (2 * h + half) * P:(2 * h + half + 1) * P])
                            if h == PH - 1 and half == 1:
                                last.then_inc(chosen, 1)
                            yield
                    assert k[0] == KEY_STEPS, k[0]
                    return
                wait_for(dve, chosen, t + 1)
                tlink(v.tensor_copy(topf, topi))
                tlink(v.tensor_tensor(cand.rearrange("p h (i j) -> p h i j", i=K16),
                                      topv[:, :, 0].unsqueeze(3).to_broadcast([P, PH, K16, K16]),
                                      topv[:, :, 1].unsqueeze(2).to_broadcast([P, PH, K16, K16]), ALU.add))
                for h in range(PH):
                    last = top16(bestv[:, h], bestc[:, h], cand[:, h])
                    yield
                tlink(last)
                for shift, half, e in ((True, 0, e1), (False, 1, e2)):
                    c = bestc.rearrange("p a b -> p (a b)")
                    if shift:
                        tlink(v.tensor_scalar(rank_u, c, 4, None, ALU.logical_shift_right))
                    else:
                        tlink(v.tensor_scalar(rank_u, c, 15, None, ALU.bitwise_and))
                    tlink(v.tensor_copy(rank, rank_u))
                    yield
                    tlink(v.tensor_tensor(onehot, rank.unsqueeze(2).to_broadcast([P, NSLOT, K16]),
                                          iota16.unsqueeze(1).to_broadcast([P, NSLOT, K16]), ALU.is_equal))
                    yield
                    oh4 = onehot.rearrange("p (h j) r -> p h j r", h=PH)
                    tlink(v.tensor_tensor(oh4, oh4, topf[:, :, half].unsqueeze(2).to_broadcast([P, PH, K16, K16]), ALU.mult))
                    yield
                    tlink(v.tensor_reduce(e, onehot, AX.X, ALU.add))
                    yield
                if isinstance(t, int) and t == 0:
                    link(v.scalar_tensor_tensor(rank, e1, float(NK), e2, ALU.mult, ALU.add))
                    v.tensor_copy(idx, rank).then_inc(idx_ready, 1)
                tlink(v.tensor_copy(gsum, bestv[:, :, 0]))
                v.tensor_tensor(bestv, bestv, gsum.unsqueeze(2).to_broadcast([P, PH, K16]), ALU.subtract).then_inc(best_ready, 1)
                yield "exp"
                wait_for(dve, gate_e, t + 1)
                g3 = gate.rearrange("p (h n) -> p h n", h=PH)
                tlink(v.tensor_reduce(gsum, g3, AX.X, ALU.add))
                tlink(v.reciprocal(gsum, gsum))
                (v.tensor_tensor(g3, g3, gsum.unsqueeze(2).to_broadcast([P, PH, K16]), ALU.mult)).then_inc(gate_ready, 1)
                assert k[0] == TOPK_STEPS, k[0]

            def tables(t):
                wait_for(dve, tab_trans, t + 1)
                v.tensor_copy(gT[:, 0], ps[:, 4, 2 * P:3 * P]).then_inc(tab_done, 1)
                v.tensor_copy(eT, ps[:, 4, 0:2 * P].rearrange("p (a n) -> p a n", a=2)).then_inc(tab_done, 1)
                wait_for(dve, tab_done, t * 3 + 2)
                v.tensor_tensor(gT[:, 1], ps[:, 4, 2 * P:3 * P], gT[:, 0], ALU.subtract).then_inc(tab_done, 1)
                wait_for(dve, tab_done, t * 3 + 3)

            def dot(rounds, slot, col):
                wait_for(dve, row_ready[slot], rounds * 16 + 16)
                x = u_rows[slot]
                v.tensor_tensor_reduce(x, x, xn, 1.0, 0.0, ALU.mult, ALU.add, dots_now[:, col:col + 1]).then_inc(row_used, 1)

            def keep_dots(at, n, used, turn):
                wait_for(dve, row_used, used)
                v.tensor_copy(dots[:, bass.ds(at, n)], dots_now[:, 0:n]).then_inc(dots_copied, 1)
                wait_for(dve, dots_copied, turn + 1)

            def plain_dots(row, rounds, turn, between=iter(())):
                for j in range(PLAIN_ROWS):
                    dot(rounds + j // RING, j % RING, j)
                    for _ in range(4):
                        next(between, None)
                keep_dots(row, PLAIN_ROWS, row + (PLAIN_ROWS + RING), turn)

            def build(n, j):
                wait_for(dve, g_mm, n + 1)
                units = oh[:, j % 2]
                every_key = iota_keys.unsqueeze(1).to_broadcast([P, TU, NK])

                def over_keys(table):
                    return table[:, TU * j:TU * j + TU].unsqueeze(2).to_broadcast([P, TU, NK])

                v.tensor_tensor(units[:, 1], every_key, over_keys(eT[:, 1]), ALU.is_equal).then_inc(oh_step, 1)
                v.tensor_tensor(units[:, 0], every_key, over_keys(eT[:, 0]), ALU.is_equal).then_inc(oh_ready, 1)
                wait_for(dve, oh_step, n + 1)
                for part in range(2):
                    v.tensor_tensor(units[:, 2 + part], units[:, 1], over_keys(gT[:, part]), ALU.mult).then_inc(oh_ready, 1)

            def tile_gates(t, following, in_plain=iter(())):
                tables(t)
                steps = following
                at_exp, left = False, 4
                for j in range(P // TU):
                    build(t * 16 + j, j)
                    while steps is not None and j >= 1 and (at_exp is False or j == 13):
                        stop = next(steps, "end")
                        left -= 1
                        at_exp = at_exp or stop == "exp"
                        if stop == "end" or (j < 12 and left == 0) or (at_exp and j < 13):
                            break
                    left = 4
                    for r in range(j * GATED_ROWS // 4, (j + 1) * GATED_ROWS // 4):
                        dot(t * (TILE_ROWS // RING) + r // RING, r % RING, r)
                n = PARTS * GATED_ROWS
                keep_dots(t * TILE_ROWS, n, t * TILE_ROWS + (n + RING), t * 2)
                plain_dots(t * TILE_ROWS + n, t * (TILE_ROWS // RING) + n // RING, t * 2 + 1, in_plain)
                for _ in in_plain:
                    pass

            dve.wait_ge(xn_done, 1)
            for _ in choose(0):
                pass
            dve.wait_ge(gate_ready, 1)
            link(v.tensor_copy(gate0, gate))
            for _ in choose(1):
                pass
            tile_gates(0, choose(2), best_keys(3))
            with dve.Fori(1, ND - 2) as t:
                tile_gates(t, best_experts(t + 2), best_keys(t + 3))
            tile_gates(ND - 2, best_experts(ND))
            tile_gates(ND - 1, None)
            with dve.Fori(0, LAST_STEPS) as i:
                plain_dots(i * PLAIN_ROWS + ND * TILE_ROWS, i + ND * TILE_ROWS // RING, i + 2 * ND)
            v.memset(rz, 0.0).then_inc(dots_done, 1)

            v.sem_inc(act_done, 2 * GRP)
            v.sem_inc(add_done, 2 * ND)

            def weigh(n, b, k, i):
                if k == 0:
                    wait_for(dve, ga_ready[b], i * 32 + 32)
                x = af[b][:, k]
                x3 = x.rearrange("p (s n) -> p s n", s=ND * PARTS)
                v.tensor_tensor(x3, x3, gf[b][:, :, k * PART:(k + 1) * PART], ALU.mult).then_inc(weighed, 1)
                dve.wait_ge(weighed, n * 2 + 1)
                v.tensor_copy(abf[:, b, 0, k], x).then_inc(weighed, 1)
                dve.wait_ge(weighed, n * 2 + 2)
                v.tensor_tensor(abf[:, b, 1, k], x, abf[:, b, 0, k], ALU.subtract).then_inc(act_done, 1)

            def add_banks(n0, outs):
                for o in outs:
                    t, half = divmod(o, 2)
                    dve.wait_ge(dn_done, n0 + (o + 1 + 4 * ND))
                    dve.wait_ge(add_done, n0 + (o + 1))
                    x = X[:, t + 1, half * 512:half * 512 + 512]
                    v.tensor_tensor(x, ps[:, o % NBANK, :], x, ALU.add).then_inc(add_done, 1)

            def add_row(rounds, n, k):
                wait_for(dve, row_ready[k], rounds * 16 + 16)
                wait_for(dve, row_used, n + (NSLOT + RING))
                v.scalar_tensor_tensor(X[:, 0], v_rows_now[k], coef[:, bass.ds(n, 1)], X[:, 0],
                                       ALU.mult, ALU.add).then_inc(row_used, 1)

            OUTS = ((0, 1, 2), (3, 4, 5), (6, 7), (8, 9))

            def group(i, b, more):
                for k in range(GRP):
                    if more:
                        if b == 0:
                            if k == 0:
                                wait_for(dve, dn_done, i * (4 * ND) + 4 * ND)
                            weigh(i * (2 * GRP) + (GRP + k), 1, k, i)
                        else:
                            if k == 0:
                                wait_for(dve, dn_done, i * (4 * ND) + 6 * ND)
                            weigh(i * (2 * GRP) + (2 * GRP + k), 0, k, i + 1)
                    add_row(i * 2 + (b + NSLOT // RING), i * (2 * GRP) + (b * GRP + k), k)
                    add_banks(i * (4 * ND) + b * 2 * ND, OUTS[k])

            for k in range(GRP):
                weigh(k, 0, k, 0)
            dve.wait_ge(coef_gelu, 1)
            v.tensor_tensor(coef, coef, gate0, ALU.mult).then_inc(coef_done, 1)
            dve.wait_ge(coef_done, 1)
            dve.wait_ge(gelu_done, NK + 2)
            for b in range(2):
                dve.wait_ge(ga_out[b], 16 * NK // 2 + 16)
            with dve.Fori(0, NGRP // 2 - 1) as i:
                group(i, 0, True)
                group(i, 1, True)
            group(NGRP // 2 - 1, 0, True)
            group(NGRP // 2 - 1, 1, False)
            dve.wait_ge(add_done, NGRP * 2 * ND + 2 * ND)
            dve.wait_ge(row_used, 2 * NSLOT + RING)
            v.memset(rz, 0.0).then_inc(x_done, 1)

            norm("ple", wbc2, 3)
            for g in range(2 * NT):
                i, t = divmod(g, NT)
                dve.wait_ge(pg_sig, g + 1)
                if g >= 2:
                    dve.wait_ge(pp_used, g - 1)
                link(v.tensor_tensor(plp[:, g % 2], ps[:, 3 + 2 * (g % 2), :], sig[:, g % 2], ALU.mult))
                x = X[:, t, 512 * i:512 * i + 512]
                v.tensor_tensor(x, x, plp[:, g % 2], ALU.add).then_inc(pp_used, 1)
            dve.wait_ge(pp_used, 2 * NT)
            norm("fin", wbc2, 4)


def kernel(**inputs):
    import numpy as np
    import concourse.bacc as bacc
    from concourse.bass_utils import run_bass_kernel_spmd

    def arr(name):
        return np.ascontiguousarray(inputs[name])

    w_in = arr("w_in")[0]
    gb = arr("gate_bias")[0]
    gate_w = np.zeros((D, 2, 36), w_in.dtype)
    gate_b = np.zeros((36, 2), gb.dtype)
    for d in range(2):
        for kind in range(2):
            c = 8 * d + 4 * kind
            gate_w[:, kind, 32 * d:32 * d + H] = w_in[:, GATE0 + c:GATE0 + c + H]
            gate_b[32 * d:32 * d + H, kind] = gb[c:c + H]
    half = np.arange(0, 2 * HALF, 2, dtype=np.float32) / np.float32(2 * HALF)
    inv = np.float32(500000.0) ** -half
    ang = np.arange(SEQS[0][1] * P, dtype=np.float32)[:, None] * inv[None, :]
    rope = np.stack([np.cos(ang), np.sin(ang)], axis=1).astype(np.float32)
    arrays = {
        "x_a": arr("x_prompt")[0], "x_b": arr("x_sample")[0],
        "pT_a": arr("p_prompt")[0, 0].T, "pT_b": arr("p_sample")[0, 0].T,
        "norm_mix": arr("norm_mix")[0], "w_in": w_in,
        "gate_w": gate_w, "gate_b": gate_b,
        "conv_w": arr("conv_qk")[0].T.reshape(2 * H, P, 5).transpose(1, 0, 2),
        "lambda_qk": arr("lambda_qk")[0], "attn_gain": arr("attn_gain")[0][:, None],
        "mlstm_gain": arr("mlstm_gain")[0].reshape(H, P).T,
        "w_out": arr("w_out")[0], "norm_ffn": arr("norm_ffn")[0], "peer_wq": arr("peer_wq")[0],
        "subkeysT": arr("peer_subkeys")[0].reshape(2 * PH, P, P).transpose(2, 0, 1),
        "uT": arr("peer_u")[0].reshape(NK, NK, DC, P).transpose(1, 3, 2, 0).reshape(NK, P, DC * NK),
        "peer_u": arr("peer_u")[0], "peer_v": arr("peer_v")[0], "norm_ple": arr("norm_ple")[0],
        "ple_w_gate": arr("ple_w_gate")[0], "ple_w_proj": arr("ple_w_proj")[0],
        "norm_final": arr("norm_final"), "rope": rope,
    }
    arrays = {k: np.ascontiguousarray(a) for k, a in arrays.items()}
    nc = bacc.Bacc("TRN2", target_bir_lowering=False, num_devices=1)
    args = [nc.dram_tensor(k, a.shape, mybir.dt.from_np(a.dtype), kind="ExternalInput").ap() for k, a in arrays.items()]
    args += [nc.dram_tensor(k, (n, D), F32, kind="ExternalOutput").ap() for k, n in (("y_a", 4 * P), ("y_b", 2 * P))]
    hymba_layer(nc, *args)
    got = run_bass_kernel_spmd(nc, [arrays], core_ids=[0]).results[0]
    return got["y_a"].reshape(1, 4 * P, D), got["y_b"].reshape(1, 2 * P, D)
```
